# Optimizing a Trainium2 kernel written in Bass

```python
import math
import jax, jax.numpy as jnp
from jax import lax
import numpy as np

D_MODEL = 1024
BATCH = 1
SEQ = 512
DEPTH = 2

DA_HEADS = 4
DA_QK_DIM = 64
DA_V_DIM = 2 * DA_QK_DIM
DA_WIDTH = DA_HEADS * DA_V_DIM
GDN_HEADS = 4
GDN_DIM = 128
GDN_WIDTH = GDN_HEADS * GDN_DIM
MIX_WIDTH = DA_WIDTH + GDN_WIDTH
CONV_K = 4
GDN_CHUNK = 64
Q_BLOCK = 128
DA_Q_COLS = DA_HEADS * 2 * DA_QK_DIM
DA_K_COLS = DA_HEADS * 2 * DA_QK_DIM
DA_V_COLS = DA_WIDTH
GDN_QKV_COLS = 3 * GDN_WIDTH
GDN_Z_COLS = GDN_WIDTH
IN_COLS = DA_Q_COLS + DA_K_COLS + DA_V_COLS + GDN_QKV_COLS + GDN_Z_COLS + 2 * GDN_HEADS
PEER_HEADS = 8
PEER_NKEYS = 128
PEER_N = PEER_NKEYS * PEER_NKEYS
PEER_QDIM = 256
PEER_HALF = PEER_QDIM // 2
PEER_TOPK = 16
PEER_TOKEN_BLOCK = 128
PLE_DIM = 256
EPS = 1e-6

kernel_name = "hybrid_diffattn_gdn_peer_ple"

def rms_norm(x, g):
    xf = x.astype(jnp.float32)
    y = xf * lax.rsqrt(jnp.mean(xf * xf, axis=-1, keepdims=True) + EPS)
    return (y * g.astype(jnp.float32)).astype(x.dtype)

def l2_normalize(x):
    return x * lax.rsqrt(jnp.sum(x * x, axis=-1, keepdims=True) + EPS)

def alibi_slopes(n):
    return jnp.exp2(-8.0 * (jnp.arange(n, dtype=jnp.float32) + 1.0) / n)

def diff_attention(q, k, v, lam, subln_g, lam_init):
    B, T = q.shape[0], q.shape[1]
    nb = T // Q_BLOCK
    scale = DA_QK_DIM ** -0.5
    qh = jnp.transpose(q, (0, 2, 3, 1, 4))
    kh = jnp.transpose(k, (0, 2, 3, 1, 4))
    vh = jnp.transpose(v, (0, 2, 1, 3))
    qb = jnp.moveaxis(qh.reshape(B, DA_HEADS, 2, nb, Q_BLOCK, DA_QK_DIM), 3, 0)
    slopes = alibi_slopes(DA_HEADS)[:, None, None, None]
    kpos = jnp.arange(T)

    def block(args):
        qblk, start = args
        qpos = start + jnp.arange(Q_BLOCK)
        dist = (qpos[:, None] - kpos[None, :]).astype(jnp.float32)
        s = jnp.einsum('bhcqd,bhckd->bhcqk', qblk, kh, preferred_element_type=jnp.float32) * scale
        s = jnp.where(dist >= 0, s - slopes * dist, -jnp.inf)
        a = jax.nn.softmax(s, axis=-1)
        w = a[:, :, 0] - lam * a[:, :, 1]
        return jnp.einsum('bhqk,bhkd->bhqd', w.astype(vh.dtype), vh)

    starts = jnp.arange(nb) * Q_BLOCK
    o = lax.map(block, (qb, starts))
    o = jnp.moveaxis(o, 0, 2).reshape(B, DA_HEADS, T, DA_V_DIM)
    o = jnp.transpose(o, (0, 2, 1, 3))
    o = rms_norm(o, subln_g) * (1.0 - lam_init)
    return o.reshape(B, T, DA_WIDTH)

def short_conv(x, w):
    T = x.shape[1]
    xp = jnp.pad(x, ((0, 0), (CONV_K - 1, 0), (0, 0)))
    y = xp[:, 0:T] * w[0]
    for j in range(1, CONV_K):
        y = y + xp[:, j:j + T] * w[j]
    return jax.nn.silu(y)

def chunk_gated_delta_rule(q, k, v, g, beta):
    B, T, H, dk = q.shape
    dv = v.shape[-1]
    C = GDN_CHUNK
    N = T // C

    def chunks(t):
        t = jnp.moveaxis(t, 2, 1)
        return t.reshape((B, H, N, C) + t.shape[3:])

    q, k, v, g, beta = chunks(q), chunks(k), chunks(v), chunks(g), chunks(beta)
    gc = jnp.cumsum(g, axis=-1)
    incl = jnp.tril(jnp.ones((C, C), dtype=bool))
    strict = jnp.tril(jnp.ones((C, C), dtype=bool), -1)
    decay = jnp.exp(jnp.where(incl, gc[..., :, None] - gc[..., None, :], -jnp.inf))
    kb = k * beta[..., None]
    L = jnp.where(strict, jnp.einsum('bhncd,bhnsd->bhncs', kb, k) * decay, 0.0)
    A = L + jnp.eye(C, dtype=jnp.float32)
    rhs = jnp.concatenate([v * beta[..., None], kb * jnp.exp(gc)[..., None]], axis=-1)
    sol = lax.linalg.triangular_solve(A, rhs, left_side=True, lower=True, unit_diagonal=True)
    u, w = sol[..., :dv], sol[..., dv:]
    intra = jnp.where(incl, jnp.einsum('bhncd,bhnsd->bhncs', q, k) * decay, 0.0)
    q_dec = q * jnp.exp(gc)[..., None]
    g_last = gc[..., -1]
    k_dec = k * jnp.exp(g_last[..., None] - gc)[..., None]

    def step(S, xs):
        qd, kd, ui, wi, ai, gl = xs
        v_new = ui - jnp.einsum('bhck,bhkv->bhcv', wi, S)
        o = jnp.einsum('bhck,bhkv->bhcv', qd, S) + jnp.einsum('bhcs,bhsv->bhcv', ai, v_new)
        S = S * jnp.exp(gl)[..., None, None] + jnp.einsum('bhck,bhcv->bhkv', kd, v_new)
        return S, o

    xs = (jnp.moveaxis(q_dec, 2, 0), jnp.moveaxis(k_dec, 2, 0), jnp.moveaxis(u, 2, 0),
          jnp.moveaxis(w, 2, 0), jnp.moveaxis(intra, 2, 0), jnp.moveaxis(g_last, 2, 0))
    S0 = jnp.zeros((B, H, dk, dv), jnp.float32)
    _, o = lax.scan(step, S0, xs)
    o = jnp.moveaxis(o, 0, 2).reshape(B, H, T, dv)
    return jnp.moveaxis(o, 1, 2)

def gated_deltanet(qkv, z, b, a, conv_w, a_log, dt_bias, norm_g):
    B, T, _ = qkv.shape
    dtype = qkv.dtype
    qkv = short_conv(qkv, conv_w).astype(jnp.float32)
    q = qkv[..., :GDN_WIDTH].reshape(B, T, GDN_HEADS, GDN_DIM)
    k = qkv[..., GDN_WIDTH:2 * GDN_WIDTH].reshape(B, T, GDN_HEADS, GDN_DIM)
    v = qkv[..., 2 * GDN_WIDTH:].reshape(B, T, GDN_HEADS, GDN_DIM)
    q = l2_normalize(q) * (GDN_DIM ** -0.5)
    k = l2_normalize(k)
    beta = jax.nn.sigmoid(b.astype(jnp.float32))
    g = -jnp.exp(a_log.astype(jnp.float32)) * jax.nn.softplus(a.astype(jnp.float32) + dt_bias.astype(jnp.float32))
    o = chunk_gated_delta_rule(q, k, v, g, beta)
    o = rms_norm(o, norm_g) * jax.nn.silu(z.reshape(B, T, GDN_HEADS, GDN_DIM).astype(jnp.float32))
    return o.reshape(B, T, GDN_WIDTH).astype(dtype)

def peer(xn, wq, subkeys, u_tab, v_tab):
    B, T, D = xn.shape
    K = PEER_TOPK
    q = (xn @ wq).reshape(B, T, PEER_HEADS, 2, PEER_HALF)
    s = jnp.einsum('bthcd,hcnd->bthcn', q, subkeys, preferred_element_type=jnp.float32)
    v1, i1 = lax.top_k(s[..., 0, :], K)
    v2, i2 = lax.top_k(s[..., 1, :], K)
    cand = (v1[..., :, None] + v2[..., None, :]).reshape(B, T, PEER_HEADS, K * K)
    cidx = (i1[..., :, None] * PEER_NKEYS + i2[..., None, :]).reshape(B, T, PEER_HEADS, K * K)
    top_v, top_p = lax.top_k(cand, K)
    idx = jnp.take_along_axis(cidx, top_p, axis=-1)
    gate = jax.nn.softmax(top_v, axis=-1)
    M = B * T
    nb = M // PEER_TOKEN_BLOCK
    E = PEER_HEADS * K
    xs = (xn.reshape(nb, PEER_TOKEN_BLOCK, D), idx.reshape(nb, PEER_TOKEN_BLOCK, E),
          gate.reshape(nb, PEER_TOKEN_BLOCK, E).astype(xn.dtype))

    def block(args):
        xb, ib, gb = args
        h = jnp.einsum('md,med->me', xb, u_tab[ib])
        return jnp.einsum('me,med->md', gb * jax.nn.gelu(h, approximate=False), v_tab[ib])

    y = lax.map(block, xs)
    return y.reshape(B, T, D)

def setup_inputs(seed: int = 0) -> dict:
    key = jax.random.key(seed)
    ks = jax.random.split(key, 24)
    f32 = jnp.float32
    nrm = lambda k, shape, s: jax.random.normal(k, shape, f32) * s
    gain = lambda k, shape: 1.0 + 0.02 * jax.random.normal(k, shape, f32)
    A = jax.random.uniform(ks[5], (DEPTH, GDN_HEADS), f32, 1.0, 16.0)
    dt = jnp.exp(jax.random.uniform(ks[6], (DEPTH, GDN_HEADS), f32, math.log(1e-3), math.log(1e-1)))
    return {
        "x": nrm(ks[0], (BATCH, SEQ, D_MODEL), 1.0),
        "p": nrm(ks[1], (DEPTH, BATCH, SEQ, PLE_DIM), 1.0),
        "ln_mix_g": gain(ks[2], (DEPTH, D_MODEL)),
        "w_in": nrm(ks[3], (DEPTH, D_MODEL, IN_COLS), D_MODEL ** -0.5),
        "conv_w": nrm(ks[4], (DEPTH, CONV_K, GDN_QKV_COLS), CONV_K ** -0.5),
        "gdn_a_log": jnp.log(A),
        "gdn_dt_bias": dt + jnp.log(-jnp.expm1(-dt)),
        "gdn_norm_g": gain(ks[7], (DEPTH, GDN_DIM)),
        "diff_lambda": nrm(ks[8], (DEPTH, 4, DA_QK_DIM), 0.1),
        "diff_subln_g": gain(ks[9], (DEPTH, DA_V_DIM)),
        "w_out": nrm(ks[10], (DEPTH, MIX_WIDTH, D_MODEL), MIX_WIDTH ** -0.5),
        "ln_ffn_g": gain(ks[11], (DEPTH, D_MODEL)),
        "peer_wq": nrm(ks[12], (DEPTH, D_MODEL, PEER_HEADS * PEER_QDIM), D_MODEL ** -0.5),
        "peer_subkeys": nrm(ks[13], (DEPTH, PEER_HEADS, 2, PEER_NKEYS, PEER_HALF), PEER_HALF ** -0.5),
        "peer_u": nrm(ks[14], (DEPTH, PEER_N, D_MODEL), D_MODEL ** -0.5),
        "peer_v": nrm(ks[15], (DEPTH, PEER_N, D_MODEL), 0.25),
        "ple_wp": nrm(ks[16], (DEPTH, PLE_DIM, D_MODEL), PLE_DIM ** -0.5),
        "ple_wg": nrm(ks[17], (DEPTH, D_MODEL, D_MODEL), D_MODEL ** -0.5),
        "ple_norm_g": gain(ks[18], (DEPTH, D_MODEL)),
        "final_norm_g": gain(ks[19], (D_MODEL,)),
    }

def reference(x, p, ln_mix_g, w_in, conv_w, gdn_a_log, gdn_dt_bias, gdn_norm_g, diff_lambda,
              diff_subln_g, w_out, ln_ffn_g, peer_wq, peer_subkeys, peer_u, peer_v,
              ple_wp, ple_wg, ple_norm_g, final_norm_g):
    B, T, _ = x.shape
    h = x
    for i in range(DEPTH):
        xn = rms_norm(h, ln_mix_g[i])
        proj = xn @ w_in[i]
        o0 = 0
        dq = proj[..., o0:o0 + DA_Q_COLS]; o0 += DA_Q_COLS
        dk = proj[..., o0:o0 + DA_K_COLS]; o0 += DA_K_COLS
        dv = proj[..., o0:o0 + DA_V_COLS]; o0 += DA_V_COLS
        gqkv = proj[..., o0:o0 + GDN_QKV_COLS]; o0 += GDN_QKV_COLS
        gz = proj[..., o0:o0 + GDN_Z_COLS]; o0 += GDN_Z_COLS
        gb = proj[..., o0:o0 + GDN_HEADS]; o0 += GDN_HEADS
        ga = proj[..., o0:o0 + GDN_HEADS]

        lam_init = 0.8 - 0.6 * math.exp(-0.3 * i)
        lp = diff_lambda[i].astype(jnp.float32)
        lam = jnp.exp(jnp.sum(lp[0] * lp[1])) - jnp.exp(jnp.sum(lp[2] * lp[3])) + lam_init
        o_da = diff_attention(dq.reshape(B, T, DA_HEADS, 2, DA_QK_DIM),
                              dk.reshape(B, T, DA_HEADS, 2, DA_QK_DIM),
                              dv.reshape(B, T, DA_HEADS, DA_V_DIM),
                              lam, diff_subln_g[i], lam_init)
        o_gdn = gated_deltanet(gqkv, gz, gb, ga, conv_w[i], gdn_a_log[i], gdn_dt_bias[i], gdn_norm_g[i])
        h = h + jnp.concatenate([o_da, o_gdn], axis=-1) @ w_out[i]

        h = h + peer(rms_norm(h, ln_ffn_g[i]), peer_wq[i], peer_subkeys[i], peer_u[i], peer_v[i])

        e = rms_norm(p[i] @ ple_wp[i], ple_norm_g[i])
        h = h + jax.nn.sigmoid(h @ ple_wg[i]) * e
    return rms_norm(h, final_norm_g)


_drawn_inputs = setup_inputs


def setup_inputs(seed=0):
    import zlib

    import numpy as np

    out = dict(_drawn_inputs(seed))
    spreads = {}
    factors = {'gdn_norm_g': 10.252,
     'diff_subln_g': 2.878,
     'ln_ffn_g': 8.603,
     'ple_norm_g': 11.368,
     'final_norm_g': 8.051}
    for name, (base, spread) in spreads.items():
        noise = np.random.default_rng([zlib.crc32(name.encode()), seed]).standard_normal(out[name].shape)
        drawn = base * np.exp(spread * noise) if base else spread * noise
        out[name] = __import__('jax').numpy.asarray(drawn.astype(out[name].dtype))
    for name, factor in factors.items():
        out[name] = (out[name] * factor).astype(out[name].dtype)
    return out
```

```python
from contextlib import ExitStack

import concourse.bass as bass
from concourse import mybir

P = 128
D = 1024
KD = D // P
T = 512
NT = T // P
DEPTH = 2
H = 4
DQK = 64
CHUNK = 64
CONV_K = 4
PH = 8
TOPK = 16
NKEYS = 128
PLE = 256
EPS = 1e-6
CAND_ROWS = [TOPK // (a + 1) for a in range(TOPK)]
CAND_AT = [sum(CAND_ROWS[:a]) for a in range(TOPK)]
NC = sum(CAND_ROWS)

S_IN = 0
S_OUT = 28
S_WQ = 36
S_U0 = 52
S_UV = 60
S_V_LAST = 300
S_WG = 308
S_WP = 316
N_SLABS = 318
RING = 4
AHEAD = 3
GROUPS = 16
GB = 8
TG = 64
DVE_HOT1 = 5
REGION = 53000

C_ID, C_ONE, C_TRI, C_CHUNK, C_NEGT, C_POSD, C_M16, C_M32, C_M64 = [P * i for i in range(9)]
C_DIST = 9 * P
C_IOTA = C_DIST + T
C_POS = C_IOTA + P
C_EPS = C_POS + NC
NCONST = C_EPS + 2
Q_MIX, Q_FFN, Q_PLE, Q_FIN = 0, 8, 16, 24
Q_CONV = 32
Q_GDN = Q_CONV + CONV_K * 12
Q_SUB = Q_GDN + 1
Q_ALOG = Q_SUB + 1
Q_DT = Q_ALOG + H
Q_LAM = Q_DT + H
Q_LINIT = Q_LAM + 4 * DQK
NPAR = Q_LINIT + 2

ALU = mybir.AluOpType
ACT = mybir.ActivationFunctionType
F32 = mybir.dt.float32
F32R = mybir.dt.float32r
BF16 = mybir.dt.bfloat16
U32 = mybir.dt.uint32
I32 = mybir.dt.int32
AX_X = mybir.AxisListType.X
NEG = -1e30


def trunk(nc, x_t, p_t, slabs, w_ba, subkeys, params, consts_d, out_t):
    g_dram = nc.dram_tensor("gates_dram", (T // TG, P, NKEYS, TG), F32).ap()

    with ExitStack() as ctx:
        def sem(name):
            return ctx.enter_context(nc.semaphore(name))

        slab_region = ctx.enter_context(nc.sbuf_tensor("region", [P, REGION], F32))
        lo_addr = nc.sbuf_base - REGION * 4
        at = [lo_addr]

        def place(name, shape, dt, where=None):
            size = 4 if dt in (F32, F32R, U32, I32) else 2
            for n in shape[1:]:
                size *= n
            size = (size + 31) // 32 * 32
            if where is None:
                where = at
            t = nc.alloc_sbuf_tensor_at(name, shape, dt, offset=where[0])
            where[0] += size
            assert where[0] <= lo_addr + REGION * 4, (name, where[0] - lo_addr)
            return t

        res = place("res", [P, KD, T], F32)
        consts = place("consts", [P, NCONST], F32)
        par = place("par", [P, NPAR], F32)
        cols = place("cols", [P, 64], F32)
        rs = place("rs", [P, 32], F32)
        at_c2 = place("at_c2", [P, 8], F32)
        raw = [place(f"raw{i}", [P, KD, P], F32) for i in range(RING)]
        whi = [place(f"whi{i}", [P, KD, P], F32R) for i in range(RING)]
        wlo = [place(f"wlo{i}", [P, KD, P], F32R) for i in range(RING)]
        act_base = at[0]
        act_hi = place("act_hi", [P, KD, T], F32R)
        act_lo = place("act_lo", [P, KD, T], F32R)
        arena = at[0]

        m = [arena]
        wide = place("wide", [P, KD, T], F32, m)
        squares = place("squares", [P, KD, T], F32, m)

        m = [act_base]
        kn_nat = place("kn_nat", [P, NT, H, P], F32, m)
        gv_nat = place("gv_nat", [P, NT, H, P], F32, m)
        v_nat = place("v_nat", [P, NT, H, P], F32, m)
        mats = m
        pow_m = place("pow_m", [P, H, P], F32, mats)
        pow_n = place("pow_n", [P, H, P], F32, mats)
        pow_m2 = place("pow_m2", [P, H, P], F32, mats)
        pow_n2 = place("pow_n2", [P, H, P], F32, mats)
        assert m[0] <= arena
        m = [arena]
        mixt = place("mixt", [P, 2 * H, T], F32, m)
        gqt = place("gqt", [P, H, T], F32, m)
        gkt = place("gkt", [P, H, T], F32, m)
        gzt = place("gzt", [P, H, T], F32, m)
        daq = place("daq", [P, H, T], F32, m)
        dak = place("dak", [P, H, T], F32, m)
        dead = m[0]
        gvt = place("gvt", [P, H, T], F32, m)
        davt = place("davt", [P, H, T], F32, m)
        gates_at = m[0]
        gsm = place("gsm", [P, 16, 16], F32, m)
        lam = place("lam", [P, 80], F32, m)
        wba = place("wba", [P, KD, 8], F32, m)
        wba_hi = place("wba_hi", [P, KD, 8], F32R, m)
        wba_lo = place("wba_lo", [P, KD, 8], F32R, m)
        craw = [place(f"craw{i}", [P, T], F32, m) for i in range(2)]
        m2 = [dead]
        low32 = place("low32", [P, H, P], F32, m2)
        low64 = place("low64", [P, H, P], F32, m2)
        inv_a = place("inv_a", [P, H, P], F32, m2)
        inv_b = place("inv_b", [P, H, P], F32, m2)
        inv_t = place("inv_t", [P, H, P], F32, m2)
        zmat = place("zmat", [P, H, P], F32, m2)
        state = [place(f"state{i}", [P, H, P], F32, m2) for i in range(2)]
        assert m2[0] <= gates_at
        m3 = [gates_at + (16 * 16 + 80) * 4]
        at_s = place("at_s", [P, 2, T], F32, m3)
        at_w = place("at_w", [P, T], F32, m3)
        at_wt = place("at_wt", [P, NT, P], F32, m3)
        at_c = place("at_c", [P, 8], F32, m3)
        dec_t = place("dec_t", [P, H, P], F32, m3)
        dec = place("dec", [P, H, P], F32, m3)
        egc_b = place("egc_b", [P, H, P], F32, m3)
        kbg = place("kbg", [P, H, P], F32, m3)
        vbeta = place("vbeta", [P, H, P], F32, m3)
        kdec = place("kdec", [P, H, P], F32, m3)
        qdec = place("qdec", [P, H, P], F32, m3)
        u_sb = place("u_sb", [P, H, P], F32, m3)
        intra = place("intra", [P, H, P], F32, m3)
        vnew = u_sb
        w_tr = pow_n2
        mixer_end = m3[0]
        m3 = [gates_at + (16 * 16 + 80) * 4]
        sq_mix = place("sq_mix", [P, 2 * H, T], F32, m3)

        m = [arena]
        qt = place("qt", [P, 2 * PH, T], F32, m)
        subk = place("subk", [P, 2 * PH, NKEYS], F32, m)
        rest = place("rest", [P, 2 * PH, NKEYS], F32, m)
        topv = place("topv", [P, PH, 2, TOPK], F32, m)
        topi = place("topi", [P, PH, 2, TOPK], U32, m)
        topf = place("topf", [P, PH, 2, TOPK], F32, m)
        cand = place("cand", [P, PH, NC], F32, m)
        cidx = place("cidx", [P, PH, NC], F32, m)
        crest = place("crest", [P, PH, NC], F32, m)
        winv = place("winv", [P, PH, TOPK], F32, m)
        winp = place("winp", [P, PH, TOPK], U32, m)
        winf = place("winf", [P, PH, TOPK], F32, m)
        onehot = place("onehot", [P, PH // 2 * TOPK, NC], F32, m)
        expert = place("expert", [P, PH * TOPK], F32, m)
        exp_i = place("exp_i", [P, PH * TOPK], I32, m)
        exp_j = place("exp_j", [P, PH * TOPK], I32, m)
        sel = place("sel", [P, 3, PH * TOPK], F32, m)
        gsum = place("gsum", [P, PH], F32, m)
        sel_at = m[0]
        selt = place("selt", [P, 3, T], F32, m)
        sel_end = m[0]
        m = [arena]
        stage = [place(f"stage{i}", [P, NKEYS, TG], F32, m) for i in range(2)]
        assert m[0] <= sel_at, (m[0] - arena, sel_at - arena)
        m = [sel_end]
        hot1 = [place(f"hot1_{i}", [P, 8, NKEYS], F32, m) for i in range(2)]
        hot2 = [place(f"hot2_{i}", [P, 8, NKEYS], F32, m) for i in range(2)]
        n1_cols = [place(f"n1_cols{i}", [P, 8], F32, m) for i in range(2)]
        m = [arena]
        w_hi = [place(f"w_hi{i}", [P, GB, T], F32R, m) for i in range(2)]
        w_lo = [place(f"w_lo{i}", [P, GB, T], F32R, m) for i in range(2)]
        act_w = [place(f"act_w{i}", [P, T], F32, m) for i in range(2)]
        g_sb = [place(f"g_sb{i}", [P, T // TG, 2, TG], F32, m) for i in range(4)]
        m = [arena + 2 * 4 * KD * T]
        gate_t = place("gate_t", [P, KD, T], F32, m)
        p_sb = place("p_sb", [P, 2, T], F32, m)
        p_hi = place("p_hi", [P, 2, T], F32R, m)
        p_lo = place("p_lo", [P, 2, T], F32R, m)

        bank = [ctx.enter_context(nc.psum_tensor(f"bank{i}", [P, T], F32)) for i in range(8)]

        ident = consts[:, C_ID:C_ID + P]
        ones = consts[:, C_ONE:C_ONE + P]
        tri = consts[:, C_TRI:C_TRI + P]
        same_chunk = consts[:, C_CHUNK:C_CHUNK + P]
        eps_col = consts[:, C_EPS:C_EPS + 1]
        one_col = consts[:, C_ONE:C_ONE + 1]
        iota = consts[:, C_IOTA:C_IOTA + P]

        def over_heads(c):
            return consts[:, c:c + P].unsqueeze(1).to_broadcast([P, H, P])

        def heads(b):
            return bank[b][:].rearrange("p (h c) -> p h c", h=H)

        consts_loaded = sem("consts_loaded")
        x_loaded = sem("x_loaded")
        layer_end = sem("layer_end")
        layer_go = sem("layer_go")
        layer_seen = sem("layer_seen")
        out_ready = sem("out_ready")
        out_stored = sem("out_stored")
        names = """at_oc2 at_rec low_dve inv_cp tk_chain par_loaded small_loaded p_loaded slab_hi slab_lo slab_used
            sq_ready ss_ready std_ready rs_ready rstd_bc norm_used act_hi_ready act_lo_ready normed res_ready
            win_evac conv_raw conv_acc conv_done conv_chain ba_ready wba_hi_ready wba_lo_ready
            gate_act gate_dve gcol_ready lam_dve lam_act
            qk_scaled nat_ready nat_copied
            sc_ready at_dve at_max at_exp at_wgt at_tr at_trc at_out at_oc
            gcb_ready arg_ready dec_ready gram_ready low_ready lowt_ready pow_ready inv_pe inv_dve
            rhs_ready uw_ready uw_copied step_v step_vn step_so step_state og_copied state_zero
            mix_scaled mix_z mix_ready wout_added wq_evac subk_ready
            score_ready score_read tk_dve tk_act selt_ready selt_copied parts_done parts_act
            n1_ready hot1_ready hot2_ready gm_ready gm_copied stored_a stored_b
            u_gelu w_ready w_hi_ready w_lo_ready v_added
            wg_evac wp_evac p_hi_ready p_lo_ready ple_dve layer_res""".split()
        S = {n: sem(n) for n in names}
        slab_loaded = [sem(f"slab_loaded{i}") for i in range(RING)]
        g_loaded = [sem(f"g_loaded{i}") for i in range(4)]
        per_layer = [S[n] for n in names] + slab_loaded + g_loaded
        s_par, s_slab_hi, s_slab_lo, s_used = S["par_loaded"], S["slab_hi"], S["slab_lo"], S["slab_used"]

        NORM = {"in": (8, 1), "qk": (8, 8), "mix": (8, 8), "ffn": (8, 1), "ple": (8, 1)}
        order = list(NORM)

        def before(use, what):
            return sum(NORM[k][what] for k in order[:order.index(use)])

        def sq_seen(use):
            return before(use, 0)

        def bc_seen(use):
            return before(use, 1)

        def used_seen(use):
            return 2 * H if use == "mix" else 0

        def nth(use):
            return order.index(use)

        def split_hi(act, n, slot=None):
            k = n % RING if slot is None else slot
            act.wait_ge(slab_loaded[k], (n // RING + 1) * 16 if slot is None else (n - slot + RING) * 4)
            if slot is not None or n >= RING:
                act.wait_ge(s_used, n - RING + 1)
            nc.scalar.activation(whi[k][:], raw[k][:], ACT.Copy).then_inc(s_slab_hi, 1)

        def split_lo(dve, n, slot=None):
            k = n % RING if slot is None else slot
            dve.wait_ge(s_slab_hi, n + 1)
            if slot is not None or n >= RING:
                dve.wait_ge(s_used, n - RING + 1)
            nc.vector.tensor_tensor(wlo[k][:], raw[k][:], whi[k][:].bitcast(F32), ALU.subtract).then_inc(s_slab_lo, 1)

        def three_pass(out, a_hi, a_lo, b_hi, b_lo, first, last):
            nc.tensor.matmul(out, a_hi, b_hi, start=first, stop=False)
            nc.tensor.matmul(out, a_hi, b_lo, start=False, stop=False)
            return nc.tensor.matmul(out, a_lo, b_hi, start=False, stop=last)

        def slab_product(pe, n, slot, out, hi, lo, fresh=None):
            pe.wait_ge(s_slab_lo, n + 1)
            for k in range(KD):
                if fresh is not None:
                    pe.wait_ge(S["act_lo_ready"], fresh + k + 1)
                last = three_pass(out, whi[slot][:, k, :], wlo[slot][:, k, :], hi[:, k, :], lo[:, k, :],
                                  k == 0, k == KD - 1)
            last.then_inc(s_used, 1)

        def norm_sums(pe, use, groups, chunks, sq):
            base = sq_seen(use)
            for g in range(groups):
                pe.wait_ge(S["sq_ready"], base + (g + 1) * chunks)
                for t in range(NT):
                    for c in range(chunks):
                        last = nc.tensor.matmul(bank[4][:, t * groups + g:t * groups + g + 1],
                                                sq[:, g * chunks + c, t * P:(t + 1) * P], one_col,
                                                start=c == 0, stop=c == chunks - 1)
            last.then_inc(S["ss_ready"], 1)

        def norm_spread(pe, use, groups):
            pe.wait_ge(S["rs_ready"], nth(use) + 1)
            for g in range(groups):
                if g >= 2:
                    pe.wait_ge(S["norm_used"], used_seen(use) + g - 1)
                for t in range(NT):
                    last = nc.tensor.matmul(bank[5 + g % 2][:, t * P:(t + 1) * P],
                                            rs[:, t * groups + g:t * groups + g + 1].to_broadcast([P, P]), ident,
                                            start=True, stop=True)
                last.then_inc(S["rstd_bc"], 1)

        def norm_std(act, use, groups, scale):
            act.wait_ge(S["ss_ready"], nth(use) + 1)
            nc.scalar.activation(cols[:, 0:NT * groups], bank[4][:, 0:NT * groups], ACT.Sqrt,
                                 bias=eps_col, scale=scale).then_inc(S["std_ready"], 1)

        def norm_rs(dve, use, groups):
            dve.wait_ge(S["std_ready"], nth(use) + 1)
            nc.vector.reciprocal(rs[:, 0:NT * groups], cols[:, 0:NT * groups]).then_inc(S["rs_ready"], 1)

        def act_squares(act, src, n, dst):
            for k in range(n):
                nc.scalar.activation(dst[:, k, :], src[:, k, :], ACT.Square).then_inc(S["sq_ready"], 1)

        def act_low_chunk(dve, src, base, k):
            dve.wait_ge(S["act_hi_ready"], base + k + 1)
            nc.vector.tensor_tensor(act_lo[:, k, :], src[:, k, :], act_hi[:, k, :].bitcast(F32),
                                    ALU.subtract).then_inc(S["act_lo_ready"], 1)

        def scale_to_wide(dve, use, gains, low_base):
            dve.wait_ge(S["rstd_bc"], bc_seen(use) + 1)
            for k in range(KD):
                last = nc.vector.scalar_tensor_tensor(wide[:, k, :], res[:, k, :], par[:, gains + k:gains + k + 1],
                                                      bank[5][:], ALU.mult, ALU.mult)
                last.then_inc(S["normed"], 1)
                if k > 0:
                    act_low_chunk(dve, wide, low_base, k - 1)
            act_low_chunk(dve, wide, low_base, KD - 1)

        def act_high(act, src, seen, base):
            for k in range(KD):
                act.wait_ge(seen, base + k + 1)
                nc.scalar.activation(act_hi[:, k, :], src[:, k, :], ACT.Copy).then_inc(S["act_hi_ready"], 1)

        def act_low(dve, src, base):
            for k in range(KD):
                act_low_chunk(dve, src, base, k)

        def mixer(delta, attend):
            for t in range(NT):
                for s in range(16):
                    delta(t, s)
                    if s % 2 == 1:
                        a = 8 * t + s // 2
                        attend(a // 2, a % 2)
            attend(H * NT, 0)

        block = ctx.enter_context(nc.Block())

        @block.sync
        def _(sp):
            sp.dma_start(consts[:], consts_d).then_inc(consts_loaded, 16)
            sp.dma_start(res[:], x_t).then_inc(x_loaded, 16)
            with sp.Fori(0, DEPTH) as layer:
                sp.dma_start(par[:], params[layer]).then_inc(s_par, 16)
                for n in range(RING):
                    sp.dma_start(raw[n][:], slabs[layer, n]).then_inc(slab_loaded[n], 16)
                sp.dma_start(wba[:], w_ba[layer]).then_inc(S["small_loaded"], 16)
                with sp.Fori(0, N_SLABS // RING - 1) as q:
                    for k in range(RING):
                        sp.wait_ge(s_slab_lo, q * RING + k + 1)
                        sp.dma_start(raw[k][:], slabs[layer, (q + 1) * RING + k]).then_inc(slab_loaded[k], 16)
                for n in range(N_SLABS // RING * RING, N_SLABS):
                    sp.wait_ge(s_slab_lo, n - RING + 1)
                    sp.dma_start(raw[n % RING][:], slabs[layer, n]).then_inc(slab_loaded[n % RING], 16)
                sp.wait_ge(S["layer_res"], KD)
                sp.sem_inc(layer_end, 1)
                sp.wait_ge(layer_go, 1)
                sp.sem_inc(layer_seen, 1)
            sp.wait_ge(out_ready, KD)
            sp.dma_start(out_t, wide[:]).then_inc(out_stored, 16)
            sp.wait_ge(out_stored, 16)

        @block.gpsimd
        def _(pool):
            pool.wait_ge(consts_loaded, 16)
            with pool.Fori(0, DEPTH) as layer:
                pool.wait_ge(S["selt_copied"], NT)
                with pool.Fori(0, NT) as q:
                    for b in range(P // 8):
                        pool.wait_ge(S["gm_ready"], q * (P // 4) + 2 * b + 2)
                        nc.gpsimd.tensor_copy(n1_cols[b % 2][:], selt[:, 0, bass.ds(q * P + 8 * b, 8)]
                                              ).then_inc(S["n1_ready"], 1)
                        pool.wait_ge(S["n1_ready"], q * (P // 8) + b + 1)
                        nc.gpsimd.tensor_tensor(at_c2[:, 6:7], one_col, one_col, ALU.add)
                        for tok in range(DVE_HOT1, 8):
                            last = nc.gpsimd.tensor_scalar(hot1[b % 2][:, tok, :], iota,
                                                           n1_cols[b % 2][:, tok:tok + 1], None, ALU.is_equal)
                        last.then_inc(S["hot1_ready"], 1)
                pool.wait_ge(layer_end, 4)
                pool.nop()
                first = per_layer[0].num
                pool.sem_clear(range(first, first + len(per_layer)))
                pool.sem_clear(layer_end)
                pool.sem_inc(layer_go, 1)
                pool.wait_ge(layer_seen, 4)
                pool.nop()
                pool.sem_clear(layer_go)
                pool.sem_clear(layer_seen)

        @block.scalar
        def _(act):
            act.wait_ge(consts_loaded, 16)
            act.wait_ge(x_loaded, 16)
            with act.Fori(0, DEPTH) as layer:
                for n in range(AHEAD):
                    split_hi(act, n)
                act_squares(act, res, KD, squares)
                norm_std(act, "in", 1, 1.0 / D)
                act_high(act, wide, S["normed"], 0)
                act.wait_ge(S["small_loaded"], 16)
                nc.scalar.activation(wba_hi[:], wba[:], ACT.Copy).then_inc(S["wba_hi_ready"], 1)
                for n in range(28):
                    split_hi(act, n + AHEAD)
                    act.wait_ge(s_used, n + 1)
                    b = bank[n % RING]
                    if n < 4:
                        i = nc.scalar.activation(daq[:, n, :], b[:], ACT.Copy)
                    elif n < 8:
                        i = nc.scalar.activation(dak[:, n - 4, :], b[:], ACT.Copy)
                    elif n < 12:
                        i = nc.scalar.activation(davt[:, n - 8, :], b[:], ACT.Copy)
                    elif n < 24:
                        c = n - 12
                        if c >= 2:
                            act.wait_ge(S["conv_acc"], c - 1)
                        i = nc.scalar.activation(craw[c % 2][:], b[:], ACT.Copy)
                    else:
                        i = nc.scalar.activation(gzt[:, n - 24, :], b[:], ACT.Silu)
                    i.then_inc(S["win_evac"], 1)
                    if 12 < n <= 24:
                        c = n - 13
                        dst = (gqt, gkt, gvt)[c // H]
                        act.wait_ge(S["conv_acc"], c + 1)
                        nc.scalar.activation(dst[:, c % H, :], dst[:, c % H, :], ACT.Silu).then_inc(S["conv_done"], 1)
                act.wait_ge(S["gate_dve"], 1)
                ba = gsm[:, 12:14, :].rearrange("p r (t c) -> p (r t) c", c=2 * H)

                def small(i):
                    return gsm[:, i, :].rearrange("p (t c) -> p t c", t=NT)
                nc.scalar.activation(small(0), ba[:, :, 0:H], ACT.Sigmoid).then_inc(S["gate_act"], 1)
                nc.scalar.activation(gsm[:, 1, 0:H], par[:, Q_ALOG:Q_ALOG + H], ACT.Exp).then_inc(S["gate_act"], 1)
                act.wait_ge(S["gate_dve"], 4)
                nc.scalar.activation(gsm[:, 4, :], gsm[:, 4, :], ACT.Exp).then_inc(S["gate_act"], 1)
                act.wait_ge(S["gate_act"], 3)
                nc.scalar.activation(gsm[:, 4, :], gsm[:, 4, :], ACT.Ln, bias=one_col).then_inc(S["gate_act"], 1)
                act.wait_ge(S["lam_dve"], 2)
                nc.scalar.activation(lam[:, 66:68], lam[:, 64:66], ACT.Exp).then_inc(S["lam_act"], 1)
                act.wait_ge(S["gate_dve"], 7)
                nc.scalar.activation(gsm[:, 7, :], gsm[:, 14, :], ACT.Exp).then_inc(S["gate_act"], 1)
                act.wait_ge(S["gate_dve"], 8)
                nc.scalar.activation(gsm[:, 9, :], gsm[:, 8, :], ACT.Exp).then_inc(S["gate_act"], 1)
                act.wait_ge(S["conv_done"], 8)
                act.wait_ge(S["at_dve"], 1)
                for j in range(2 * H):
                    src = gqt if j < H else gkt
                    nc.scalar.activation(sq_mix[:, j, :], src[:, j % H, :], ACT.Square).then_inc(S["sq_ready"], 1)
                for i in range(12):
                    if i == 8:
                        norm_std(act, "qk", 2 * H, 1.0)
                    act.wait_ge(S["nat_ready"], i + 1)
                    dst = (v_nat, gv_nat, kn_nat)[i // NT]
                    nc.scalar.activation(dst[:, i % NT].rearrange("p h c -> p (h c)"), bank[(4, 7)[i % 2]][:],
                                         ACT.Copy).then_inc(S["nat_copied"], 1)

                def attend(u, half):
                    t = u % NT
                    kl = (t + 1) * P
                    if half == 0:
                        if u > 0 and t == 0:
                            act.wait_ge(S["at_out"], u)
                            nc.scalar.activation(mixt[:, u // NT - 1, :], bank[4][:], ACT.Copy).then_inc(S["at_oc"], 1)
                        for c in range(2):
                            if u == H * NT:
                                break
                            act.wait_ge(S["at_max"], 2 * u + c + 1)
                            nc.scalar.activation(at_s[:, c, 0:kl], at_s[:, c, 0:kl], ACT.Exp, bias=at_c[:, c:c + 1],
                                                 scale=DQK ** -0.5, accum_out=at_c[:, 2 + c:3 + c]
                                                 ).then_inc(S["at_exp"], 1)
                    else:
                        act.wait_ge(S["at_tr"], u + 1)
                        if u > 0:
                            act.wait_ge(S["at_out"], u)
                        nc.scalar.activation(at_wt[:, 0:t + 1, :], heads(5)[:, 0:t + 1, :],
                                             ACT.Copy).then_inc(S["at_trc"], 1)

                def delta(t, s):
                    if s == 0:
                        act.wait_ge(S["arg_ready"], 8 * t + 8)
                        nc.scalar.activation(egc_b[:], heads(6), ACT.Exp).then_inc(S["dec_ready"], 1)
                        nc.scalar.activation(dec_t[:], dec_t[:], ACT.Exp).then_inc(S["dec_ready"], 1)
                        nc.scalar.activation(dec[:], dec[:], ACT.Exp, scale=-1.0).then_inc(S["dec_ready"], 1)
                    elif s == 11:
                        act.wait_ge(S["uw_ready"], t + 1)
                        nc.scalar.activation(w_tr[:], heads(7), ACT.Copy).then_inc(S["uw_copied"], 1)
                    elif s in (13, 15):
                        j = (s - 13) // 2
                        act.wait_ge(S["step_so"], 2 * t + j + 1)
                        src = bank[3][:, 0:H * CHUNK].rearrange("p (h c) -> p h c", h=H)
                        dst = mixt[:, H:2 * H, t * P + j * CHUNK:t * P + (j + 1) * CHUNK]
                        nc.scalar.activation(dst, src, ACT.Copy).then_inc(S["og_copied"], 1)

                mixer(delta, attend)
                act.wait_ge(S["at_oc"], H)
                act.wait_ge(S["og_copied"], 2 * NT)
                act.wait_ge(S["step_state"], 2 * NT)
                act_squares(act, mixt, 2 * H, sq_mix)
                norm_std(act, "mix", 2 * H, 1.0 / P)
                for k in range(KD):
                    if k < H:
                        act.wait_ge(S["norm_used"], used_seen("mix") + k + 1)
                    else:
                        act.wait_ge(S["mix_ready"], k - H + 1)
                    nc.scalar.activation(act_hi[:, k, :], mixt[:, k, :], ACT.Copy).then_inc(S["act_hi_ready"], 1)
                for n in range(S_OUT, S_WQ):
                    split_hi(act, n + AHEAD)
                for k in range(KD):
                    act.wait_ge(S["wout_added"], k + 1)
                    nc.scalar.activation(squares[:, k, :], res[:, k, :], ACT.Square).then_inc(S["sq_ready"], 1)
                norm_std(act, "ffn", 1, 1.0 / D)
                act.wait_ge(s_used, S_WQ)
                act_high(act, wide, S["normed"], KD)
                act.dma_start(subk[:], subkeys[layer]).then_inc(S["subk_ready"], 16)
                for i in range(2 * PH):
                    split_hi(act, S_WQ + i + AHEAD)
                    act.wait_ge(s_used, S_WQ + i + 1)
                    if i == 0:
                        act.wait_ge(S["act_lo_ready"], 3 * KD)
                    nc.scalar.activation(qt[:, i, :], bank[i % RING][:], ACT.Copy).then_inc(S["wq_evac"], 1)
                for t in range(NT):
                    act.wait_ge(S["tk_dve"], 3 * t + 2)
                    nc.scalar.activation(winv[:], winv[:], ACT.Exp).then_inc(S["tk_act"], 1)
                with act.Fori(0, NT) as q:
                    for i in range(P // 4):
                        half = i // (TG // 4)
                        act.wait_ge(S["gm_ready"], q * (P // 4) + i + 5)
                        if i % (TG // 4) == 0:
                            act.wait_ge((S["stored_a"], S["stored_b"])[half], q * 16 + 1)
                        dst = stage[half][:, :, 4 * (i % (TG // 4)):4 * (i % (TG // 4)) + 4].rearrange("p n t -> p t n")
                        nc.scalar.activation(dst, heads(4 + i % 4), ACT.Copy).then_inc(S["gm_copied"], 1)
                        if i % (TG // 4) == TG // 4 - 1:
                            act.wait_ge(S["gm_copied"], q * (P // 4) + i + 5)
                            act.dma_start(g_dram[q * 2 + half], stage[half][:]).then_inc(
                                (S["stored_a"], S["stored_b"])[half], 16)
                act.wait_ge(S["stored_a"], NT * 16 + 1)
                act.wait_ge(S["stored_b"], NT * 16 + 1)

                def load_gates(g, j):
                    act.dma_start(g_sb[j][:].rearrange("p s b t -> p s (b t)"),
                                  g_dram[:, :, bass.ds(g * GB + 2 * j, 2), :].rearrange("s p n t -> p s (n t)")
                                  ).then_inc(g_loaded[j], 16)

                def gelu_block(g, j, used):
                    act.wait_ge(s_used, used)
                    if not (isinstance(g, int) and g * GB + j < 2):
                        act.wait_ge(S["w_lo_ready"], g * GB + j - 1)
                    nc.scalar.activation(act_w[j % 2][:], bank[2 * (j % 2)][:], ACT.Gelu).then_inc(S["u_gelu"], 1)

                def w_high(g, j, par_g):
                    act.wait_ge(S["w_ready"], g * GB + j + 1)
                    nc.scalar.activation(w_hi[par_g][:, j, :], act_w[j % 2][:], ACT.Copy).then_inc(S["w_hi_ready"], 1)

                load_gates(0, 0)
                load_gates(0, 1)
                for j in range(GB):
                    if j % 2 == 0:
                        if j // 2 + 2 < 4:
                            load_gates(0, j // 2 + 2)
                        else:
                            act.wait_ge(S["w_ready"], j - 2)
                            load_gates(1, j // 2 - 2)
                    split_hi(act, S_U0 + j + AHEAD)
                    gelu_block(0, j, S_U0 + j + 1)
                    w_high(0, j, 0)

                def group(g, pg, last=False):
                    for j in range(GB):
                        n = g * 16 + (S_UV - 16 + 2 * j)
                        if j % 2 == 0:
                            act.wait_ge(S["w_ready"], g * GB + j - 2)
                            if j // 2 + 2 < 4:
                                load_gates(g, j // 2 + 2)
                            elif not last:
                                load_gates(g + 1, j // 2 - 2)
                        split_hi(act, n + AHEAD, (2 * j + AHEAD) % RING)
                        gelu_block(g, j, n + 1)
                        w_high(g, j, pg)
                        split_hi(act, n + 1 + AHEAD, (2 * j + 1 + AHEAD) % RING)
                with act.Fori(0, 7) as it:
                    group(it * 2 + 1, 1)
                    group(it * 2 + 2, 0)
                group(15, 1, True)
                for j in range(GB):
                    split_hi(act, S_V_LAST + j + AHEAD)
                act.wait_ge(s_used, S_WG)
                act.dma_start(p_sb[:], p_t[layer]).then_inc(S["p_loaded"], 16)
                for k in range(KD):
                    act.wait_ge(S["v_added"], GROUPS * KD - KD + k + 2)
                    if k == 0:
                        act.wait_ge(s_used, S_V_LAST)
                    nc.scalar.activation(act_hi[:, k, :], res[:, k, :], ACT.Copy).then_inc(S["act_hi_ready"], 1)
                act.wait_ge(S["p_loaded"], 16)
                nc.scalar.activation(p_hi[:], p_sb[:], ACT.Copy).then_inc(S["p_hi_ready"], 1)
                for i in range(KD):
                    if S_WG + i + AHEAD < N_SLABS:
                        split_hi(act, S_WG + i + AHEAD)
                    act.wait_ge(s_used, S_WG + i + 1)
                    nc.scalar.activation(gate_t[:, i, :], bank[i % RING][:], ACT.Sigmoid).then_inc(S["wg_evac"], 1)
                for i in range(KD):
                    act.wait_ge(s_used, S_WP + i // 4 + 1)
                    if i == 0:
                        act.wait_ge(s_used, S_WG + 1)
                    nc.scalar.activation(wide[:, i, :], bank[(i % 4)][:], ACT.Copy).then_inc(S["wp_evac"], 1)
                for k in range(KD):
                    act.wait_ge(S["wp_evac"], k + 1)
                    nc.scalar.activation(squares[:, k, :], wide[:, k, :], ACT.Square).then_inc(S["sq_ready"], 1)
                norm_std(act, "ple", 1, 1.0 / D)
                act.wait_ge(S["layer_res"], KD)
                act.sem_inc(layer_end, 1)
                act.wait_ge(layer_go, 1)
                act.sem_inc(layer_seen, 1)
            act_squares(act, res, KD, squares)
            norm_std(act, "in", 1, 1.0 / D)

        @block.tensor
        def _(pe):
            pe.wait_ge(consts_loaded, 16)
            with pe.Fori(0, DEPTH) as layer:
                norm_sums(pe, "in", 1, KD, squares)
                norm_spread(pe, "in", 1)
                for n in range(RING):
                    slab_product(pe, n, n, bank[n][:], act_hi, act_lo, 0 if n == 0 else None)
                with pe.Fori(0, 6) as q:
                    for k in range(RING):
                        pe.wait_ge(S["win_evac"], q * RING + k + 1)
                        slab_product(pe, q * RING + k + RING, k, bank[k][:], act_hi, act_lo)
                pe.wait_ge(S["wba_lo_ready"], 1)
                for t in range(NT):
                    for k in range(KD):
                        ts = slice(t * P, (t + 1) * P)
                        last = three_pass(bank[4][:, 8 * t:8 * t + 8], act_hi[:, k, ts], act_lo[:, k, ts],
                                          wba_hi[:, k, :], wba_lo[:, k, :], k == 0, k == KD - 1)
                last.then_inc(S["ba_ready"], 1)
                pe.wait_ge(S["gate_dve"], 6)
                nc.tensor.matmul(bank[4][:, 64:80], tri, gsm[:, 6, :], start=True, stop=True)
                nc.tensor.matmul(bank[4][:, 80:96], same_chunk, gsm[:, 6, :], start=True,
                                 stop=True).then_inc(S["gcol_ready"], 1)
                pe.wait_ge(S["gate_dve"], 7)
                pe.wait_ge(S["conv_done"], 12)
                pe.wait_ge(s_used, S_OUT)
                for i in range(12):
                    if i >= 2:
                        pe.wait_ge(S["nat_copied"], i - 1)
                    if i == 8:
                        pe.wait_ge(S["nat_copied"], 8)
                        norm_sums(pe, "qk", 2 * H, 1, sq_mix)
                        norm_spread(pe, "qk", 2 * H)
                        pe.wait_ge(S["norm_used"], used_seen("qk") + 2 * H)
                    src = (davt, gvt, gkt)[i // NT]
                    t = i % NT
                    for hd in range(H):
                        last = nc.tensor.transpose(heads((4, 7)[i % 2])[:, hd, :], src[:, hd, t * P:(t + 1) * P], ident)
                    last.then_inc(S["nat_ready"], 1)

                def attend(u, half):
                    if half == 0 and u > 0:
                        hd, t = divmod(u - 1, NT)
                        pe.wait_ge(S["at_trc"], u)
                        if t == 0 and hd > 0:
                            pe.wait_ge(S["at_oc"], hd)
                        for k in range(t + 1):
                            last = nc.tensor.matmul(bank[4][:, t * P:(t + 1) * P], v_nat[:, k, hd, :], at_wt[:, k, :],
                                                    start=k == 0, stop=k == t)
                        last.then_inc(S["at_out"], 1)
                    if u == H * NT:
                        return
                    hd, t = divmod(u, NT)
                    kl = (t + 1) * P
                    if half == 0:
                        if u > 0:
                            pe.wait_ge(S["at_dve"], 1 + 2 * u)
                        for c in range(2):
                            cs = slice(c * DQK, (c + 1) * DQK)
                            nc.tensor.matmul(bank[c][:, 0:kl], daq[cs, hd, t * P:(t + 1) * P], dak[cs, hd, 0:kl],
                                             start=True, stop=True).then_inc(S["sc_ready"], 1)
                    else:
                        pe.wait_ge(S["at_wgt"], u + 1)
                        if u > 0:
                            pe.wait_ge(S["at_trc"], u)
                        for k in range(t + 1):
                            last = nc.tensor.transpose(heads(5)[:, k, :], at_w[:, k * P:(k + 1) * P], ident)
                        last.then_inc(S["at_tr"], 1)

                def four(out, lhs, rhs):
                    for hd in range(H):
                        last = nc.tensor.matmul(out[:, hd, :], lhs[:, hd, :], rhs[:, hd, :], start=True, stop=True)
                    return last

                def delta(t, s):
                    ts = slice(t * P, (t + 1) * P)
                    b = 5 * t
                    if s == 0:
                        if t > 0:
                            pe.wait_ge(S["step_state"], 2 * t)
                            pe.wait_ge(S["og_copied"], 2 * t)
                        for hd in range(H):
                            col = gsm[:, 6, t * H + hd:t * H + hd + 1]
                            last = nc.tensor.matmul(heads(6)[:, hd, :], col.to_broadcast([P, P]), tri,
                                                    start=True, stop=True)
                        last.then_inc(S["gcb_ready"], 1)
                        for hd in range(H):
                            nc.tensor.matmul(heads(2)[:, hd, :], gkt[:, hd, ts], gkt[:, hd, ts], start=True, stop=True)
                        for hd in range(H):
                            last = nc.tensor.matmul(heads(3)[:, hd, :], gkt[:, hd, ts], gqt[:, hd, ts],
                                                    start=True, stop=True)
                        last.then_inc(S["gram_ready"], 1)
                    elif s == 2:
                        pe.wait_ge(S["low_ready"], t + 1)
                        for hd in range(H):
                            last = nc.tensor.transpose(heads(7)[:, hd, :], low64[:, hd, :], ident)
                        last.then_inc(S["lowt_ready"], 1)
                    elif s == 3:
                        pe.wait_ge(S["pow_ready"], b + 1)
                        four(heads(2), pow_n, pow_m)
                        four(heads(7), pow_m, pow_n).then_inc(S["inv_pe"], 1)
                    elif s == 4:
                        pe.wait_ge(S["pow_ready"], b + 2)
                        four(heads(6), pow_m2, inv_a)
                        four(heads(2), pow_n2, pow_m2)
                        four(heads(7), pow_m2, pow_n2).then_inc(S["inv_pe"], 1)
                    elif s == 5:
                        pe.wait_ge(S["pow_ready"], b + 3)
                        four(heads(6), pow_m, inv_b)
                        four(heads(2), pow_n, pow_m).then_inc(S["inv_pe"], 1)
                    elif s == 6:
                        pe.wait_ge(S["pow_ready"], b + 4)
                        four(heads(6), pow_m2, inv_a).then_inc(S["inv_pe"], 1)
                    elif s in (7, 9):
                        i = (s - 7) // 2
                        low, cur = ((low32, inv_b), (low64, inv_a))[i]
                        pe.wait_ge(S["inv_dve"], 6 * t + 1 + 3 * i)
                        four(heads(2), low, cur)
                        for hd in range(H):
                            last = nc.tensor.transpose(heads(7)[:, hd, :], cur[:, hd, :], ident)
                        last.then_inc(S["inv_pe"], 1)
                    elif s in (8, 10):
                        pe.wait_ge(S["inv_dve"], 6 * t + 3 + 3 * ((s - 8) // 2))
                        four(heads(6), inv_t, zmat).then_inc(S["inv_pe"], 1)
                    elif s == 11:
                        pe.wait_ge(S["pow_ready"], b + 5)
                        pe.wait_ge(S["rhs_ready"], 16 * (t + 1))
                        four(heads(2), inv_b, vbeta)
                        four(heads(7), kbg, inv_b).then_inc(S["uw_ready"], 1)
                    elif s >= 12:
                        j = (s - 12) // 2
                        c = 2 * t + j
                        rows = slice(j * CHUNK, (j + 1) * CHUNK)
                        s_in = state[c % 2]
                        if s % 2 == 0:
                            pe.wait_ge(S["uw_copied"], 2 * t + 2)
                            if c == 0:
                                pe.wait_ge(S["state_zero"], 1)
                            else:
                                pe.wait_ge(S["step_state"], c)
                            for hd in range(H):
                                last = nc.tensor.matmul(heads(6)[rows, hd, :], w_tr[:, hd, rows], s_in[:, hd, :],
                                                        start=True, stop=True)
                            last.then_inc(S["step_v"], 1)
                        else:
                            pe.wait_ge(S["step_vn"], c + 1)
                            if c > 0:
                                pe.wait_ge(S["og_copied"], c)
                            for hd in range(H):
                                out = bank[3][:, hd * CHUNK:(hd + 1) * CHUNK]
                                nc.tensor.matmul(out, s_in[:, hd, :], qdec[:, hd, rows], start=True, stop=False)
                                last = nc.tensor.matmul(out, vnew[rows, hd, :], intra[rows, hd, rows],
                                                        start=False, stop=True)
                            for hd in range(H):
                                last = nc.tensor.matmul(heads(2)[:, hd, :], kdec[rows, hd, :], vnew[rows, hd, :],
                                                        start=True, stop=True)
                            last.then_inc(S["step_so"], 1)

                pe.wait_ge(S["nat_copied"], 12)
                mixer(delta, attend)
                pe.wait_ge(S["at_oc"], H)
                norm_sums(pe, "mix", 2 * H, 1, sq_mix)
                norm_spread(pe, "mix", 2 * H)
                for i in range(KD):
                    if i >= RING:
                        pe.wait_ge(S["wout_added"], i - RING + 1)
                    slab_product(pe, S_OUT + i, i % RING, bank[i % RING][:], act_hi, act_lo, KD if i == 0 else None)
                norm_sums(pe, "ffn", 1, KD, squares)
                norm_spread(pe, "ffn", 1)
                for k in range(RING):
                    slab_product(pe, S_WQ + k, k, bank[k][:], act_hi, act_lo, 2 * KD if k == 0 else None)
                with pe.Fori(0, 3) as q:
                    for k in range(RING):
                        pe.wait_ge(S["wq_evac"], q * RING + k + 1)
                        slab_product(pe, q * RING + k + S_WQ + RING, k, bank[k][:], act_hi, act_lo)
                pe.wait_ge(S["subk_ready"], 16)
                pe.wait_ge(S["wq_evac"], 2 * PH)
                for t in range(NT):
                    if t > 0:
                        pe.wait_ge(S["score_read"], t)
                    for i in range(2 * PH):
                        last = nc.tensor.matmul(heads(4 + i // 4)[:, i % 4, :], qt[:, i, t * P:(t + 1) * P],
                                                subk[:, i, :], start=True, stop=True)
                    last.then_inc(S["score_ready"], 1)
                    pe.wait_ge(S["tk_dve"], 3 * t + 3)
                    for i in range(3):
                        last = nc.tensor.transpose(heads(0)[:, i, :], sel[:, i, :], ident)
                    last.then_inc(S["selt_ready"], 1)
                pe.sem_inc(S["gm_ready"], 4)
                pe.sem_inc(S["gm_copied"], 4)
                with pe.Fori(0, NT) as q:
                    for b in range(P // 8):
                        pe.wait_ge(S["hot1_ready"], q * (P // 8) + b + 1)
                        pe.wait_ge(S["hot2_ready"], q * (P // 8) + b + 1)
                        for half in range(2):
                            i = 2 * b + half
                            pe.wait_ge(S["gm_copied"], q * (P // 4) + i + 1)
                            for s in range(4):
                                tok = 4 * half + s
                                last = nc.tensor.matmul(heads(4 + i % 4)[:, s, :], hot1[b % 2][:, tok, :],
                                                        hot2[b % 2][:, tok, :], start=True, stop=True)
                            last.then_inc(S["gm_ready"], 1)

                def u_slab(g, j, n, slot):
                    if not (isinstance(g, int) and g * GB + j < 2):
                        pe.wait_ge(S["u_gelu"], g * GB + j - 1)
                    slab_product(pe, n, slot, bank[2 * (j % 2)][:], act_hi, act_lo)

                def v_slab(g, pg, j, n, slot):
                    pe.wait_ge(S["w_lo_ready"], g * GB + GB)
                    if j > 0:
                        pe.wait_ge(S["v_added"], g * GB + j)
                    slab_product(pe, n, slot, bank[1 + 2 * (j % 2)][:], w_hi[pg], w_lo[pg])

                for j in range(GB):
                    u_slab(0, j, S_U0 + j, j % RING)

                def group(g, pg):
                    for j in range(GB):
                        n = g * 16 + (S_UV - 16 + 2 * j)
                        u_slab(g, j, n, 2 * j % RING)
                        v_slab(g - 1, 1 - pg, j, n + 1, (2 * j + 1) % RING)
                with pe.Fori(0, 7) as it:
                    group(it * 2 + 1, 1)
                    group(it * 2 + 2, 0)
                group(15, 1)
                for j in range(GB):
                    v_slab(15, 1, j, S_V_LAST + j, j % RING)
                for i in range(KD):
                    if i >= RING:
                        pe.wait_ge(S["wg_evac"], i - RING + 1)
                    slab_product(pe, S_WG + i, i % RING, bank[i % RING][:], act_hi, act_lo, 3 * KD if i == 0 else None)
                pe.wait_ge(S["p_lo_ready"], 1)
                for s in range(2):
                    n = S_WP + s
                    pe.wait_ge(s_slab_lo, n + 1)
                    for i in range(4):
                        pe.wait_ge(S["wg_evac"], KD - 3 + i) if s == 0 else pe.wait_ge(S["wp_evac"], i + 1)
                        if s == 0:
                            pe.wait_ge(S["wg_evac"], 5 + i)
                        for k in range(2):
                            last = three_pass(bank[i][:], whi[n % RING][:, 2 * i + k, :], wlo[n % RING][:, 2 * i + k, :],
                                              p_hi[:, k, :], p_lo[:, k, :], k == 0, k == 1)
                    last.then_inc(s_used, 1)
                norm_sums(pe, "ple", 1, KD, squares)
                norm_spread(pe, "ple", 1)
                pe.wait_ge(S["layer_res"], KD)
                pe.sem_inc(layer_end, 1)
                pe.wait_ge(layer_go, 1)
                pe.sem_inc(layer_seen, 1)
            norm_sums(pe, "in", 1, KD, squares)
            norm_spread(pe, "in", 1)

        @block.vector
        def _(dve):
            V = nc.vector
            dve.wait_ge(consts_loaded, 16)
            dve.wait_ge(x_loaded, 16)
            with dve.Fori(0, DEPTH) as layer:
                for n in range(AHEAD):
                    split_lo(dve, n)
                dve.wait_ge(s_par, 16)
                lamv = par[:, Q_LAM:Q_LAM + 4 * DQK].rearrange("p (i c) -> p i c", i=4)
                V.tensor_tensor_reduce(lam[:, 0:DQK], lamv[:, 0, :], lamv[:, 1, :], 1.0, 0.0, ALU.mult, ALU.add,
                                       lam[:, 64:65]).then_inc(S["lam_dve"], 1)
                dve.wait_ge(S["lam_dve"], 1)
                V.tensor_tensor_reduce(lam[:, 0:DQK], lamv[:, 2, :], lamv[:, 3, :], 1.0, 0.0, ALU.mult, ALU.add,
                                       lam[:, 65:66]).then_inc(S["lam_dve"], 1)
                norm_rs(dve, "in", 1)
                scale_to_wide(dve, "in", Q_MIX, 0)
                dve.wait_ge(S["wba_hi_ready"], 1)
                V.tensor_tensor(wba_lo[:], wba[:], wba_hi[:].bitcast(F32), ALU.subtract).then_inc(S["wba_lo_ready"], 1)
                for n in range(28):
                    split_lo(dve, n + AHEAD)
                    if 12 <= n < 24:
                        c = n - 12
                        dst = (gqt, gkt, gvt)[c // H][:, c % H, :]
                        dve.wait_ge(S["win_evac"], n + 1)
                        taps = [par[:, Q_CONV + tap * 12 + c:Q_CONV + tap * 12 + c + 1] for tap in range(CONV_K)]
                        V.tensor_scalar(dst, craw[c % 2][:], taps[3], None, ALU.mult).then_inc(S["conv_chain"], 1)
                        for lag in range(1, CONV_K):
                            dve.wait_ge(S["conv_chain"], 3 * c + lag)
                            i = V.scalar_tensor_tensor(dst[:, lag:T], craw[c % 2][:, 0:T - lag], taps[3 - lag],
                                                       dst[:, lag:T], ALU.mult, ALU.add)
                            i.then_inc(S["conv_chain"] if lag < 3 else S["conv_acc"], 1)
                dve.wait_ge(S["conv_acc"], 12)
                dve.sem_inc(S["at_dve"], 1)
                dve.wait_ge(S["ba_ready"], 1)
                ba = gsm[:, 12:14, :].rearrange("p r (t c) -> p (r t) c", c=2 * H)

                def small(i):
                    return gsm[:, i, :].rearrange("p (t c) -> p t c", t=NT)
                gd = S["gate_dve"]
                V.tensor_copy(gsm[:, 12:14, :], bank[4][:, 0:32].rearrange("p (r c) -> p r c", r=2)).then_inc(gd, 1)
                dve.wait_ge(gd, 1)
                V.tensor_tensor(small(2), ba[:, :, H:2 * H], par[:, Q_DT:Q_DT + H].unsqueeze(1).to_broadcast([P, NT, H]),
                                ALU.add).then_inc(gd, 1)
                dve.wait_ge(gd, 2)
                V.tensor_scalar(gsm[:, 3, :], gsm[:, 2, :], 0.0, None, ALU.max).then_inc(gd, 1)
                V.scalar_tensor_tensor(gsm[:, 4, :], gsm[:, 2, :], -1.0, gsm[:, 2, :], ALU.mult, ALU.min).then_inc(gd, 1)
                dve.wait_ge(S["gate_act"], 4)
                dve.wait_ge(gd, 4)
                V.tensor_tensor(gsm[:, 5, :], gsm[:, 3, :], gsm[:, 4, :], ALU.add).then_inc(gd, 1)
                dve.wait_ge(gd, 5)
                V.scalar_tensor_tensor(small(6), small(5), -1.0, gsm[:, 1, 0:H].unsqueeze(1).to_broadcast([P, NT, H]),
                                       ALU.mult, ALU.mult).then_inc(gd, 1)
                dve.wait_ge(S["gcol_ready"], 1)
                V.tensor_copy(gsm[:, 14:16, :], bank[4][:, 64:96].rearrange("p (r c) -> p r c", r=2)).then_inc(gd, 1)
                dve.wait_ge(gd, 7)
                V.tensor_tensor(gsm[:, 8, :], gsm[:, 15, :], gsm[:, 14, :], ALU.subtract).then_inc(gd, 1)
                dve.wait_ge(S["gate_act"], 5)
                V.tensor_tensor(gsm[:, 11, :], gsm[:, 0, :], gsm[:, 7, :], ALU.mult).then_inc(gd, 1)
                dve.wait_ge(S["lam_act"], 1)
                V.tensor_tensor(lam[:, 68:69], lam[:, 66:67], lam[:, 67:68], ALU.subtract).then_inc(S["lam_dve"], 1)
                dve.wait_ge(S["lam_dve"], 3)
                V.tensor_tensor(lam[:, 69:70], lam[:, 68:69], par[:, Q_LINIT:Q_LINIT + 1], ALU.add).then_inc(S["lam_dve"], 1)
                V.tensor_tensor(lam[:, 70:71], par[:, Q_SUB:Q_SUB + 1], par[:, Q_LINIT + 1:Q_LINIT + 2],
                                ALU.mult).then_inc(S["lam_dve"], 1)
                norm_rs(dve, "qk", 2 * H)
                for j in range(2 * H):
                    dve.wait_ge(S["rstd_bc"], bc_seen("qk") + j + 1)
                    x = (gqt if j < H else gkt)[:, j % H, :]
                    V.scalar_tensor_tensor(x, x, P ** -0.5 if j < H else 1.0, bank[5 + j % 2][:], ALU.mult,
                                           ALU.mult).then_inc(S["norm_used"], 1)

                ad = S["at_dve"]
                aw = {"max": 0}
                SLOPE = [2.0 ** (-8.0 * (i + 1) / H) for i in range(H)]

                def attend(u, half):
                    if u == H * NT:
                        return
                    hd, t = divmod(u, NT)
                    kl = (t + 1) * P
                    if half == 1:
                        weights(u, kl)
                        return
                    if u > 0:
                        dve.wait_ge(S["at_wgt"], u)
                        dve.wait_ge(S["at_exp"], 2 * u)
                    bias = consts[:, C_DIST + T - kl:C_DIST + T]
                    for c in range(2):
                        dve.wait_ge(S["sc_ready"], 2 * u + c + 1)
                        V.scalar_tensor_tensor(at_s[:, c, 0:kl], bias, SLOPE[hd] * DQK ** 0.5, bank[c][:, 0:kl],
                                               ALU.mult, ALU.add).then_inc(ad, 1)
                    for c in range(2):
                        dve.wait_ge(ad, 1 + 2 * u + c + 1)
                        V.tensor_reduce(at_c[:, 4 + c:5 + c], at_s[:, c, 0:kl], AX_X, ALU.max).then_inc(S["at_oc2"], 1)
                    for c in range(2):
                        dve.wait_ge(S["at_oc2"], 2 * u + c + 1)
                        V.tensor_scalar(at_c[:, c:c + 1], at_c[:, 4 + c:5 + c], -DQK ** -0.5, None,
                                        ALU.mult).then_inc(S["at_max"], 1)

                def weights(u, kl):
                    dve.wait_ge(S["at_exp"], 2 * u + 2)
                    V.reciprocal(at_c[:, 4:6], at_c[:, 2:4]).then_inc(S["at_rec"], 1)
                    dve.wait_ge(S["at_rec"], 3 * u + 1)
                    V.tensor_tensor(at_c[:, 6:7], at_c[:, 5:6], lam[:, 69:70], ALU.mult).then_inc(S["at_rec"], 1)
                    dve.wait_ge(S["at_rec"], 3 * u + 2)
                    V.tensor_scalar(at_s[:, 1, 0:kl], at_s[:, 1, 0:kl], at_c[:, 6:7], None,
                                    ALU.mult).then_inc(S["at_rec"], 1)
                    dve.wait_ge(S["at_rec"], 3 * u + 3)
                    if u > 0:
                        dve.wait_ge(S["at_tr"], u)
                    V.scalar_tensor_tensor(at_w[:, 0:kl], at_s[:, 0, 0:kl], at_c[:, 4:5], at_s[:, 1, 0:kl],
                                           ALU.mult, ALU.subtract).then_inc(S["at_wgt"], 1)

                def delta(t, s):
                    if s == 0:
                        if t == 0:
                            V.memset(state[0][:], 0.0).then_inc(S["state_zero"], 1)
                        dve.wait_ge(S["gcb_ready"], t + 1)
                        for hd in range(H):
                            col = gsm[:, 14, t * H + hd:t * H + hd + 1]
                            V.scalar_tensor_tensor(dec_t[:, hd, :], heads(6)[:, hd, :], col,
                                                   consts[:, C_NEGT:C_NEGT + P],
                                                   ALU.subtract, ALU.add).then_inc(S["arg_ready"], 1)
                            V.scalar_tensor_tensor(dec[:, hd, :], heads(6)[:, hd, :], col,
                                                   consts[:, C_POSD:C_POSD + P],
                                                   ALU.subtract, ALU.add).then_inc(S["arg_ready"], 1)
                        for hd in range(H):
                            i = t * H + hd
                            V.tensor_scalar(vbeta[:, hd, :], gv_nat[:, t, hd, :], gsm[:, 0, i:i + 1], None,
                                            ALU.mult).then_inc(S["rhs_ready"], 1)
                            V.tensor_scalar(kbg[:, hd, :], kn_nat[:, t, hd, :], gsm[:, 11, i:i + 1], None,
                                            ALU.mult).then_inc(S["rhs_ready"], 1)
                            V.tensor_scalar(kdec[:, hd, :], kn_nat[:, t, hd, :], gsm[:, 9, i:i + 1], None,
                                            ALU.mult).then_inc(S["rhs_ready"], 1)
                    elif s == 1:
                        dve.wait_ge(S["dec_ready"], 3 * t + 3)
                        dve.wait_ge(S["gram_ready"], t + 1)
                        for hd in range(H):
                            V.scalar_tensor_tensor(low64[:, hd, :], heads(2)[:, hd, :],
                                                   gsm[:, 0, t * H + hd:t * H + hd + 1],
                                                   dec[:, hd, :], ALU.mult, ALU.mult).then_inc(S["low_dve"], 1)
                        V.tensor_tensor(intra[:], heads(3), dec_t[:], ALU.mult).then_inc(S["low_dve"], 1)
                        dve.wait_ge(S["low_dve"], 8 * t + 5)
                        V.tensor_tensor(pow_m[:], low64[:], over_heads(C_M16), ALU.mult).then_inc(S["low_ready"], 1)
                        V.tensor_tensor(low32[:], low64[:], over_heads(C_M32), ALU.mult).then_inc(S["low_dve"], 1)
                        for hd in range(H):
                            V.tensor_tensor(qdec[:, hd, :], gqt[:, hd, t * P:(t + 1) * P], egc_b[:, hd, :],
                                            ALU.mult).then_inc(S["rhs_ready"], 1)
                    elif s == 2:
                        dve.wait_ge(S["lowt_ready"], t + 1)
                        V.tensor_tensor(pow_n[:], heads(7), over_heads(C_M16), ALU.mult).then_inc(S["low_dve"], 1)
                        V.tensor_tensor(low64[:], low64[:], over_heads(C_M64), ALU.mult).then_inc(S["low_dve"], 1)
                        dve.wait_ge(S["low_dve"], 8 * t + 8)
                        V.tensor_tensor(inv_a[:], over_heads(C_ID), pow_n[:], ALU.subtract).then_inc(S["pow_ready"], 1)
                    elif s == 3:
                        dve.wait_ge(S["inv_pe"], 8 * t + 1)
                        V.tensor_copy(pow_m2[:], heads(2)).then_inc(S["inv_cp"], 1)
                        V.tensor_copy(pow_n2[:], heads(7)).then_inc(S["pow_ready"], 1)
                    elif s == 4:
                        dve.wait_ge(S["inv_pe"], 8 * t + 2)
                        V.tensor_copy(pow_m[:], heads(2)).then_inc(S["inv_cp"], 1)
                        V.tensor_copy(pow_n[:], heads(7)).then_inc(S["inv_cp"], 1)
                        V.tensor_tensor(inv_b[:], inv_a[:], heads(6), ALU.add).then_inc(S["pow_ready"], 1)
                    elif s == 5:
                        dve.wait_ge(S["inv_pe"], 8 * t + 3)
                        V.tensor_copy(pow_m2[:], heads(2)).then_inc(S["inv_cp"], 1)
                        dve.wait_ge(S["pow_ready"], 5 * t + 3)
                        V.tensor_tensor(inv_a[:], inv_b[:], heads(6), ALU.add).then_inc(S["pow_ready"], 1)
                    elif s == 6:
                        dve.wait_ge(S["inv_pe"], 8 * t + 4)
                        dve.wait_ge(S["pow_ready"], 5 * t + 4)
                        V.tensor_tensor(inv_b[:], inv_a[:], heads(6), ALU.add).then_inc(S["inv_dve"], 1)
                    elif s in (7, 9):
                        dve.wait_ge(S["inv_pe"], 8 * t + s - 2)
                        V.tensor_copy(zmat[:], heads(2)).then_inc(S["inv_dve"], 1)
                        V.tensor_copy(inv_t[:], heads(7)).then_inc(S["inv_dve"], 1)
                    elif s in (8, 10):
                        i = (s - 8) // 2
                        cur, new = ((inv_b, inv_a), (inv_a, inv_b))[i]
                        dve.wait_ge(S["inv_pe"], 8 * t + s - 2)
                        dve.wait_ge(S["inv_dve"], 6 * t + 1 + 3 * i)
                        V.tensor_tensor(new[:], cur[:], heads(6), ALU.subtract).then_inc(
                            S["inv_dve"] if i == 0 else S["pow_ready"], 1)
                    elif s == 11:
                        dve.wait_ge(S["uw_ready"], t + 1)
                        V.tensor_copy(u_sb[:], heads(2)).then_inc(S["uw_copied"], 1)
                    else:
                        j = (s - 12) // 2
                        c = 2 * t + j
                        rows = slice(j * CHUNK, (j + 1) * CHUNK)
                        if s % 2 == 0:
                            dve.wait_ge(S["step_v"], c + 1)
                            dve.wait_ge(S["uw_copied"], 2 * t + 2)
                            V.tensor_tensor(vnew[rows], u_sb[rows], heads(6)[rows], ALU.subtract).then_inc(S["step_vn"], 1)
                        else:
                            dve.wait_ge(S["step_so"], c + 1)
                            end = j * CHUNK + CHUNK - 1
                            for hd in range(H):
                                i = V.scalar_tensor_tensor(state[(c + 1) % 2][:, hd, :], state[c % 2][:, hd, :],
                                                           egc_b[:, hd, end:end + 1], heads(2)[:, hd, :],
                                                           ALU.mult, ALU.add)
                            i.then_inc(S["step_state"], 1)

                dve.wait_ge(S["nat_copied"], 12)
                dve.wait_ge(S["lam_dve"], 5)
                mixer(delta, attend)
                norm_rs(dve, "mix", 2 * H)
                for j in range(2 * H):
                    dve.wait_ge(S["rstd_bc"], bc_seen("mix") + j + 1)
                    gain = lam[:, 70:71] if j < H else par[:, Q_GDN:Q_GDN + 1]
                    i = V.scalar_tensor_tensor(mixt[:, j, :], mixt[:, j, :], gain, bank[5 + j % 2][:], ALU.mult, ALU.mult)
                    i.then_inc(S["norm_used"], 1)
                for j in range(2 * H):
                    dve.wait_ge(S["norm_used"], used_seen("mix") + j + 1)
                    if j >= H:
                        V.tensor_tensor(mixt[:, j, :], mixt[:, j, :], gzt[:, j - H, :], ALU.mult).then_inc(S["mix_ready"], 1)
                act_low(dve, mixt, KD)
                for i in range(KD):
                    split_lo(dve, S_OUT + i + AHEAD)
                    dve.wait_ge(s_used, S_OUT + i + 1)
                    V.tensor_tensor(res[:, i, :], res[:, i, :], bank[i % RING][:], ALU.add).then_inc(S["wout_added"], 1)
                norm_rs(dve, "ffn", 1)
                dve.wait_ge(S["wout_added"], KD)
                scale_to_wide(dve, "ffn", Q_FFN, 2 * KD)
                for i in range(2 * PH):
                    split_lo(dve, S_WQ + i + AHEAD)

                tks = S["tk_chain"]
                tk = {"n": 0}

                def step(ins):
                    tk["n"] += 1
                    ins.then_inc(tks, 1)

                def settle():
                    dve.wait_ge(tks, tk["n"])

                def score(i):
                    return heads(4 + i // 4)[:, i % 4, :]

                for t in range(NT):
                    dve.wait_ge(S["score_ready"], t + 1)
                    tv = topv[:].rearrange("p h c k -> p (h c) k")
                    ti = topi[:].rearrange("p h c k -> p (h c) k")
                    for i in range(2 * PH):
                        step(V.max(tv[:, i, 0:8], score(i)))
                    settle()
                    for i in range(2 * PH):
                        step(V.match_replace(rest[:, i, :], tv[:, i, 0:8], score(i), NEG))
                        step(V.max_index(ti[:, i, 0:8], tv[:, i, 0:8], score(i)))
                    settle()
                    dve.sem_inc(S["score_read"], 1)
                    for i in range(2 * PH):
                        step(V.max(tv[:, i, 8:16], rest[:, i, :]))
                    settle()
                    for i in range(2 * PH):
                        step(V.max_index(ti[:, i, 8:16], tv[:, i, 8:16], rest[:, i, :]))
                    settle()
                    step(V.tensor_copy(topf[:], topi[:]))
                    settle()
                    step(V.tensor_scalar(topf[:, :, 0, :], topf[:, :, 0, :], float(NKEYS), None, ALU.mult))
                    settle()
                    for a in range(TOPK):
                        if a >= 8 and a > 8:
                            continue
                        if a == 8:
                            o, n = CAND_AT[8], TOPK - 8
                            for dst, src in ((cand, topv), (cidx, topf)):
                                step(V.tensor_tensor(dst[:, :, o:o + n], src[:, :, 0, 8:TOPK],
                                                     src[:, :, 1, 0:1].to_broadcast([P, PH, n]), ALU.add))
                            continue
                        o, n = CAND_AT[a], CAND_ROWS[a]
                        for dst, src in ((cand, topv), (cidx, topf)):
                            step(V.tensor_tensor(dst[:, :, o:o + n], src[:, :, 1, 0:n],
                                                 src[:, :, 0, a:a + 1].to_broadcast([P, PH, n]), ALU.add))
                    settle()
                    for i in range(PH):
                        step(V.max(winv[:, i, 0:8], cand[:, i, :]))
                    settle()
                    for i in range(PH):
                        step(V.match_replace(crest[:, i, :], winv[:, i, 0:8], cand[:, i, :], NEG))
                        step(V.max_index(winp[:, i, 0:8], winv[:, i, 0:8], cand[:, i, :]))
                    settle()
                    for i in range(PH):
                        step(V.max(winv[:, i, 8:16], crest[:, i, :]))
                    settle()
                    for i in range(PH):
                        step(V.max_index(winp[:, i, 8:16], winv[:, i, 8:16], crest[:, i, :]))
                    settle()
                    step(V.tensor_copy(winf[:], winp[:]))
                    V.tensor_copy(gsum[:], winv[:, :, 0]).then_inc(S["tk_dve"], 1)
                    dve.wait_ge(S["tk_dve"], 3 * t + 1)
                    settle()
                    V.tensor_tensor(winv[:], winv[:], gsum[:].unsqueeze(2).to_broadcast([P, PH, TOPK]),
                                    ALU.subtract).then_inc(S["tk_dve"], 1)
                    for half in range(2):
                        hs = slice(half * PH // 2, (half + 1) * PH // 2)
                        oh = onehot[:].rearrange("p (h k) c -> p h k c", h=PH // 2)
                        for i, hd in enumerate(range(half * PH // 2, (half + 1) * PH // 2)):
                            step(V.tensor_tensor(oh[:, i], winf[:, hd, :].unsqueeze(2).to_broadcast([P, TOPK, NC]),
                                                 consts[:, C_POS:C_POS + NC].unsqueeze(1).to_broadcast([P, TOPK, NC]),
                                                 ALU.is_equal))
                        settle()
                        for i, hd in enumerate(range(half * PH // 2, (half + 1) * PH // 2)):
                            step(V.tensor_tensor(oh[:, i], oh[:, i], cidx[:, hd, :].unsqueeze(1).to_broadcast([P, TOPK, NC]),
                                                 ALU.mult))
                        settle()
                        step(V.tensor_reduce(expert[:, half * 64:half * 64 + 64], onehot[:], AX_X, ALU.add))
                        settle()
                    step(V.tensor_copy(exp_i[:], expert[:]))
                    dve.wait_ge(S["tk_act"], t + 1)
                    step(V.tensor_reduce(gsum[:], winv[:], AX_X, ALU.add))
                    settle()
                    step(V.tensor_scalar(exp_j[:], exp_i[:], 7, None, ALU.logical_shift_right))
                    step(V.tensor_scalar(exp_i[:], exp_i[:], 127, None, ALU.bitwise_and))
                    step(V.reciprocal(gsum[:], gsum[:]))
                    settle()
                    if t > 0:
                        dve.wait_ge(S["selt_ready"], t)
                    step(V.tensor_copy(sel[:, 0, :], exp_j[:]))
                    step(V.tensor_copy(sel[:, 1, :], exp_i[:]))
                    V.tensor_tensor(sel[:, 2, :].rearrange("p (h k) -> p h k", h=PH), winv[:],
                                    gsum[:].unsqueeze(2).to_broadcast([P, PH, TOPK]), ALU.mult).then_inc(tks, 1)
                    tk["n"] += 1
                    settle()
                    dve.sem_inc(S["tk_dve"], 1)
                    dve.wait_ge(S["selt_ready"], t + 1)
                    V.tensor_copy(selt[:, :, t * P:(t + 1) * P], heads(0)[:, 0:3, :]).then_inc(S["selt_copied"], 1)
                dve.wait_ge(S["selt_copied"], NT)
                settle()
                dve.sem_inc(S["stored_a"], 1)
                dve.sem_inc(S["stored_b"], 1)
                with dve.Fori(0, NT) as q:
                    for b in range(P // 8):
                        dve.wait_ge(S["gm_ready"], q * (P // 4) + 2 * b + 2)
                        V.tensor_tensor(hot1[b % 2][:, 0:DVE_HOT1, :], iota.unsqueeze(1).to_broadcast([P, DVE_HOT1, NKEYS]),
                                        selt[:, 0, bass.ds(q * P + 8 * b, DVE_HOT1)].unsqueeze(2).to_broadcast(
                                            [P, DVE_HOT1, NKEYS]), ALU.is_equal)
                        for tok in range(8):
                            at_tok = q * P + (8 * b + tok)
                            last = V.tensor_scalar(hot2[b % 2][:, tok, :], iota, selt[:, 1, bass.ds(at_tok, 1)],
                                                   selt[:, 2, bass.ds(at_tok, 1)], ALU.is_equal, ALU.mult)
                        last.then_inc(S["hot2_ready"], 1)

                dve.sem_inc(S["v_added"], 1)

                def weigh(g, j):
                    dve.wait_ge(S["u_gelu"], g * GB + j + 1)
                    dve.wait_ge(g_loaded[j // 2], g * 16 + 16)
                    aw_ = act_w[j % 2][:].rearrange("p (s t) -> p s t", t=TG)
                    V.tensor_tensor(aw_, aw_, g_sb[j // 2][:, :, j % 2, :], ALU.mult).then_inc(S["w_ready"], 1)

                def w_low(g, j, pg):
                    dve.wait_ge(S["w_hi_ready"], g * GB + j + 1)
                    V.tensor_tensor(w_lo[pg][:, j, :], act_w[j % 2][:], w_hi[pg][:, j, :].bitcast(F32),
                                    ALU.subtract).then_inc(S["w_lo_ready"], 1)

                def add_block(j, used):
                    dve.wait_ge(s_used, used)
                    V.tensor_tensor(res[:, j, :], res[:, j, :], bank[1 + 2 * (j % 2)][:], ALU.add).then_inc(S["v_added"], 1)

                for j in range(GB):
                    split_lo(dve, S_U0 + j + AHEAD)
                    weigh(0, j)
                    w_low(0, j, 0)

                def group(g, pg):
                    for j in range(GB):
                        n = g * 16 + (S_UV - 16 + 2 * j)
                        split_lo(dve, n + AHEAD, (2 * j + AHEAD) % RING)
                        weigh(g, j)
                        w_low(g, j, pg)
                        split_lo(dve, n + 1 + AHEAD, (2 * j + 1 + AHEAD) % RING)
                        add_block(j, n + 2)
                with dve.Fori(0, 7) as it:
                    group(it * 2 + 1, 1)
                    group(it * 2 + 2, 0)
                group(15, 1)
                for j in range(GB):
                    split_lo(dve, S_V_LAST + j + AHEAD)
                    add_block(j, S_V_LAST + j + 1)
                act_low(dve, res, 3 * KD)
                dve.wait_ge(S["p_hi_ready"], 1)
                V.tensor_tensor(p_lo[:], p_sb[:], p_hi[:].bitcast(F32), ALU.subtract).then_inc(S["p_lo_ready"], 1)
                for n in range(S_WG + AHEAD, N_SLABS):
                    split_lo(dve, n)
                norm_rs(dve, "ple", 1)
                dve.wait_ge(S["rstd_bc"], bc_seen("ple") + 1)
                dve.wait_ge(S["wp_evac"], KD)
                dve.wait_ge(S["wg_evac"], KD)
                dve.wait_ge(S["ss_ready"], nth("ple") + 1)
                pd = S["ple_dve"]
                for k in range(KD):
                    V.scalar_tensor_tensor(wide[:, k, :], wide[:, k, :], par[:, Q_PLE + k:Q_PLE + k + 1], bank[5][:],
                                           ALU.mult, ALU.mult).then_inc(pd, 1)
                for k in range(KD):
                    dve.wait_ge(pd, k + 1)
                    V.tensor_tensor(wide[:, k, :], wide[:, k, :], gate_t[:, k, :], ALU.mult).then_inc(pd, 1)
                for k in range(KD):
                    dve.wait_ge(pd, KD + k + 1)
                    V.tensor_tensor(res[:, k, :], res[:, k, :], wide[:, k, :], ALU.add).then_inc(S["layer_res"], 1)
                dve.wait_ge(S["layer_res"], KD)
                dve.sem_inc(layer_end, 1)
                dve.wait_ge(layer_go, 1)
                dve.sem_inc(layer_seen, 1)
            norm_rs(dve, "in", 1)
            dve.wait_ge(S["rstd_bc"], 1)
            for k in range(KD):
                nc.vector.scalar_tensor_tensor(wide[:, k, :], res[:, k, :], par[:, Q_FIN + k:Q_FIN + k + 1], bank[5][:],
                                               ALU.mult, ALU.mult).then_inc(out_ready, 1)


def constants():
    import numpy as np
    c = np.zeros((P, NCONST), np.float32)
    i = np.arange(P)
    row, col = i[:, None], i[None, :]
    same = row // CHUNK == col // CHUNK
    c[:, C_ID:C_ID + P] = row == col
    c[:, C_ONE:C_ONE + P] = 1
    c[:, C_TRI:C_TRI + P] = (row <= col) & same
    c[:, C_CHUNK:C_CHUNK + P] = same
    c[:, C_NEGT:C_NEGT + P] = np.where((row <= col) & same, 0, NEG)
    c[:, C_POSD:C_POSD + P] = np.where((col < row) & same, 0, -NEG)
    c[:, C_M16:C_M16 + P] = row // 16 == col // 16
    c[:, C_M32:C_M32 + P] = (row // 32 == col // 32) & (row // 16 != col // 16)
    c[:, C_M64:C_M64 + P] = same & (row // 32 != col // 32)
    j = np.arange(T)[None, :] - (T - P)
    c[:, C_DIST:C_DIST + T] = np.where(j <= row, j - row, NEG)
    c[:, C_IOTA:C_IOTA + P] = col
    c[:, C_POS:C_POS + NC] = np.arange(NC)
    c[:, C_EPS] = EPS
    return c


def kernel(**inputs):
    import math
    import numpy as np
    import concourse.bacc as bacc
    from concourse.bass_utils import run_bass_kernel_spmd

    a = {k: np.asarray(v) for k, v in inputs.items()}

    def by_columns(w):
        n = w.shape[1] // P
        return w.reshape(-1, P, n, P).transpose(2, 1, 0, 3)

    def chunked(v):
        return v.reshape(-1, P).T

    slabs = np.empty((DEPTH, N_SLABS, P, KD, P), np.float32)
    w_ba = np.empty((DEPTH, P, KD, 8), np.float32)
    subkeys = np.empty((DEPTH, P, 2 * PH, NKEYS), np.float32)
    params = np.zeros((DEPTH, P, NPAR), np.float32)
    for i in range(DEPTH):
        w_in = a["w_in"][i]
        slabs[i, S_IN:S_OUT] = by_columns(w_in[:, :28 * P])
        w_ba[i] = w_in[:, 28 * P:].reshape(KD, P, 8).transpose(1, 0, 2)
        slabs[i, S_OUT:S_WQ] = by_columns(a["w_out"][i])
        slabs[i, S_WQ:S_U0] = by_columns(a["peer_wq"][i])
        u = a["peer_u"][i].reshape(NKEYS, NKEYS, KD, P).transpose(1, 3, 2, 0)
        v = a["peer_v"][i].reshape(NKEYS, GROUPS, GB, KD, P).transpose(1, 3, 0, 2, 4).reshape(-1, P, GB, P)
        slabs[i, S_U0:S_UV] = u[:GB]
        slabs[i, S_UV:S_V_LAST:2] = u[GB:]
        slabs[i, S_UV + 1:S_V_LAST:2] = v[:(GROUPS - 1) * KD]
        slabs[i, S_V_LAST:S_WG] = v[(GROUPS - 1) * KD:]
        slabs[i, S_WG:S_WP] = by_columns(a["ple_wg"][i])
        wp = by_columns(a["ple_wp"][i])
        slabs[i, S_WP:] = wp.reshape(2, 4, P, 2, P).transpose(0, 2, 1, 3, 4).reshape(2, P, KD, P)
        subkeys[i] = a["peer_subkeys"][i].reshape(2 * PH, NKEYS, P).transpose(2, 0, 1)
        q = params[i]
        q[:, Q_MIX:Q_MIX + 8] = chunked(a["ln_mix_g"][i])
        q[:, Q_FFN:Q_FFN + 8] = chunked(a["ln_ffn_g"][i])
        q[:, Q_PLE:Q_PLE + 8] = chunked(a["ple_norm_g"][i])
        q[:, Q_FIN:Q_FIN + 8] = chunked(a["final_norm_g"])
        for tap in range(CONV_K):
            q[:, Q_CONV + 12 * tap:Q_CONV + 12 * tap + 12] = chunked(a["conv_w"][i, tap])
        q[:, Q_GDN] = a["gdn_norm_g"][i]
        q[:, Q_SUB] = a["diff_subln_g"][i]
        q[:, Q_ALOG:Q_ALOG + H] = a["gdn_a_log"][i][None]
        q[:, Q_DT:Q_DT + H] = a["gdn_dt_bias"][i][None]
        q[:, Q_LAM:Q_LAM + 4 * DQK] = a["diff_lambda"][i].reshape(1, -1)
        lam_init = 0.8 - 0.6 * math.exp(-0.3 * i)
        q[:, Q_LINIT] = lam_init
        q[:, Q_LINIT + 1] = 1.0 - lam_init
    x_t = a["x"][0].T.reshape(KD, P, T).transpose(1, 0, 2)
    p_t = a["p"][:DEPTH, 0].transpose(0, 2, 1).reshape(DEPTH, 2, P, T).transpose(0, 2, 1, 3)
    arrays = {"x_t": x_t, "p_t": p_t, "slabs": slabs, "w_ba": w_ba, "subkeys": subkeys,
              "params": params, "constants": constants()}
    arrays = {k: np.ascontiguousarray(v) for k, v in arrays.items()}

    nc = bacc.Bacc("TRN2", target_bir_lowering=False, num_devices=1)
    args = [nc.dram_tensor(k, v.shape, F32, kind="ExternalInput").ap() for k, v in arrays.items()]
    out = nc.dram_tensor("out_t", (P, KD, T), F32, kind="ExternalOutput").ap()
    trunk(nc, *args, out)
    r = run_bass_kernel_spmd(nc, [arrays], core_ids=[0])
    y = r.results[0]["out_t"]
    return np.ascontiguousarray(y.transpose(1, 0, 2).reshape(D, T).T)[None]
```

```python
from contextlib import ExitStack

import concourse.bass as bass
from concourse import mybir

P = 128
D = 1024
KD = D // P
T = 512
NT = T // P
DEPTH = 2
H = 4
DQK = 64
CHUNK = 64
CONV_K = 4
PH = 8
TOPK = 16
NKEYS = 128
PLE = 256
EPS = 1e-6
CAND_ROWS = [TOPK // (a + 1) for a in range(TOPK)]
CAND_AT = [sum(CAND_ROWS[:a]) for a in range(TOPK)]
NC = sum(CAND_ROWS)

S_IN = 0
S_OUT = 28
S_WQ = 36
SEL_SEQ = [("q", 0), ("q", 1)]
for _hd in range(1, 8):
    SEL_SEQ += [("q", 2 * _hd), ("q", 2 * _hd + 1), ("u", 2 * _hd - 2), ("u", 2 * _hd - 1)]
SEL_SEQ += [("u", 14), ("u", 15)]
S_UV = S_WQ + len(SEL_SEQ)
S_V_LAST = 292
S_WG = 308
S_WP = 316
N_SLABS = 318
RING = 4
AHEAD = 3
GROUPS = 16
GB = 8
TG = 32
DVE_HOT1 = 5
REGION = 53200

C_ID, C_ONE, C_TRI, C_CHUNK, C_NEGT, C_POSD, C_M16, C_M32, C_M64 = [P * i for i in range(9)]
C_DIST = 9 * P
C_IOTA = C_DIST + T
C_POS = C_IOTA + P
C_EPS = C_POS + NC
NCONST = C_EPS + 2
Q_MIX, Q_FFN, Q_PLE, Q_FIN = 0, 8, 16, 24
Q_CONV = 32
Q_GDN = Q_CONV + CONV_K * 12
Q_SUB = Q_GDN + 1
Q_ALOG = Q_SUB + 1
Q_DT = Q_ALOG + H
Q_LAM = Q_DT + H
Q_LINIT = Q_LAM + 4 * DQK
NPAR = Q_LINIT + 2

ALU = mybir.AluOpType
ACT = mybir.ActivationFunctionType
F32 = mybir.dt.float32
F32R = mybir.dt.float32r
BF16 = mybir.dt.bfloat16
U32 = mybir.dt.uint32
I32 = mybir.dt.int32
AX_X = mybir.AxisListType.X
NEG = -1e30


def trunk(nc, x_t, p_t, slabs, w_ba, subkeys, params, consts_d, out_t):
    g_dram = nc.dram_tensor("gates_dram", (T // TG, P, NKEYS, TG), F32).ap()

    with ExitStack() as ctx:
        def sem(name):
            return ctx.enter_context(nc.semaphore(name))

        slab_region = ctx.enter_context(nc.sbuf_tensor("region", [P, REGION], F32))
        lo_addr = nc.sbuf_base - REGION * 4
        at = [lo_addr]

        def place(name, shape, dt, where=None):
            size = 4 if dt in (F32, F32R, U32, I32) else 2
            for n in shape[1:]:
                size *= n
            size = (size + 31) // 32 * 32
            if where is None:
                where = at
            t = nc.alloc_sbuf_tensor_at(name, shape, dt, offset=where[0])
            where[0] += size
            assert where[0] <= lo_addr + REGION * 4, (name, where[0] - lo_addr)
            return t

        res = place("res", [P, KD, T], F32)
        consts = place("consts", [P, NCONST], F32)
        par = place("par", [P, NPAR], F32)
        cols = place("cols", [P, 64], F32)
        rs = place("rs", [P, 32], F32)
        at_c2 = place("at_c2", [P, 8], F32)
        raw = [place(f"raw{i}", [P, KD, P], F32) for i in range(RING)]
        whi = [place(f"whi{i}", [P, KD, P], F32R) for i in range(RING)]
        wlo = [place(f"wlo{i}", [P, KD, P], F32R) for i in range(RING)]
        act_base = at[0]
        act_hi = place("act_hi", [P, KD, T], F32R)
        act_lo = place("act_lo", [P, KD, T], F32R)
        arena = at[0]

        m = [arena]
        wide = place("wide", [P, KD, T], F32, m)
        squares = place("squares", [P, KD, T], F32, m)

        m = [act_base]
        kn_nat = place("kn_nat", [P, NT, H, P], F32, m)
        gv_nat = place("gv_nat", [P, NT, H, P], F32, m)
        v_nat = place("v_nat", [P, NT, H, P], F32, m)
        mats = m
        pow_m = place("pow_m", [P, H, P], F32, mats)
        pow_n = place("pow_n", [P, H, P], F32, mats)
        pow_m2 = place("pow_m2", [P, H, P], F32, mats)
        pow_n2 = place("pow_n2", [P, H, P], F32, mats)
        assert m[0] <= arena
        m = [arena]
        mixt = place("mixt", [P, 2 * H, T], F32, m)
        gqt = place("gqt", [P, H, T], F32, m)
        gkt = place("gkt", [P, H, T], F32, m)
        gzt = place("gzt", [P, H, T], F32, m)
        daq = place("daq", [P, H, T], F32, m)
        dak = place("dak", [P, H, T], F32, m)
        dead = m[0]
        gvt = place("gvt", [P, H, T], F32, m)
        davt = place("davt", [P, H, T], F32, m)
        gates_at = m[0]
        gsm = place("gsm", [P, 16, 16], F32, m)
        lam = place("lam", [P, 80], F32, m)
        wba = place("wba", [P, KD, 8], F32, m)
        wba_hi = place("wba_hi", [P, KD, 8], F32R, m)
        wba_lo = place("wba_lo", [P, KD, 8], F32R, m)
        craw = [place(f"craw{i}", [P, T], F32, m) for i in range(2)]
        m2 = [dead]
        low32 = place("low32", [P, H, P], F32, m2)
        low64 = place("low64", [P, H, P], F32, m2)
        inv_a = place("inv_a", [P, H, P], F32, m2)
        inv_b = place("inv_b", [P, H, P], F32, m2)
        inv_t = place("inv_t", [P, H, P], F32, m2)
        zmat = place("zmat", [P, H, P], F32, m2)
        state = [place(f"state{i}", [P, H, P], F32, m2) for i in range(2)]
        assert m2[0] <= gates_at
        m3 = [gates_at + (16 * 16 + 80) * 4]
        at_s = place("at_s", [P, 2, T], F32, m3)
        at_w = place("at_w", [P, T], F32, m3)
        at_wt = place("at_wt", [P, NT, P], F32, m3)
        at_c = place("at_c", [P, 8], F32, m3)
        dec_t = place("dec_t", [P, H, P], F32, m3)
        dec = place("dec", [P, H, P], F32, m3)
        egc_b = place("egc_b", [P, H, P], F32, m3)
        kbg = place("kbg", [P, H, P], F32, m3)
        vbeta = place("vbeta", [P, H, P], F32, m3)
        kdec = place("kdec", [P, H, P], F32, m3)
        qdec = place("qdec", [P, H, P], F32, m3)
        u_sb = place("u_sb", [P, H, P], F32, m3)
        intra = place("intra", [P, H, P], F32, m3)
        vnew = u_sb
        w_tr = pow_n2
        mixer_end = m3[0]
        m3 = [gates_at + (16 * 16 + 80) * 4]
        sq_mix = place("sq_mix", [P, 2 * H, T], F32, m3)

        m = [arena]
        w_hi1 = place("w_hi1", [P, GB, T], F32R, m)
        w_lo1 = place("w_lo1", [P, GB, T], F32R, m)
        w_hi = [place("w_hi0", [P, GB, T], F32R, m), w_hi1]
        w_lo = [place("w_lo0", [P, GB, T], F32R, m), w_lo1]
        act_w = [place(f"act_w{i}", [P, T], F32, m) for i in range(2)]
        g_sb = [place(f"g_sb{i}", [P, T // TG, 4, TG], F32, m) for i in range(2)]
        ring_at = m[0]
        h_ring = place("h_ring", [P, GB, T], F32, m)
        m = [arena]
        hb = place("hb", [P, GB, T], F32, m)
        selt = place("selt", [P, 3, T], F32, m)
        sel_end = m[0]
        qt = place("qt", [P, 4, T], F32, m)
        subk = place("subk", [P, 2 * PH, NKEYS], F32, m)
        rest = place("rest", [P, 2 * NT, NKEYS], F32, m)
        topv = place("topv", [P, NT, 2, TOPK], F32, m)
        topi = place("topi", [P, NT, 2, TOPK], U32, m)
        topf = place("topf", [P, NT, 2, TOPK], F32, m)
        cand = place("cand", [P, NT, NC], F32, m)
        cidx = place("cidx", [P, NT, NC], F32, m)
        crest = place("crest", [P, NT, NC], F32, m)
        winp = place("winp", [P, NT, TOPK], U32, m)
        winf = place("winf", [P, NT, TOPK], F32, m)
        onehot = place("onehot", [P, NT * TOPK, NC], F32, m)
        winv = place("winv", [P, NT, PH, TOPK], F32, m)
        expert = place("expert", [P, NT, PH, TOPK], F32, m)
        exp_i = place("exp_i", [P, T], I32, m)
        exp_j = place("exp_j", [P, T], I32, m)
        sel = place("sel", [P, 2, NT, P], F32, m)
        gsum = place("gsum", [P, NT * PH], F32, m)
        assert m[0] <= ring_at
        m = [sel_end]
        stage = [place(f"stage{i}", [P, NKEYS, TG], F32, m) for i in range(2)]
        hot1 = [place(f"hot1_{i}", [P, 8, NKEYS], F32, m) for i in range(2)]
        hot2 = [place(f"hot2_{i}", [P, 8, NKEYS], F32, m) for i in range(2)]
        n1_cols = [place(f"n1_cols{i}", [P, 8], F32, m) for i in range(2)]
        assert m[0] <= ring_at
        m = [arena + 2 * 4 * KD * T]
        gate_t = place("gate_t", [P, KD, T], F32, m)
        p_sb = place("p_sb", [P, 2, T], F32, m)
        p_hi = place("p_hi", [P, 2, T], F32R, m)
        p_lo = place("p_lo", [P, 2, T], F32R, m)

        bank = [ctx.enter_context(nc.psum_tensor(f"bank{i}", [P, T], F32)) for i in range(8)]

        ident = consts[:, C_ID:C_ID + P]
        ones = consts[:, C_ONE:C_ONE + P]
        tri = consts[:, C_TRI:C_TRI + P]
        same_chunk = consts[:, C_CHUNK:C_CHUNK + P]
        eps_col = consts[:, C_EPS:C_EPS + 1]
        one_col = consts[:, C_ONE:C_ONE + 1]
        iota = consts[:, C_IOTA:C_IOTA + P]

        def over_heads(c):
            return consts[:, c:c + P].unsqueeze(1).to_broadcast([P, H, P])

        def heads(b):
            return bank[b][:].rearrange("p (h c) -> p h c", h=H)

        consts_loaded = sem("consts_loaded")
        x_loaded = sem("x_loaded")
        layer_end = sem("layer_end")
        layer_go = sem("layer_go")
        layer_seen = sem("layer_seen")
        out_ready = sem("out_ready")
        out_stored = sem("out_stored")
        names = """at_oc2 at_rec low_dve inv_cp tk_chain par_loaded small_loaded p_loaded slab_hi slab_lo slab_used
            sq_ready ss_ready std_ready rs_ready rstd_bc norm_used act_hi_ready act_lo_ready normed res_ready
            win_evac conv_raw conv_acc conv_done conv_chain ba_ready wba_hi_ready wba_lo_ready
            gate_act gate_dve gcol_ready lam_dve lam_act
            qk_scaled nat_ready nat_copied
            sc_ready at_dve at_max at_exp at_wgt at_tr at_trc at_out at_oc
            gcb_ready arg_ready dec_ready gram_ready low_ready lowt_ready pow_ready inv_pe inv_dve
            rhs_ready uw_ready uw_copied step_v step_vn step_so step_state og_copied state_zero
            mix_scaled mix_z mix_ready wout_added wq_evac subk_ready
            score_ready score_read tk_dve tk_act selt_ready selt_copied
            n1_ready hot1_ready hot2_ready gm_ready gm_copied stored_a stored_b
            u_gelu w_ready w_hi_ready w_lo_ready v_added
            wg_evac wp_evac p_hi_ready p_lo_ready ple_dve layer_res""".split()
        S = {n: sem(n) for n in names}
        slab_loaded = [sem(f"slab_loaded{i}") for i in range(RING)]
        g_loaded = [sem(f"g_loaded{i}") for i in range(2)]
        per_layer = [S[n] for n in names] + slab_loaded + g_loaded
        s_par, s_slab_hi, s_slab_lo, s_used = S["par_loaded"], S["slab_hi"], S["slab_lo"], S["slab_used"]

        NORM = {"in": (8, 1), "qk": (8, 8), "mix": (8, 8), "ffn": (8, 1), "ple": (8, 1)}
        order = list(NORM)

        def before(use, what):
            return sum(NORM[k][what] for k in order[:order.index(use)])

        def sq_seen(use):
            return before(use, 0)

        def bc_seen(use):
            return before(use, 1)

        def used_seen(use):
            return 2 * H if use == "mix" else 0

        def nth(use):
            return order.index(use)

        def split_hi(act, n, slot=None):
            k = n % RING if slot is None else slot
            act.wait_ge(slab_loaded[k], (n // RING + 1) * 16 if slot is None else (n - slot + RING) * 4)
            if slot is not None or n >= RING:
                act.wait_ge(s_used, n - RING + 1)
            nc.scalar.activation(whi[k][:], raw[k][:], ACT.Copy).then_inc(s_slab_hi, 1)

        def split_lo(dve, n, slot=None):
            k = n % RING if slot is None else slot
            dve.wait_ge(s_slab_hi, n + 1)
            if slot is not None or n >= RING:
                dve.wait_ge(s_used, n - RING + 1)
            nc.vector.tensor_tensor(wlo[k][:], raw[k][:], whi[k][:].bitcast(F32), ALU.subtract).then_inc(s_slab_lo, 1)

        def three_pass(out, a_hi, a_lo, b_hi, b_lo, first, last):
            nc.tensor.matmul(out, a_hi, b_hi, start=first, stop=False)
            nc.tensor.matmul(out, a_hi, b_lo, start=False, stop=False)
            return nc.tensor.matmul(out, a_lo, b_hi, start=False, stop=last)

        def slab_product(pe, n, slot, out, hi, lo, fresh=None):
            pe.wait_ge(s_slab_lo, n + 1)
            for k in range(KD):
                if fresh is not None:
                    pe.wait_ge(S["act_lo_ready"], fresh + k + 1)
                last = three_pass(out, whi[slot][:, k, :], wlo[slot][:, k, :], hi[:, k, :], lo[:, k, :],
                                  k == 0, k == KD - 1)
            last.then_inc(s_used, 1)

        def norm_sums(pe, use, groups, chunks, sq):
            base = sq_seen(use)
            for g in range(groups):
                pe.wait_ge(S["sq_ready"], base + (g + 1) * chunks)
                for t in range(NT):
                    for c in range(chunks):
                        last = nc.tensor.matmul(bank[4][:, t * groups + g:t * groups + g + 1],
                                                sq[:, g * chunks + c, t * P:(t + 1) * P], one_col,
                                                start=c == 0, stop=c == chunks - 1)
            last.then_inc(S["ss_ready"], 1)

        def norm_spread(pe, use, groups):
            pe.wait_ge(S["rs_ready"], nth(use) + 1)
            for g in range(groups):
                if g >= 2:
                    pe.wait_ge(S["norm_used"], used_seen(use) + g - 1)
                for t in range(NT):
                    last = nc.tensor.matmul(bank[5 + g % 2][:, t * P:(t + 1) * P],
                                            rs[:, t * groups + g:t * groups + g + 1].to_broadcast([P, P]), ident,
                                            start=True, stop=True)
                last.then_inc(S["rstd_bc"], 1)

        def norm_std(act, use, groups, scale):
            act.wait_ge(S["ss_ready"], nth(use) + 1)
            nc.scalar.activation(cols[:, 0:NT * groups], bank[4][:, 0:NT * groups], ACT.Sqrt,
                                 bias=eps_col, scale=scale).then_inc(S["std_ready"], 1)

        def norm_rs(dve, use, groups):
            dve.wait_ge(S["std_ready"], nth(use) + 1)
            nc.vector.reciprocal(rs[:, 0:NT * groups], cols[:, 0:NT * groups]).then_inc(S["rs_ready"], 1)

        def act_squares(act, src, n, dst):
            for k in range(n):
                nc.scalar.activation(dst[:, k, :], src[:, k, :], ACT.Square).then_inc(S["sq_ready"], 1)

        def act_low_chunk(dve, src, base, k):
            dve.wait_ge(S["act_hi_ready"], base + k + 1)
            nc.vector.tensor_tensor(act_lo[:, k, :], src[:, k, :], act_hi[:, k, :].bitcast(F32),
                                    ALU.subtract).then_inc(S["act_lo_ready"], 1)

        def scale_to_wide(dve, use, gains, low_base):
            dve.wait_ge(S["rstd_bc"], bc_seen(use) + 1)
            for k in range(KD):
                last = nc.vector.scalar_tensor_tensor(wide[:, k, :], res[:, k, :], par[:, gains + k:gains + k + 1],
                                                      bank[5][:], ALU.mult, ALU.mult)
                last.then_inc(S["normed"], 1)
                if k > 0:
                    act_low_chunk(dve, wide, low_base, k - 1)
            act_low_chunk(dve, wide, low_base, KD - 1)

        def act_high(act, src, seen, base):
            for k in range(KD):
                act.wait_ge(seen, base + k + 1)
                nc.scalar.activation(act_hi[:, k, :], src[:, k, :], ACT.Copy).then_inc(S["act_hi_ready"], 1)

        def act_low(dve, src, base):
            for k in range(KD):
                act_low_chunk(dve, src, base, k)

        def mixer(delta, attend):
            for t in range(NT):
                for s in range(16):
                    delta(t, s)
                    if s % 2 == 1:
                        a = 8 * t + s // 2
                        attend(a // 2, a % 2)
            attend(H * NT, 0)

        block = ctx.enter_context(nc.Block())

        @block.sync
        def _(sp):
            sp.dma_start(consts[:], consts_d).then_inc(consts_loaded, 16)
            sp.dma_start(res[:], x_t).then_inc(x_loaded, 16)
            with sp.Fori(0, DEPTH) as layer:
                sp.dma_start(par[:], params[layer]).then_inc(s_par, 16)
                for n in range(RING):
                    sp.dma_start(raw[n][:], slabs[layer, n]).then_inc(slab_loaded[n], 16)
                sp.dma_start(wba[:], w_ba[layer]).then_inc(S["small_loaded"], 16)
                with sp.Fori(0, N_SLABS // RING - 1) as q:
                    for k in range(RING):
                        sp.wait_ge(s_slab_lo, q * RING + k + 1)
                        sp.dma_start(raw[k][:], slabs[layer, (q + 1) * RING + k]).then_inc(slab_loaded[k], 16)
                for n in range(N_SLABS // RING * RING, N_SLABS):
                    sp.wait_ge(s_slab_lo, n - RING + 1)
                    sp.dma_start(raw[n % RING][:], slabs[layer, n]).then_inc(slab_loaded[n % RING], 16)
                sp.wait_ge(S["layer_res"], KD)
                sp.sem_inc(layer_end, 1)
                sp.wait_ge(layer_go, 1)
                sp.sem_inc(layer_seen, 1)
            sp.wait_ge(out_ready, KD)
            sp.dma_start(out_t, wide[:]).then_inc(out_stored, 16)
            sp.wait_ge(out_stored, 16)

        @block.gpsimd
        def _(pool):
            pool.wait_ge(consts_loaded, 16)
            with pool.Fori(0, DEPTH) as layer:
                pool.wait_ge(S["selt_copied"], NT)
                with pool.Fori(0, T // TG // 2) as q:
                    for b in range(2 * TG // 8):
                        pool.wait_ge(S["gm_ready"], q * (TG // 2) + 2 * b + 2)
                        nc.gpsimd.tensor_copy(n1_cols[b % 2][:], selt[:, 0, bass.ds(q * 2 * TG + 8 * b, 8)]
                                              ).then_inc(S["n1_ready"], 1)
                        pool.wait_ge(S["n1_ready"], q * (TG // 4) + b + 1)
                        nc.gpsimd.tensor_tensor(at_c2[:, 6:7], one_col, one_col, ALU.add)
                        for tok in range(DVE_HOT1, 8):
                            last = nc.gpsimd.tensor_scalar(hot1[b % 2][:, tok, :], iota,
                                                           n1_cols[b % 2][:, tok:tok + 1], None, ALU.is_equal)
                        last.then_inc(S["hot1_ready"], 1)
                pool.wait_ge(layer_end, 4)
                pool.nop()
                first = per_layer[0].num
                pool.sem_clear(range(first, first + len(per_layer)))
                pool.sem_clear(layer_end)
                pool.sem_inc(layer_go, 1)
                pool.wait_ge(layer_seen, 4)
                pool.nop()
                pool.sem_clear(layer_go)
                pool.sem_clear(layer_seen)

        @block.scalar
        def _(act):
            act.wait_ge(consts_loaded, 16)
            act.wait_ge(x_loaded, 16)
            with act.Fori(0, DEPTH) as layer:
                for n in range(AHEAD):
                    split_hi(act, n)
                act_squares(act, res, KD, squares)
                norm_std(act, "in", 1, 1.0 / D)
                act_high(act, wide, S["normed"], 0)
                act.wait_ge(S["small_loaded"], 16)
                nc.scalar.activation(wba_hi[:], wba[:], ACT.Copy).then_inc(S["wba_hi_ready"], 1)
                for n in range(28):
                    split_hi(act, n + AHEAD)
                    act.wait_ge(s_used, n + 1)
                    b = bank[n % RING]
                    if n < 4:
                        i = nc.scalar.activation(daq[:, n, :], b[:], ACT.Copy)
                    elif n < 8:
                        i = nc.scalar.activation(dak[:, n - 4, :], b[:], ACT.Copy)
                    elif n < 12:
                        i = nc.scalar.activation(davt[:, n - 8, :], b[:], ACT.Copy)
                    elif n < 24:
                        c = n - 12
                        if c >= 2:
                            act.wait_ge(S["conv_acc"], c - 1)
                        i = nc.scalar.activation(craw[c % 2][:], b[:], ACT.Copy)
                    else:
                        i = nc.scalar.activation(gzt[:, n - 24, :], b[:], ACT.Silu)
                    i.then_inc(S["win_evac"], 1)
                    if 12 < n <= 24:
                        c = n - 13
                        dst = (gqt, gkt, gvt)[c // H]
                        act.wait_ge(S["conv_acc"], c + 1)
                        nc.scalar.activation(dst[:, c % H, :], dst[:, c % H, :], ACT.Silu).then_inc(S["conv_done"], 1)
                act.wait_ge(S["gate_dve"], 1)
                ba = gsm[:, 12:14, :].rearrange("p r (t c) -> p (r t) c", c=2 * H)

                def small(i):
                    return gsm[:, i, :].rearrange("p (t c) -> p t c", t=NT)
                nc.scalar.activation(small(0), ba[:, :, 0:H], ACT.Sigmoid).then_inc(S["gate_act"], 1)
                nc.scalar.activation(gsm[:, 1, 0:H], par[:, Q_ALOG:Q_ALOG + H], ACT.Exp).then_inc(S["gate_act"], 1)
                act.wait_ge(S["gate_dve"], 4)
                nc.scalar.activation(gsm[:, 4, :], gsm[:, 4, :], ACT.Exp).then_inc(S["gate_act"], 1)
                act.wait_ge(S["gate_act"], 3)
                nc.scalar.activation(gsm[:, 4, :], gsm[:, 4, :], ACT.Ln, bias=one_col).then_inc(S["gate_act"], 1)
                act.wait_ge(S["lam_dve"], 2)
                nc.scalar.activation(lam[:, 66:68], lam[:, 64:66], ACT.Exp).then_inc(S["lam_act"], 1)
                act.wait_ge(S["gate_dve"], 7)
                nc.scalar.activation(gsm[:, 7, :], gsm[:, 14, :], ACT.Exp).then_inc(S["gate_act"], 1)
                act.wait_ge(S["gate_dve"], 8)
                nc.scalar.activation(gsm[:, 9, :], gsm[:, 8, :], ACT.Exp).then_inc(S["gate_act"], 1)
                act.wait_ge(S["conv_done"], 8)
                act.wait_ge(S["at_dve"], 1)
                for j in range(2 * H):
                    src = gqt if j < H else gkt
                    nc.scalar.activation(sq_mix[:, j, :], src[:, j % H, :], ACT.Square).then_inc(S["sq_ready"], 1)
                for i in range(12):
                    if i == 8:
                        norm_std(act, "qk", 2 * H, 1.0)
                    act.wait_ge(S["nat_ready"], i + 1)
                    dst = (v_nat, gv_nat, kn_nat)[i // NT]
                    nc.scalar.activation(dst[:, i % NT].rearrange("p h c -> p (h c)"), bank[(4, 7)[i % 2]][:],
                                         ACT.Copy).then_inc(S["nat_copied"], 1)

                def attend(u, half):
                    t = u % NT
                    kl = (t + 1) * P
                    if half == 0:
                        if u > 0 and t == 0:
                            act.wait_ge(S["at_out"], u)
                            nc.scalar.activation(mixt[:, u // NT - 1, :], bank[4][:], ACT.Copy).then_inc(S["at_oc"], 1)
                        for c in range(2):
                            if u == H * NT:
                                break
                            act.wait_ge(S["at_max"], 2 * u + c + 1)
                            nc.scalar.activation(at_s[:, c, 0:kl], at_s[:, c, 0:kl], ACT.Exp, bias=at_c[:, c:c + 1],
                                                 scale=DQK ** -0.5, accum_out=at_c[:, 2 + c:3 + c]
                                                 ).then_inc(S["at_exp"], 1)
                    else:
                        act.wait_ge(S["at_tr"], u + 1)
                        if u > 0:
                            act.wait_ge(S["at_out"], u)
                        nc.scalar.activation(at_wt[:, 0:t + 1, :], heads(5)[:, 0:t + 1, :],
                                             ACT.Copy).then_inc(S["at_trc"], 1)

                def delta(t, s):
                    if s == 0:
                        act.wait_ge(S["arg_ready"], 8 * t + 8)
                        nc.scalar.activation(egc_b[:], heads(6), ACT.Exp).then_inc(S["dec_ready"], 1)
                        nc.scalar.activation(dec_t[:], dec_t[:], ACT.Exp).then_inc(S["dec_ready"], 1)
                        nc.scalar.activation(dec[:], dec[:], ACT.Exp, scale=-1.0).then_inc(S["dec_ready"], 1)
                    elif s == 11:
                        act.wait_ge(S["uw_ready"], t + 1)
                        nc.scalar.activation(w_tr[:], heads(7), ACT.Copy).then_inc(S["uw_copied"], 1)
                    elif s in (13, 15):
                        j = (s - 13) // 2
                        act.wait_ge(S["step_so"], 2 * t + j + 1)
                        src = bank[3][:, 0:H * CHUNK].rearrange("p (h c) -> p h c", h=H)
                        dst = mixt[:, H:2 * H, t * P + j * CHUNK:t * P + (j + 1) * CHUNK]
                        nc.scalar.activation(dst, src, ACT.Copy).then_inc(S["og_copied"], 1)

                mixer(delta, attend)
                act.wait_ge(S["at_oc"], H)
                act.wait_ge(S["og_copied"], 2 * NT)
                act.wait_ge(S["step_state"], 2 * NT)
                act_squares(act, mixt, 2 * H, sq_mix)
                norm_std(act, "mix", 2 * H, 1.0 / P)
                for k in range(KD):
                    if k < H:
                        act.wait_ge(S["norm_used"], used_seen("mix") + k + 1)
                    else:
                        act.wait_ge(S["mix_ready"], k - H + 1)
                    nc.scalar.activation(act_hi[:, k, :], mixt[:, k, :], ACT.Copy).then_inc(S["act_hi_ready"], 1)
                for n in range(S_OUT, S_WQ):
                    split_hi(act, n + AHEAD)
                for k in range(KD):
                    act.wait_ge(S["wout_added"], k + 1)
                    nc.scalar.activation(squares[:, k, :], res[:, k, :], ACT.Square).then_inc(S["sq_ready"], 1)
                norm_std(act, "ffn", 1, 1.0 / D)
                act.wait_ge(s_used, S_WQ)
                act_high(act, wide, S["normed"], KD)
                act.dma_start(subk[:], subkeys[layer]).then_inc(S["subk_ready"], 16)
                for p, (kind, i) in enumerate(SEL_SEQ):
                    n = S_WQ + p
                    split_hi(act, n + AHEAD)
                    act.wait_ge(s_used, n + 1)
                    if p == 0:
                        act.wait_ge(S["act_lo_ready"], 3 * KD)
                    if kind == "q":
                        if i >= 4:
                            act.wait_ge(S["score_ready"], i // 2 - 1)
                        nc.scalar.activation(qt[:, i % 4, :], bank[i % 2][:], ACT.Copy).then_inc(S["wq_evac"], 1)
                    else:
                        dst = hb if i < GB else h_ring
                        nc.scalar.activation(dst[:, i % GB, :], bank[2 + i % 2][:], ACT.Gelu).then_inc(S["u_gelu"], 1)
                act.wait_ge(S["tk_dve"], 1)
                nc.scalar.activation(winv[:], winv[:], ACT.Exp).then_inc(S["tk_act"], 1)
                with act.Fori(0, T // TG // 2) as q:
                    for i in range(2 * TG // 4):
                        half, at4 = divmod(i, TG // 4)
                        act.wait_ge(S["gm_ready"], q * (TG // 2) + i + 5)
                        if at4 == 0:
                            act.wait_ge((S["stored_a"], S["stored_b"])[half], q * 16 + 1)
                        dst = stage[half][:, :, 4 * at4:4 * at4 + 4].rearrange("p n t -> p t n")
                        nc.scalar.activation(dst, heads(4 + i % 4), ACT.Copy).then_inc(S["gm_copied"], 1)
                        if at4 == TG // 4 - 1:
                            act.wait_ge(S["gm_copied"], q * (TG // 2) + i + 5)
                            act.dma_start(g_dram[q * 2 + half], stage[half][:]).then_inc(
                                (S["stored_a"], S["stored_b"])[half], 16)
                act.wait_ge(S["stored_a"], T // TG // 2 * 16 + 1)
                act.wait_ge(S["stored_b"], T // TG // 2 * 16 + 1)

                def load_gates(g, s):
                    act.dma_start(g_sb[s][:].rearrange("p s b t -> p s (b t)"),
                                  g_dram[:, :, bass.ds(g * GB + 4 * s, 4), :].rearrange("s p n t -> p s (n t)")
                                  ).then_inc(g_loaded[s], 16)

                def w_high(g, j, pg):
                    act.wait_ge(S["w_ready"], g * GB + j + 1)
                    nc.scalar.activation(w_hi[pg][:, j, :], act_w[j % 2][:], ACT.Copy).then_inc(S["w_hi_ready"], 1)
                    if j % 4 == 3 and not (isinstance(g, int) and g == GROUPS - 1):
                        load_gates(g + 1, j // 4)

                load_gates(0, 0)
                load_gates(0, 1)
                for j in range(GB):
                    w_high(0, j, 0)

                def group(g, pg):
                    for j in range(GB):
                        n = g * 16 + (S_UV + 2 * j)
                        split_hi(act, n + AHEAD, (2 * j + AHEAD) % RING)
                        w_high(g + 1, j, 1 - pg)
                        act.wait_ge(s_used, n + 1)
                        nc.scalar.activation(h_ring[:, j, :], bank[2 * (j % 2)][:], ACT.Gelu).then_inc(S["u_gelu"], 1)
                        split_hi(act, n + 1 + AHEAD, (2 * j + 1 + AHEAD) % RING)
                with act.Fori(0, 7) as it:
                    group(it * 2, 0)
                    group(it * 2 + 1, 1)
                for j in range(2 * GB):
                    split_hi(act, S_V_LAST + j + AHEAD)
                    if j < GB:
                        w_high(GROUPS - 1, j, 1)
                act.wait_ge(s_used, S_WG)
                act.dma_start(p_sb[:], p_t[layer]).then_inc(S["p_loaded"], 16)
                for k in range(KD):
                    act.wait_ge(S["v_added"], GROUPS * KD - KD + k + 2)
                    nc.scalar.activation(act_hi[:, k, :], res[:, k, :], ACT.Copy).then_inc(S["act_hi_ready"], 1)
                act.wait_ge(S["p_loaded"], 16)
                nc.scalar.activation(p_hi[:], p_sb[:], ACT.Copy).then_inc(S["p_hi_ready"], 1)
                for i in range(KD):
                    if S_WG + i + AHEAD < N_SLABS:
                        split_hi(act, S_WG + i + AHEAD)
                    act.wait_ge(s_used, S_WG + i + 1)
                    nc.scalar.activation(gate_t[:, i, :], bank[i % RING][:], ACT.Sigmoid).then_inc(S["wg_evac"], 1)
                for i in range(KD):
                    act.wait_ge(s_used, S_WP + i // 4 + 1)
                    if i == 0:
                        act.wait_ge(s_used, S_WG + 1)
                    nc.scalar.activation(wide[:, i, :], bank[(i % 4)][:], ACT.Copy).then_inc(S["wp_evac"], 1)
                for k in range(KD):
                    act.wait_ge(S["wp_evac"], k + 1)
                    nc.scalar.activation(squares[:, k, :], wide[:, k, :], ACT.Square).then_inc(S["sq_ready"], 1)
                norm_std(act, "ple", 1, 1.0 / D)
                act.wait_ge(S["layer_res"], KD)
                act.sem_inc(layer_end, 1)
                act.wait_ge(layer_go, 1)
                act.sem_inc(layer_seen, 1)
            act_squares(act, res, KD, squares)
            norm_std(act, "in", 1, 1.0 / D)

        @block.tensor
        def _(pe):
            pe.wait_ge(consts_loaded, 16)
            with pe.Fori(0, DEPTH) as layer:
                norm_sums(pe, "in", 1, KD, squares)
                norm_spread(pe, "in", 1)
                for n in range(RING):
                    slab_product(pe, n, n, bank[n][:], act_hi, act_lo, 0 if n == 0 else None)
                with pe.Fori(0, 6) as q:
                    for k in range(RING):
                        pe.wait_ge(S["win_evac"], q * RING + k + 1)
                        slab_product(pe, q * RING + k + RING, k, bank[k][:], act_hi, act_lo)
                pe.wait_ge(S["wba_lo_ready"], 1)
                for t in range(NT):
                    for k in range(KD):
                        ts = slice(t * P, (t + 1) * P)
                        last = three_pass(bank[4][:, 8 * t:8 * t + 8], act_hi[:, k, ts], act_lo[:, k, ts],
                                          wba_hi[:, k, :], wba_lo[:, k, :], k == 0, k == KD - 1)
                last.then_inc(S["ba_ready"], 1)
                pe.wait_ge(S["gate_dve"], 6)
                nc.tensor.matmul(bank[4][:, 64:80], tri, gsm[:, 6, :], start=True, stop=True)
                nc.tensor.matmul(bank[4][:, 80:96], same_chunk, gsm[:, 6, :], start=True,
                                 stop=True).then_inc(S["gcol_ready"], 1)
                pe.wait_ge(S["gate_dve"], 7)
                pe.wait_ge(S["conv_done"], 12)
                pe.wait_ge(s_used, S_OUT)
                for i in range(12):
                    if i >= 2:
                        pe.wait_ge(S["nat_copied"], i - 1)
                    if i == 8:
                        pe.wait_ge(S["nat_copied"], 8)
                        norm_sums(pe, "qk", 2 * H, 1, sq_mix)
                        norm_spread(pe, "qk", 2 * H)
                        pe.wait_ge(S["norm_used"], used_seen("qk") + 2 * H)
                    src = (davt, gvt, gkt)[i // NT]
                    t = i % NT
                    for hd in range(H):
                        last = nc.tensor.transpose(heads((4, 7)[i % 2])[:, hd, :], src[:, hd, t * P:(t + 1) * P], ident)
                    last.then_inc(S["nat_ready"], 1)

                def attend(u, half):
                    if half == 0 and u > 0:
                        hd, t = divmod(u - 1, NT)
                        pe.wait_ge(S["at_trc"], u)
                        if t == 0 and hd > 0:
                            pe.wait_ge(S["at_oc"], hd)
                        for k in range(t + 1):
                            last = nc.tensor.matmul(bank[4][:, t * P:(t + 1) * P], v_nat[:, k, hd, :], at_wt[:, k, :],
                                                    start=k == 0, stop=k == t)
                        last.then_inc(S["at_out"], 1)
                    if u == H * NT:
                        return
                    hd, t = divmod(u, NT)
                    kl = (t + 1) * P
                    if half == 0:
                        if u > 0:
                            pe.wait_ge(S["at_dve"], 1 + 2 * u)
                        for c in range(2):
                            cs = slice(c * DQK, (c + 1) * DQK)
                            nc.tensor.matmul(bank[c][:, 0:kl], daq[cs, hd, t * P:(t + 1) * P], dak[cs, hd, 0:kl],
                                             start=True, stop=True).then_inc(S["sc_ready"], 1)
                    else:
                        pe.wait_ge(S["at_wgt"], u + 1)
                        if u > 0:
                            pe.wait_ge(S["at_trc"], u)
                        for k in range(t + 1):
                            last = nc.tensor.transpose(heads(5)[:, k, :], at_w[:, k * P:(k + 1) * P], ident)
                        last.then_inc(S["at_tr"], 1)

                def four(out, lhs, rhs):
                    for hd in range(H):
                        last = nc.tensor.matmul(out[:, hd, :], lhs[:, hd, :], rhs[:, hd, :], start=True, stop=True)
                    return last

                def delta(t, s):
                    ts = slice(t * P, (t + 1) * P)
                    b = 5 * t
                    if s == 0:
                        if t > 0:
                            pe.wait_ge(S["step_state"], 2 * t)
                            pe.wait_ge(S["og_copied"], 2 * t)
                        for hd in range(H):
                            col = gsm[:, 6, t * H + hd:t * H + hd + 1]
                            last = nc.tensor.matmul(heads(6)[:, hd, :], col.to_broadcast([P, P]), tri,
                                                    start=True, stop=True)
                        last.then_inc(S["gcb_ready"], 1)
                        for hd in range(H):
                            nc.tensor.matmul(heads(2)[:, hd, :], gkt[:, hd, ts], gkt[:, hd, ts], start=True, stop=True)
                        for hd in range(H):
                            last = nc.tensor.matmul(heads(3)[:, hd, :], gkt[:, hd, ts], gqt[:, hd, ts],
                                                    start=True, stop=True)
                        last.then_inc(S["gram_ready"], 1)
                    elif s == 2:
                        pe.wait_ge(S["low_ready"], t + 1)
                        for hd in range(H):
                            last = nc.tensor.transpose(heads(7)[:, hd, :], low64[:, hd, :], ident)
                        last.then_inc(S["lowt_ready"], 1)
                    elif s == 3:
                        pe.wait_ge(S["pow_ready"], b + 1)
                        four(heads(2), pow_n, pow_m)
                        four(heads(7), pow_m, pow_n).then_inc(S["inv_pe"], 1)
                    elif s == 4:
                        pe.wait_ge(S["pow_ready"], b + 2)
                        four(heads(6), pow_m2, inv_a)
                        four(heads(2), pow_n2, pow_m2)
                        four(heads(7), pow_m2, pow_n2).then_inc(S["inv_pe"], 1)
                    elif s == 5:
                        pe.wait_ge(S["pow_ready"], b + 3)
                        four(heads(6), pow_m, inv_b)
                        four(heads(2), pow_n, pow_m).then_inc(S["inv_pe"], 1)
                    elif s == 6:
                        pe.wait_ge(S["pow_ready"], b + 4)
                        four(heads(6), pow_m2, inv_a).then_inc(S["inv_pe"], 1)
                    elif s in (7, 9):
                        i = (s - 7) // 2
                        low, cur = ((low32, inv_b), (low64, inv_a))[i]
                        pe.wait_ge(S["inv_dve"], 6 * t + 1 + 3 * i)
                        four(heads(2), low, cur)
                        for hd in range(H):
                            last = nc.tensor.transpose(heads(7)[:, hd, :], cur[:, hd, :], ident)
                        last.then_inc(S["inv_pe"], 1)
                    elif s in (8, 10):
                        pe.wait_ge(S["inv_dve"], 6 * t + 3 + 3 * ((s - 8) // 2))
                        four(heads(6), inv_t, zmat).then_inc(S["inv_pe"], 1)
                    elif s == 11:
                        pe.wait_ge(S["pow_ready"], b + 5)
                        pe.wait_ge(S["rhs_ready"], 16 * (t + 1))
                        four(heads(2), inv_b, vbeta)
                        four(heads(7), kbg, inv_b).then_inc(S["uw_ready"], 1)
                    elif s >= 12:
                        j = (s - 12) // 2
                        c = 2 * t + j
                        rows = slice(j * CHUNK, (j + 1) * CHUNK)
                        s_in = state[c % 2]
                        if s % 2 == 0:
                            pe.wait_ge(S["uw_copied"], 2 * t + 2)
                            if c == 0:
                                pe.wait_ge(S["state_zero"], 1)
                            else:
                                pe.wait_ge(S["step_state"], c)
                            for hd in range(H):
                                last = nc.tensor.matmul(heads(6)[rows, hd, :], w_tr[:, hd, rows], s_in[:, hd, :],
                                                        start=True, stop=True)
                            last.then_inc(S["step_v"], 1)
                        else:
                            pe.wait_ge(S["step_vn"], c + 1)
                            if c > 0:
                                pe.wait_ge(S["og_copied"], c)
                            for hd in range(H):
                                out = bank[3][:, hd * CHUNK:(hd + 1) * CHUNK]
                                nc.tensor.matmul(out, s_in[:, hd, :], qdec[:, hd, rows], start=True, stop=False)
                                last = nc.tensor.matmul(out, vnew[rows, hd, :], intra[rows, hd, rows],
                                                        start=False, stop=True)
                            for hd in range(H):
                                last = nc.tensor.matmul(heads(2)[:, hd, :], kdec[rows, hd, :], vnew[rows, hd, :],
                                                        start=True, stop=True)
                            last.then_inc(S["step_so"], 1)

                pe.wait_ge(S["nat_copied"], 12)
                mixer(delta, attend)
                pe.wait_ge(S["at_oc"], H)
                norm_sums(pe, "mix", 2 * H, 1, sq_mix)
                norm_spread(pe, "mix", 2 * H)
                for i in range(KD):
                    if i >= RING:
                        pe.wait_ge(S["wout_added"], i - RING + 1)
                    slab_product(pe, S_OUT + i, i % RING, bank[i % RING][:], act_hi, act_lo, KD if i == 0 else None)
                norm_sums(pe, "ffn", 1, KD, squares)
                norm_spread(pe, "ffn", 1)
                pe.wait_ge(S["subk_ready"], 16)
                for p, (kind, i) in enumerate(SEL_SEQ):
                    if i >= 2:
                        pe.wait_ge(S["wq_evac" if kind == "q" else "u_gelu"], i - 1)
                    b = bank[i % 2 if kind == "q" else 2 + i % 2]
                    slab_product(pe, S_WQ + p, p % RING, b[:], act_hi, act_lo, 2 * KD if p == 0 else None)
                    if (kind == "u" and i % 2 == 0 and i < 14) or p == 1:
                        for hd in ([0] if p == 1 else [i // 2 + 1]):
                            pe.wait_ge(S["wq_evac"], 2 * hd + 2)
                            if hd >= 2:
                                pe.wait_ge(S["score_read"], hd - 1)
                            for t in range(NT):
                                for c in range(2):
                                    last = nc.tensor.matmul(heads(4 + 2 * (hd % 2) + t // 2)[:, t % 2 * 2 + c, :],
                                                            qt[:, 2 * (hd % 2) + c, t * P:(t + 1) * P],
                                                            subk[:, 2 * hd + c, :], start=True, stop=True)
                            last.then_inc(S["score_ready"], 1)
                pe.wait_ge(S["tk_dve"], 2)
                pe.wait_ge(S["u_gelu"], 2 * GB)
                for t in range(NT):
                    for i in range(3):
                        src = sel[:, i, t, :] if i < 2 else winv[:, t].rearrange("p h k -> p (h k)")
                        last = nc.tensor.transpose(heads(t)[:, i, :], src, ident)
                    last.then_inc(S["selt_ready"], 1)
                pe.sem_inc(S["gm_ready"], 4)
                pe.sem_inc(S["gm_copied"], 4)
                with pe.Fori(0, T // TG // 2) as q:
                    for b in range(2 * TG // 8):
                        pe.wait_ge(S["hot1_ready"], q * (TG // 4) + b + 1)
                        pe.wait_ge(S["hot2_ready"], q * (TG // 4) + b + 1)
                        for half in range(2):
                            i = 2 * b + half
                            pe.wait_ge(S["gm_copied"], q * (TG // 2) + i + 1)
                            for s in range(4):
                                tok = 4 * half + s
                                last = nc.tensor.matmul(heads(4 + i % 4)[:, s, :], hot1[b % 2][:, tok, :],
                                                        hot2[b % 2][:, tok, :], start=True, stop=True)
                            last.then_inc(S["gm_ready"], 1)

                def v_slab(g, pg, j, n, slot):
                    pe.wait_ge(S["w_lo_ready"], g * GB + GB)
                    if j > 0:
                        pe.wait_ge(S["v_added"], g * GB + j)
                    slab_product(pe, n, slot, bank[1 + 2 * (j % 2)][:], w_hi[pg], w_lo[pg])

                def group(g, pg):
                    for j in range(GB):
                        n = g * 16 + (S_UV + 2 * j)
                        pe.wait_ge(S["u_gelu"], g * GB + (2 * GB + j - 1))
                        slab_product(pe, n, 2 * j % RING, bank[2 * (j % 2)][:], act_hi, act_lo)
                        v_slab(g, pg, j, n + 1, (2 * j + 1) % RING)
                with pe.Fori(0, 7) as it:
                    group(it * 2, 0)
                    group(it * 2 + 1, 1)
                for j in range(2 * GB):
                    v_slab(GROUPS - 2 + j // GB, j // GB, j % GB, S_V_LAST + j, j % RING)
                for i in range(KD):
                    if i >= RING:
                        pe.wait_ge(S["wg_evac"], i - RING + 1)
                    slab_product(pe, S_WG + i, i % RING, bank[i % RING][:], act_hi, act_lo, 3 * KD if i == 0 else None)
                pe.wait_ge(S["p_lo_ready"], 1)
                for s in range(2):
                    n = S_WP + s
                    pe.wait_ge(s_slab_lo, n + 1)
                    for i in range(4):
                        pe.wait_ge(S["wg_evac"], KD - 3 + i) if s == 0 else pe.wait_ge(S["wp_evac"], i + 1)
                        if s == 0:
                            pe.wait_ge(S["wg_evac"], 5 + i)
                        for k in range(2):
                            last = three_pass(bank[i][:], whi[n % RING][:, 2 * i + k, :], wlo[n % RING][:, 2 * i + k, :],
                                              p_hi[:, k, :], p_lo[:, k, :], k == 0, k == 1)
                    last.then_inc(s_used, 1)
                norm_sums(pe, "ple", 1, KD, squares)
                norm_spread(pe, "ple", 1)
                pe.wait_ge(S["layer_res"], KD)
                pe.sem_inc(layer_end, 1)
                pe.wait_ge(layer_go, 1)
                pe.sem_inc(layer_seen, 1)
            norm_sums(pe, "in", 1, KD, squares)
            norm_spread(pe, "in", 1)

        @block.vector
        def _(dve):
            V = nc.vector
            dve.wait_ge(consts_loaded, 16)
            dve.wait_ge(x_loaded, 16)
            with dve.Fori(0, DEPTH) as layer:
                for n in range(AHEAD):
                    split_lo(dve, n)
                dve.wait_ge(s_par, 16)
                lamv = par[:, Q_LAM:Q_LAM + 4 * DQK].rearrange("p (i c) -> p i c", i=4)
                V.tensor_tensor_reduce(lam[:, 0:DQK], lamv[:, 0, :], lamv[:, 1, :], 1.0, 0.0, ALU.mult, ALU.add,
                                       lam[:, 64:65]).then_inc(S["lam_dve"], 1)
                dve.wait_ge(S["lam_dve"], 1)
                V.tensor_tensor_reduce(lam[:, 0:DQK], lamv[:, 2, :], lamv[:, 3, :], 1.0, 0.0, ALU.mult, ALU.add,
                                       lam[:, 65:66]).then_inc(S["lam_dve"], 1)
                norm_rs(dve, "in", 1)
                scale_to_wide(dve, "in", Q_MIX, 0)
                dve.wait_ge(S["wba_hi_ready"], 1)
                V.tensor_tensor(wba_lo[:], wba[:], wba_hi[:].bitcast(F32), ALU.subtract).then_inc(S["wba_lo_ready"], 1)
                for n in range(28):
                    split_lo(dve, n + AHEAD)
                    if 12 <= n < 24:
                        c = n - 12
                        dst = (gqt, gkt, gvt)[c // H][:, c % H, :]
                        dve.wait_ge(S["win_evac"], n + 1)
                        taps = [par[:, Q_CONV + tap * 12 + c:Q_CONV + tap * 12 + c + 1] for tap in range(CONV_K)]
                        V.tensor_scalar(dst, craw[c % 2][:], taps[3], None, ALU.mult).then_inc(S["conv_chain"], 1)
                        for lag in range(1, CONV_K):
                            dve.wait_ge(S["conv_chain"], 3 * c + lag)
                            i = V.scalar_tensor_tensor(dst[:, lag:T], craw[c % 2][:, 0:T - lag], taps[3 - lag],
                                                       dst[:, lag:T], ALU.mult, ALU.add)
                            i.then_inc(S["conv_chain"] if lag < 3 else S["conv_acc"], 1)
                dve.wait_ge(S["conv_acc"], 12)
                dve.sem_inc(S["at_dve"], 1)
                dve.wait_ge(S["ba_ready"], 1)
                ba = gsm[:, 12:14, :].rearrange("p r (t c) -> p (r t) c", c=2 * H)

                def small(i):
                    return gsm[:, i, :].rearrange("p (t c) -> p t c", t=NT)
                gd = S["gate_dve"]
                V.tensor_copy(gsm[:, 12:14, :], bank[4][:, 0:32].rearrange("p (r c) -> p r c", r=2)).then_inc(gd, 1)
                dve.wait_ge(gd, 1)
                V.tensor_tensor(small(2), ba[:, :, H:2 * H], par[:, Q_DT:Q_DT + H].unsqueeze(1).to_broadcast([P, NT, H]),
                                ALU.add).then_inc(gd, 1)
                dve.wait_ge(gd, 2)
                V.tensor_scalar(gsm[:, 3, :], gsm[:, 2, :], 0.0, None, ALU.max).then_inc(gd, 1)
                V.scalar_tensor_tensor(gsm[:, 4, :], gsm[:, 2, :], -1.0, gsm[:, 2, :], ALU.mult, ALU.min).then_inc(gd, 1)
                dve.wait_ge(S["gate_act"], 4)
                dve.wait_ge(gd, 4)
                V.tensor_tensor(gsm[:, 5, :], gsm[:, 3, :], gsm[:, 4, :], ALU.add).then_inc(gd, 1)
                dve.wait_ge(gd, 5)
                V.scalar_tensor_tensor(small(6), small(5), -1.0, gsm[:, 1, 0:H].unsqueeze(1).to_broadcast([P, NT, H]),
                                       ALU.mult, ALU.mult).then_inc(gd, 1)
                dve.wait_ge(S["gcol_ready"], 1)
                V.tensor_copy(gsm[:, 14:16, :], bank[4][:, 64:96].rearrange("p (r c) -> p r c", r=2)).then_inc(gd, 1)
                dve.wait_ge(gd, 7)
                V.tensor_tensor(gsm[:, 8, :], gsm[:, 15, :], gsm[:, 14, :], ALU.subtract).then_inc(gd, 1)
                dve.wait_ge(S["gate_act"], 5)
                V.tensor_tensor(gsm[:, 11, :], gsm[:, 0, :], gsm[:, 7, :], ALU.mult).then_inc(gd, 1)
                dve.wait_ge(S["lam_act"], 1)
                V.tensor_tensor(lam[:, 68:69], lam[:, 66:67], lam[:, 67:68], ALU.subtract).then_inc(S["lam_dve"], 1)
                dve.wait_ge(S["lam_dve"], 3)
                V.tensor_tensor(lam[:, 69:70], lam[:, 68:69], par[:, Q_LINIT:Q_LINIT + 1], ALU.add).then_inc(S["lam_dve"], 1)
                V.tensor_tensor(lam[:, 70:71], par[:, Q_SUB:Q_SUB + 1], par[:, Q_LINIT + 1:Q_LINIT + 2],
                                ALU.mult).then_inc(S["lam_dve"], 1)
                norm_rs(dve, "qk", 2 * H)
                for j in range(2 * H):
                    dve.wait_ge(S["rstd_bc"], bc_seen("qk") + j + 1)
                    x = (gqt if j < H else gkt)[:, j % H, :]
                    V.scalar_tensor_tensor(x, x, P ** -0.5 if j < H else 1.0, bank[5 + j % 2][:], ALU.mult,
                                           ALU.mult).then_inc(S["norm_used"], 1)

                ad = S["at_dve"]
                aw = {"max": 0}
                SLOPE = [2.0 ** (-8.0 * (i + 1) / H) for i in range(H)]

                def attend(u, half):
                    if u == H * NT:
                        return
                    hd, t = divmod(u, NT)
                    kl = (t + 1) * P
                    if half == 1:
                        weights(u, kl)
                        return
                    if u > 0:
                        dve.wait_ge(S["at_wgt"], u)
                        dve.wait_ge(S["at_exp"], 2 * u)
                    bias = consts[:, C_DIST + T - kl:C_DIST + T]
                    for c in range(2):
                        dve.wait_ge(S["sc_ready"], 2 * u + c + 1)
                        V.scalar_tensor_tensor(at_s[:, c, 0:kl], bias, SLOPE[hd] * DQK ** 0.5, bank[c][:, 0:kl],
                                               ALU.mult, ALU.add).then_inc(ad, 1)
                    for c in range(2):
                        dve.wait_ge(ad, 1 + 2 * u + c + 1)
                        V.tensor_reduce(at_c[:, 4 + c:5 + c], at_s[:, c, 0:kl], AX_X, ALU.max).then_inc(S["at_oc2"], 1)
                    for c in range(2):
                        dve.wait_ge(S["at_oc2"], 2 * u + c + 1)
                        V.tensor_scalar(at_c[:, c:c + 1], at_c[:, 4 + c:5 + c], -DQK ** -0.5, None,
                                        ALU.mult).then_inc(S["at_max"], 1)

                def weights(u, kl):
                    dve.wait_ge(S["at_exp"], 2 * u + 2)
                    V.reciprocal(at_c[:, 4:6], at_c[:, 2:4]).then_inc(S["at_rec"], 1)
                    dve.wait_ge(S["at_rec"], 3 * u + 1)
                    V.tensor_tensor(at_c[:, 6:7], at_c[:, 5:6], lam[:, 69:70], ALU.mult).then_inc(S["at_rec"], 1)
                    dve.wait_ge(S["at_rec"], 3 * u + 2)
                    V.tensor_scalar(at_s[:, 1, 0:kl], at_s[:, 1, 0:kl], at_c[:, 6:7], None,
                                    ALU.mult).then_inc(S["at_rec"], 1)
                    dve.wait_ge(S["at_rec"], 3 * u + 3)
                    if u > 0:
                        dve.wait_ge(S["at_tr"], u)
                    V.scalar_tensor_tensor(at_w[:, 0:kl], at_s[:, 0, 0:kl], at_c[:, 4:5], at_s[:, 1, 0:kl],
                                           ALU.mult, ALU.subtract).then_inc(S["at_wgt"], 1)

                def delta(t, s):
                    if s == 0:
                        if t == 0:
                            V.memset(state[0][:], 0.0).then_inc(S["state_zero"], 1)
                        dve.wait_ge(S["gcb_ready"], t + 1)
                        for hd in range(H):
                            col = gsm[:, 14, t * H + hd:t * H + hd + 1]
                            V.scalar_tensor_tensor(dec_t[:, hd, :], heads(6)[:, hd, :], col,
                                                   consts[:, C_NEGT:C_NEGT + P],
                                                   ALU.subtract, ALU.add).then_inc(S["arg_ready"], 1)
                            V.scalar_tensor_tensor(dec[:, hd, :], heads(6)[:, hd, :], col,
                                                   consts[:, C_POSD:C_POSD + P],
                                                   ALU.subtract, ALU.add).then_inc(S["arg_ready"], 1)
                        for hd in range(H):
                            i = t * H + hd
                            V.tensor_scalar(vbeta[:, hd, :], gv_nat[:, t, hd, :], gsm[:, 0, i:i + 1], None,
                                            ALU.mult).then_inc(S["rhs_ready"], 1)
                            V.tensor_scalar(kbg[:, hd, :], kn_nat[:, t, hd, :], gsm[:, 11, i:i + 1], None,
                                            ALU.mult).then_inc(S["rhs_ready"], 1)
                            V.tensor_scalar(kdec[:, hd, :], kn_nat[:, t, hd, :], gsm[:, 9, i:i + 1], None,
                                            ALU.mult).then_inc(S["rhs_ready"], 1)
                    elif s == 1:
                        dve.wait_ge(S["dec_ready"], 3 * t + 3)
                        dve.wait_ge(S["gram_ready"], t + 1)
                        for hd in range(H):
                            V.scalar_tensor_tensor(low64[:, hd, :], heads(2)[:, hd, :],
                                                   gsm[:, 0, t * H + hd:t * H + hd + 1],
                                                   dec[:, hd, :], ALU.mult, ALU.mult).then_inc(S["low_dve"], 1)
                        V.tensor_tensor(intra[:], heads(3), dec_t[:], ALU.mult).then_inc(S["low_dve"], 1)
                        dve.wait_ge(S["low_dve"], 8 * t + 5)
                        V.tensor_tensor(pow_m[:], low64[:], over_heads(C_M16), ALU.mult).then_inc(S["low_ready"], 1)
                        V.tensor_tensor(low32[:], low64[:], over_heads(C_M32), ALU.mult).then_inc(S["low_dve"], 1)
                        for hd in range(H):
                            V.tensor_tensor(qdec[:, hd, :], gqt[:, hd, t * P:(t + 1) * P], egc_b[:, hd, :],
                                            ALU.mult).then_inc(S["rhs_ready"], 1)
                    elif s == 2:
                        dve.wait_ge(S["lowt_ready"], t + 1)
                        V.tensor_tensor(pow_n[:], heads(7), over_heads(C_M16), ALU.mult).then_inc(S["low_dve"], 1)
                        V.tensor_tensor(low64[:], low64[:], over_heads(C_M64), ALU.mult).then_inc(S["low_dve"], 1)
                        dve.wait_ge(S["low_dve"], 8 * t + 8)
                        V.tensor_tensor(inv_a[:], over_heads(C_ID), pow_n[:], ALU.subtract).then_inc(S["pow_ready"], 1)
                    elif s == 3:
                        dve.wait_ge(S["inv_pe"], 8 * t + 1)
                        V.tensor_copy(pow_m2[:], heads(2)).then_inc(S["inv_cp"], 1)
                        V.tensor_copy(pow_n2[:], heads(7)).then_inc(S["pow_ready"], 1)
                    elif s == 4:
                        dve.wait_ge(S["inv_pe"], 8 * t + 2)
                        V.tensor_copy(pow_m[:], heads(2)).then_inc(S["inv_cp"], 1)
                        V.tensor_copy(pow_n[:], heads(7)).then_inc(S["inv_cp"], 1)
                        V.tensor_tensor(inv_b[:], inv_a[:], heads(6), ALU.add).then_inc(S["pow_ready"], 1)
                    elif s == 5:
                        dve.wait_ge(S["inv_pe"], 8 * t + 3)
                        V.tensor_copy(pow_m2[:], heads(2)).then_inc(S["inv_cp"], 1)
                        dve.wait_ge(S["pow_ready"], 5 * t + 3)
                        V.tensor_tensor(inv_a[:], inv_b[:], heads(6), ALU.add).then_inc(S["pow_ready"], 1)
                    elif s == 6:
                        dve.wait_ge(S["inv_pe"], 8 * t + 4)
                        dve.wait_ge(S["pow_ready"], 5 * t + 4)
                        V.tensor_tensor(inv_b[:], inv_a[:], heads(6), ALU.add).then_inc(S["inv_dve"], 1)
                    elif s in (7, 9):
                        dve.wait_ge(S["inv_pe"], 8 * t + s - 2)
                        V.tensor_copy(zmat[:], heads(2)).then_inc(S["inv_dve"], 1)
                        V.tensor_copy(inv_t[:], heads(7)).then_inc(S["inv_dve"], 1)
                    elif s in (8, 10):
                        i = (s - 8) // 2
                        cur, new = ((inv_b, inv_a), (inv_a, inv_b))[i]
                        dve.wait_ge(S["inv_pe"], 8 * t + s - 2)
                        dve.wait_ge(S["inv_dve"], 6 * t + 1 + 3 * i)
                        V.tensor_tensor(new[:], cur[:], heads(6), ALU.subtract).then_inc(
                            S["inv_dve"] if i == 0 else S["pow_ready"], 1)
                    elif s == 11:
                        dve.wait_ge(S["uw_ready"], t + 1)
                        V.tensor_copy(u_sb[:], heads(2)).then_inc(S["uw_copied"], 1)
                    else:
                        j = (s - 12) // 2
                        c = 2 * t + j
                        rows = slice(j * CHUNK, (j + 1) * CHUNK)
                        if s % 2 == 0:
                            dve.wait_ge(S["step_v"], c + 1)
                            dve.wait_ge(S["uw_copied"], 2 * t + 2)
                            V.tensor_tensor(vnew[rows], u_sb[rows], heads(6)[rows], ALU.subtract).then_inc(S["step_vn"], 1)
                        else:
                            dve.wait_ge(S["step_so"], c + 1)
                            end = j * CHUNK + CHUNK - 1
                            for hd in range(H):
                                i = V.scalar_tensor_tensor(state[(c + 1) % 2][:, hd, :], state[c % 2][:, hd, :],
                                                           egc_b[:, hd, end:end + 1], heads(2)[:, hd, :],
                                                           ALU.mult, ALU.add)
                            i.then_inc(S["step_state"], 1)

                dve.wait_ge(S["nat_copied"], 12)
                dve.wait_ge(S["lam_dve"], 5)
                mixer(delta, attend)
                norm_rs(dve, "mix", 2 * H)
                for j in range(2 * H):
                    dve.wait_ge(S["rstd_bc"], bc_seen("mix") + j + 1)
                    gain = lam[:, 70:71] if j < H else par[:, Q_GDN:Q_GDN + 1]
                    i = V.scalar_tensor_tensor(mixt[:, j, :], mixt[:, j, :], gain, bank[5 + j % 2][:], ALU.mult, ALU.mult)
                    i.then_inc(S["norm_used"], 1)
                for j in range(2 * H):
                    dve.wait_ge(S["norm_used"], used_seen("mix") + j + 1)
                    if j >= H:
                        V.tensor_tensor(mixt[:, j, :], mixt[:, j, :], gzt[:, j - H, :], ALU.mult).then_inc(S["mix_ready"], 1)
                act_low(dve, mixt, KD)
                for i in range(KD):
                    split_lo(dve, S_OUT + i + AHEAD)
                    dve.wait_ge(s_used, S_OUT + i + 1)
                    V.tensor_tensor(res[:, i, :], res[:, i, :], bank[i % RING][:], ALU.add).then_inc(S["wout_added"], 1)
                norm_rs(dve, "ffn", 1)
                dve.wait_ge(S["wout_added"], KD)
                scale_to_wide(dve, "ffn", Q_FFN, 2 * KD)
                tks = S["tk_chain"]
                tk = {"n": 0}

                def step(ins):
                    tk["n"] += 1
                    ins.then_inc(tks, 1)

                def settle():
                    dve.wait_ge(tks, tk["n"])

                def select(hd, part):
                    def score(i):
                        return heads(4 + 2 * (hd % 2) + i // 4)[:, i % 4, :]
                    units = range(2 * NT)
                    tv = topv[:].rearrange("p t c k -> p (t c) k")
                    ti = topi[:].rearrange("p t c k -> p (t c) k")
                    wv = winv[:, :, hd, :]
                    if part == 0:
                        dve.wait_ge(S["score_ready"], hd + 1)
                        settle()
                        for i in units:
                            step(V.max(tv[:, i, 0:8], score(i)))
                        settle()
                        for i in units:
                            step(V.match_replace(rest[:, i, :], tv[:, i, 0:8], score(i), NEG))
                            step(V.max_index(ti[:, i, 0:8], tv[:, i, 0:8], score(i)))
                        settle()
                        dve.sem_inc(S["score_read"], 1)
                    elif part == 1:
                        for i in units:
                            step(V.max(tv[:, i, 8:16], rest[:, i, :]))
                        settle()
                        for i in units:
                            step(V.max_index(ti[:, i, 8:16], tv[:, i, 8:16], rest[:, i, :]))
                        settle()
                        step(V.tensor_copy(topf[:], topi[:]))
                        settle()
                        step(V.tensor_scalar(topf[:, :, 0, :], topf[:, :, 0, :], float(NKEYS), None, ALU.mult))
                        settle()
                        for dst, src in ((cand, topv), (cidx, topf)):
                            for a in range(8):
                                o, n = CAND_AT[a], CAND_ROWS[a]
                                step(V.tensor_tensor(dst[:, :, o:o + n], src[:, :, 1, 0:n],
                                                     src[:, :, 0, a:a + 1].to_broadcast([P, NT, n]), ALU.add))
                            o, n = CAND_AT[8], TOPK - 8
                            step(V.tensor_tensor(dst[:, :, o:o + n], src[:, :, 0, 8:TOPK],
                                                 src[:, :, 1, 0:1].to_broadcast([P, NT, n]), ALU.add))
                    elif part == 2:
                        settle()
                        for t in range(NT):
                            step(V.max(wv[:, t, 0:8], cand[:, t, :]))
                        settle()
                        for t in range(NT):
                            step(V.match_replace(crest[:, t, :], wv[:, t, 0:8], cand[:, t, :], NEG))
                            step(V.max_index(winp[:, t, 0:8], wv[:, t, 0:8], cand[:, t, :]))
                        settle()
                        for t in range(NT):
                            step(V.max(wv[:, t, 8:16], crest[:, t, :]))
                        settle()
                        for t in range(NT):
                            step(V.max_index(winp[:, t, 8:16], wv[:, t, 8:16], crest[:, t, :]))
                        settle()
                        step(V.tensor_copy(winf[:], winp[:]))
                        settle()
                    else:
                        oh = onehot[:].rearrange("p (t k) c -> p t k c", t=NT)
                        for t in range(NT):
                            step(V.tensor_tensor(oh[:, t], winf[:, t, :].unsqueeze(2).to_broadcast([P, TOPK, NC]),
                                                 consts[:, C_POS:C_POS + NC].unsqueeze(1).to_broadcast([P, TOPK, NC]),
                                                 ALU.is_equal))
                        settle()
                        for t in range(NT):
                            step(V.tensor_tensor(oh[:, t], oh[:, t], cidx[:, t, :].unsqueeze(1).to_broadcast([P, TOPK, NC]),
                                                 ALU.mult))
                        settle()
                        step(V.tensor_reduce(expert[:, :, hd, :], oh, AX_X, ALU.add))
                        settle()

                for p in range(2):
                    split_lo(dve, S_WQ + p + AHEAD)
                for hd in range(PH):
                    for part in range(4):
                        p = 2 + 4 * hd + part
                        if p < len(SEL_SEQ):
                            split_lo(dve, S_WQ + p + AHEAD)
                        select(hd, part)
                wv = winv[:].rearrange("p t h k -> p (t h) k")
                step(V.tensor_copy(gsum[:], wv[:, :, 0]))
                step(V.tensor_copy(exp_i[:], expert[:].rearrange("p t h k -> p (t h k)")))
                settle()
                step(V.tensor_tensor(wv, wv, gsum[:].unsqueeze(2).to_broadcast([P, NT * PH, TOPK]), ALU.subtract))
                step(V.tensor_scalar(exp_j[:], exp_i[:], 7, None, ALU.logical_shift_right))
                settle()
                dve.sem_inc(S["tk_dve"], 1)
                step(V.tensor_scalar(exp_i[:], exp_i[:], NKEYS - 1, None, ALU.bitwise_and))
                step(V.tensor_copy(sel[:, 0].rearrange("p t c -> p (t c)"), exp_j[:]))
                settle()
                step(V.tensor_copy(sel[:, 1].rearrange("p t c -> p (t c)"), exp_i[:]))
                dve.wait_ge(S["tk_act"], 1)
                step(V.tensor_reduce(gsum[:], wv, AX_X, ALU.add))
                settle()
                step(V.reciprocal(gsum[:], gsum[:]))
                settle()
                step(V.tensor_tensor(wv, wv, gsum[:].unsqueeze(2).to_broadcast([P, NT * PH, TOPK]), ALU.mult))
                settle()
                dve.sem_inc(S["tk_dve"], 1)
                for t in range(NT):
                    dve.wait_ge(S["selt_ready"], t + 1)
                    V.tensor_copy(selt[:, :, t * P:(t + 1) * P], heads(t)[:, 0:3, :]).then_inc(S["selt_copied"], 1)
                dve.wait_ge(S["selt_copied"], NT)
                dve.sem_inc(S["stored_a"], 1)
                dve.sem_inc(S["stored_b"], 1)
                with dve.Fori(0, T // TG // 2) as q:
                    for b in range(2 * TG // 8):
                        dve.wait_ge(S["gm_ready"], q * (TG // 2) + 2 * b + 2)
                        V.tensor_tensor(hot1[b % 2][:, 0:DVE_HOT1, :], iota.unsqueeze(1).to_broadcast([P, DVE_HOT1, NKEYS]),
                                        selt[:, 0, bass.ds(q * 2 * TG + 8 * b, DVE_HOT1)].unsqueeze(2).to_broadcast(
                                            [P, DVE_HOT1, NKEYS]), ALU.is_equal)
                        for tok in range(8):
                            at_tok = q * 2 * TG + (8 * b + tok)
                            last = V.tensor_scalar(hot2[b % 2][:, tok, :], iota, selt[:, 1, bass.ds(at_tok, 1)],
                                                   selt[:, 2, bass.ds(at_tok, 1)], ALU.is_equal, ALU.mult)
                        last.then_inc(S["hot2_ready"], 1)

                dve.sem_inc(S["v_added"], 1)

                def weigh(g, j, h):
                    if j >= 4:
                        dve.wait_ge(g_loaded[1], g * 16 + 16)
                    else:
                        dve.wait_ge(g_loaded[0], g * 16 + 16)
                    if not (isinstance(g, int) and g * GB + j < 2):
                        dve.wait_ge(S["w_lo_ready"], g * GB + j - 1)

                    def tokens(x):
                        return x.rearrange("p (s t) -> p s t", t=TG)
                    V.tensor_tensor(tokens(act_w[j % 2][:]), tokens(h[:, j, :]), g_sb[j // 4][:, :, j % 4, :],
                                    ALU.mult).then_inc(S["w_ready"], 1)

                def w_low(g, j, pg):
                    dve.wait_ge(S["w_hi_ready"], g * GB + j + 1)
                    V.tensor_tensor(w_lo[pg][:, j, :], act_w[j % 2][:], w_hi[pg][:, j, :].bitcast(F32),
                                    ALU.subtract).then_inc(S["w_lo_ready"], 1)

                def add_block(j, used):
                    dve.wait_ge(s_used, used)
                    V.tensor_tensor(res[:, j, :], res[:, j, :], bank[1 + 2 * (j % 2)][:], ALU.add).then_inc(S["v_added"], 1)

                dve.wait_ge(S["u_gelu"], 2 * GB)
                for j in range(GB):
                    weigh(0, j, hb)
                    if j > 0:
                        w_low(0, j - 1, 0)
                w_low(0, GB - 1, 0)

                def group(g, pg):
                    for j in range(GB):
                        n = g * 16 + (S_UV + 2 * j)
                        split_lo(dve, n + AHEAD, (2 * j + AHEAD) % RING)
                        dve.wait_ge(S["u_gelu"], g * GB + (GB + j + 1))
                        weigh(g + 1, j, h_ring)
                        split_lo(dve, n + 1 + AHEAD, (2 * j + 1 + AHEAD) % RING)
                        w_low(g + 1, j, 1 - pg)
                        add_block(j, n + 2)
                with dve.Fori(0, 7) as it:
                    group(it * 2, 0)
                    group(it * 2 + 1, 1)
                for j in range(2 * GB):
                    split_lo(dve, S_V_LAST + j + AHEAD)
                    if j < GB:
                        dve.wait_ge(S["u_gelu"], (GROUPS - 1) * GB + j + 1)
                        weigh(GROUPS - 1, j, h_ring)
                        w_low(GROUPS - 1, j, 1)
                    add_block(j % GB, S_V_LAST + j + 1)
                act_low(dve, res, 3 * KD)
                dve.wait_ge(S["p_hi_ready"], 1)
                V.tensor_tensor(p_lo[:], p_sb[:], p_hi[:].bitcast(F32), ALU.subtract).then_inc(S["p_lo_ready"], 1)
                for n in range(S_WG + AHEAD, N_SLABS):
                    split_lo(dve, n)
                norm_rs(dve, "ple", 1)
                dve.wait_ge(S["rstd_bc"], bc_seen("ple") + 1)
                dve.wait_ge(S["wp_evac"], KD)
                dve.wait_ge(S["wg_evac"], KD)
                dve.wait_ge(S["ss_ready"], nth("ple") + 1)
                pd = S["ple_dve"]
                for k in range(KD):
                    V.scalar_tensor_tensor(wide[:, k, :], wide[:, k, :], par[:, Q_PLE + k:Q_PLE + k + 1], bank[5][:],
                                           ALU.mult, ALU.mult).then_inc(pd, 1)
                for k in range(KD):
                    dve.wait_ge(pd, k + 1)
                    V.tensor_tensor(wide[:, k, :], wide[:, k, :], gate_t[:, k, :], ALU.mult).then_inc(pd, 1)
                for k in range(KD):
                    dve.wait_ge(pd, KD + k + 1)
                    V.tensor_tensor(res[:, k, :], res[:, k, :], wide[:, k, :], ALU.add).then_inc(S["layer_res"], 1)
                dve.wait_ge(S["layer_res"], KD)
                dve.sem_inc(layer_end, 1)
                dve.wait_ge(layer_go, 1)
                dve.sem_inc(layer_seen, 1)
            norm_rs(dve, "in", 1)
            dve.wait_ge(S["rstd_bc"], 1)
            for k in range(KD):
                nc.vector.scalar_tensor_tensor(wide[:, k, :], res[:, k, :], par[:, Q_FIN + k:Q_FIN + k + 1], bank[5][:],
                                               ALU.mult, ALU.mult).then_inc(out_ready, 1)


def constants():
    import numpy as np
    c = np.zeros((P, NCONST), np.float32)
    i = np.arange(P)
    row, col = i[:, None], i[None, :]
    same = row // CHUNK == col // CHUNK
    c[:, C_ID:C_ID + P] = row == col
    c[:, C_ONE:C_ONE + P] = 1
    c[:, C_TRI:C_TRI + P] = (row <= col) & same
    c[:, C_CHUNK:C_CHUNK + P] = same
    c[:, C_NEGT:C_NEGT + P] = np.where((row <= col) & same, 0, NEG)
    c[:, C_POSD:C_POSD + P] = np.where((col < row) & same, 0, -NEG)
    c[:, C_M16:C_M16 + P] = row // 16 == col // 16
    c[:, C_M32:C_M32 + P] = (row // 32 == col // 32) & (row // 16 != col // 16)
    c[:, C_M64:C_M64 + P] = same & (row // 32 != col // 32)
    j = np.arange(T)[None, :] - (T - P)
    c[:, C_DIST:C_DIST + T] = np.where(j <= row, j - row, NEG)
    c[:, C_IOTA:C_IOTA + P] = col
    c[:, C_POS:C_POS + NC] = np.arange(NC)
    c[:, C_EPS] = EPS
    return c


def kernel(**inputs):
    import math
    import numpy as np
    import concourse.bacc as bacc
    from concourse.bass_utils import run_bass_kernel_spmd

    a = {k: np.asarray(v) for k, v in inputs.items()}

    def by_columns(w):
        n = w.shape[1] // P
        return w.reshape(-1, P, n, P).transpose(2, 1, 0, 3)

    def chunked(v):
        return v.reshape(-1, P).T

    slabs = np.empty((DEPTH, N_SLABS, P, KD, P), np.float32)
    w_ba = np.empty((DEPTH, P, KD, 8), np.float32)
    subkeys = np.empty((DEPTH, P, 2 * PH, NKEYS), np.float32)
    params = np.zeros((DEPTH, P, NPAR), np.float32)
    for i in range(DEPTH):
        w_in = a["w_in"][i]
        slabs[i, S_IN:S_OUT] = by_columns(w_in[:, :28 * P])
        w_ba[i] = w_in[:, 28 * P:].reshape(KD, P, 8).transpose(1, 0, 2)
        slabs[i, S_OUT:S_WQ] = by_columns(a["w_out"][i])
        wq = by_columns(a["peer_wq"][i])
        u = a["peer_u"][i].reshape(NKEYS, NKEYS, KD, P).transpose(1, 3, 2, 0)
        v = a["peer_v"][i].reshape(NKEYS, GROUPS, GB, KD, P).transpose(1, 3, 0, 2, 4).reshape(-1, P, GB, P)
        for n, (kind, j) in enumerate(SEL_SEQ):
            slabs[i, S_WQ + n] = wq[j] if kind == "q" else u[j]
        slabs[i, S_UV:S_V_LAST:2] = u[2 * GB:]
        slabs[i, S_UV + 1:S_V_LAST:2] = v[:(GROUPS - 2) * KD]
        slabs[i, S_V_LAST:S_WG] = v[(GROUPS - 2) * KD:]
        slabs[i, S_WG:S_WP] = by_columns(a["ple_wg"][i])
        wp = by_columns(a["ple_wp"][i])
        slabs[i, S_WP:] = wp.reshape(2, 4, P, 2, P).transpose(0, 2, 1, 3, 4).reshape(2, P, KD, P)
        subkeys[i] = a["peer_subkeys"][i].reshape(2 * PH, NKEYS, P).transpose(2, 0, 1)
        q = params[i]
        q[:, Q_MIX:Q_MIX + 8] = chunked(a["ln_mix_g"][i])
        q[:, Q_FFN:Q_FFN + 8] = chunked(a["ln_ffn_g"][i])
        q[:, Q_PLE:Q_PLE + 8] = chunked(a["ple_norm_g"][i])
        q[:, Q_FIN:Q_FIN + 8] = chunked(a["final_norm_g"])
        for tap in range(CONV_K):
            q[:, Q_CONV + 12 * tap:Q_CONV + 12 * tap + 12] = chunked(a["conv_w"][i, tap])
        q[:, Q_GDN] = a["gdn_norm_g"][i]
        q[:, Q_SUB] = a["diff_subln_g"][i]
        q[:, Q_ALOG:Q_ALOG + H] = a["gdn_a_log"][i][None]
        q[:, Q_DT:Q_DT + H] = a["gdn_dt_bias"][i][None]
        q[:, Q_LAM:Q_LAM + 4 * DQK] = a["diff_lambda"][i].reshape(1, -1)
        lam_init = 0.8 - 0.6 * math.exp(-0.3 * i)
        q[:, Q_LINIT] = lam_init
        q[:, Q_LINIT + 1] = 1.0 - lam_init
    x_t = a["x"][0].T.reshape(KD, P, T).transpose(1, 0, 2)
    p_t = a["p"][:DEPTH, 0].transpose(0, 2, 1).reshape(DEPTH, 2, P, T).transpose(0, 2, 1, 3)
    arrays = {"x_t": x_t, "p_t": p_t, "slabs": slabs, "w_ba": w_ba, "subkeys": subkeys,
              "params": params, "constants": constants()}
    arrays = {k: np.ascontiguousarray(v) for k, v in arrays.items()}

    nc = bacc.Bacc("TRN2", target_bir_lowering=False, num_devices=1)
    args = [nc.dram_tensor(k, v.shape, F32, kind="ExternalInput").ap() for k, v in arrays.items()]
    out = nc.dram_tensor("out_t", (P, KD, T), F32, kind="ExternalOutput").ap()
    trunk(nc, *args, out)
    r = run_bass_kernel_spmd(nc, [arrays], core_ids=[0])
    y = r.results[0]["out_t"]
    return np.ascontiguousarray(y.transpose(1, 0, 2).reshape(D, T).T)[None]
```

```python
from contextlib import ExitStack

import concourse.bass as bass
from concourse import mybir

P = 128
D = 1024
KD = D // P
T = 512
NT = T // P
DEPTH = 2
H = 4
DQK = 64
CHUNK = 64
CONV_K = 4
PH = 8
TOPK = 16
NKEYS = 128
EPS = 1e-6
CAND_ROWS = [TOPK // (a + 1) for a in range(TOPK)]
CAND_AT = [sum(CAND_ROWS[:a]) for a in range(TOPK)]
NC = sum(CAND_ROWS)

S_IN = 0
S_OUT = 28
S_WQ = 36
SEL_SEQ = [("q", 0), ("q", 1)]
for _hd in range(1, 8):
    SEL_SEQ += [("q", 2 * _hd), ("q", 2 * _hd + 1), ("u", 2 * _hd - 2), ("u", 2 * _hd - 1)]
SEL_SEQ += [("u", 14), ("u", 15)]
S_UV = S_WQ + len(SEL_SEQ)
S_V_LAST = 292
TAIL = [("v", j) for j in range(12)] + [("p", 0), ("p", 1)] + [("v", j) for j in range(12, 16)]
S_WG = S_V_LAST + len(TAIL)
IN_ORDER = list(range(12, 28)) + list(range(12))
N_SLABS = 318
RING = 4
AHEAD = 3
GROUPS = 16
GB = 8
TG = 32
DVE_HOT1 = 5
ACT_HOT2 = 1
REGION = 53200

assert N_SLABS == S_WG + 8

C_ID, C_ONE, C_TRI, C_CHUNK, C_NEGT, C_POSD, C_M16, C_M32, C_M64 = [P * i for i in range(9)]
C_DIST = 9 * P
C_IOTA = C_DIST + T
C_POS = C_IOTA + P
C_EPS = C_POS + NC
NCONST = C_EPS + 2
Q_MIX, Q_FFN, Q_PLE, Q_FIN = 0, 8, 16, 24
Q_CONV = 32
Q_GDN = Q_CONV + CONV_K * 12
Q_SUB = Q_GDN + 1
Q_ALOG = Q_SUB + 1
Q_DT = Q_ALOG + H
Q_LAM = Q_DT + H
Q_LINIT = Q_LAM + 4 * DQK
NPAR = Q_LINIT + 2

ALU = mybir.AluOpType
ACT = mybir.ActivationFunctionType
F32 = mybir.dt.float32
F32R = mybir.dt.float32r
U32 = mybir.dt.uint32
I32 = mybir.dt.int32
AX_X = mybir.AxisListType.X
NEG = -1e30


def trunk(nc, x_t, p_t, slabs, w_ba, subkeys, params, consts_d, out_t):
    g_dram = nc.dram_tensor("gates_dram", (T // TG, P, NKEYS, TG), F32).ap()

    with ExitStack() as ctx:
        def sem(name):
            return ctx.enter_context(nc.semaphore(name))

        ctx.enter_context(nc.sbuf_tensor("region", [P, REGION], F32))
        lo_addr = nc.sbuf_base - REGION * 4
        at = [lo_addr]

        def place(name, shape, dt, where=None):
            size = 4 if dt in (F32, F32R, U32, I32) else 2
            for n in shape[1:]:
                size *= n
            size = (size + 31) // 32 * 32
            if where is None:
                where = at
            t = nc.alloc_sbuf_tensor_at(name, shape, dt, offset=where[0])
            where[0] += size
            assert where[0] <= lo_addr + REGION * 4, (name, where[0] - lo_addr)
            return t

        res = place("res", [P, KD, T], F32)
        consts = place("consts", [P, NCONST], F32)
        par = place("par", [P, NPAR], F32)
        cols = place("cols", [P, 64], F32)
        rs = place("rs", [P, 32], F32)
        at_c2 = place("at_c2", [P, 8], F32)
        raw = [place(f"raw{i}", [P, KD, P], F32) for i in range(RING)]
        whi = [place(f"whi{i}", [P, KD, P], F32R) for i in range(RING)]
        wlo = [place(f"wlo{i}", [P, KD, P], F32R) for i in range(RING)]
        act_base = at[0]
        act_hi = place("act_hi", [P, KD, T], F32R)
        act_lo = place("act_lo", [P, KD, T], F32R)
        arena = at[0]

        m = [arena]
        wide = place("wide", [P, KD, T], F32, m)
        squares = place("squares", [P, KD, T], F32, m)

        m = [act_base]
        kn_nat = place("kn_nat", [P, NT, H, P], F32, m)
        gv_nat = place("gv_nat", [P, NT, H, P], F32, m)
        v_nat = place("v_nat", [P, NT, H, P], F32, m)
        mats = m
        pow_m = place("pow_m", [P, H, P], F32, mats)
        pow_n = place("pow_n", [P, H, P], F32, mats)
        pow_m2 = place("pow_m2", [P, H, P], F32, mats)
        pow_n2 = place("pow_n2", [P, H, P], F32, mats)
        assert m[0] <= arena
        m = [arena]
        mixt = place("mixt", [P, 2 * H, T], F32, m)
        gqt = place("gqt", [P, H, T], F32, m)
        gkt = place("gkt", [P, H, T], F32, m)
        gzt = place("gzt", [P, H, T], F32, m)
        daq = place("daq", [P, H, T], F32, m)
        dak = place("dak", [P, H, T], F32, m)
        dead = m[0]
        gvt = place("gvt", [P, H, T], F32, m)
        davt = place("davt", [P, H, T], F32, m)
        gates_at = m[0]
        gsm = place("gsm", [P, 16, 16], F32, m)
        lam = place("lam", [P, 80], F32, m)
        wba = place("wba", [P, KD, 8], F32, m)
        wba_hi = place("wba_hi", [P, KD, 8], F32R, m)
        wba_lo = place("wba_lo", [P, KD, 8], F32R, m)
        craw = [place(f"craw{i}", [P, T], F32, m) for i in range(2)]
        m2 = [dead]
        low32 = place("low32", [P, H, P], F32, m2)
        low64 = place("low64", [P, H, P], F32, m2)
        inv_a = place("inv_a", [P, H, P], F32, m2)
        inv_b = place("inv_b", [P, H, P], F32, m2)
        inv_t = place("inv_t", [P, H, P], F32, m2)
        zmat = place("zmat", [P, H, P], F32, m2)
        state = [place(f"state{i}", [P, H, P], F32, m2) for i in range(2)]
        assert m2[0] <= gates_at
        m3 = [gates_at + (16 * 16 + 80) * 4]
        at_s = place("at_s", [P, 2, T], F32, m3)
        at_w = place("at_w", [P, T], F32, m3)
        at_wt = place("at_wt", [P, NT, P], F32, m3)
        at_c = place("at_c", [P, 8], F32, m3)
        dec_t = place("dec_t", [P, H, P], F32, m3)
        dec = place("dec", [P, H, P], F32, m3)
        egc_b = place("egc_b", [P, H, P], F32, m3)
        kbg = place("kbg", [P, H, P], F32, m3)
        vbeta = place("vbeta", [P, H, P], F32, m3)
        kdec = place("kdec", [P, H, P], F32, m3)
        qdec = place("qdec", [P, H, P], F32, m3)
        u_sb = place("u_sb", [P, H, P], F32, m3)
        intra = place("intra", [P, H, P], F32, m3)
        vnew = u_sb
        w_tr = pow_n2
        m3 = [gates_at + (16 * 16 + 80) * 4]
        sq_mix = place("sq_mix", [P, 2 * H, T], F32, m3)

        m = [arena]
        w_hi1 = place("w_hi1", [P, GB, T], F32R, m)
        w_lo1 = place("w_lo1", [P, GB, T], F32R, m)
        w_hi = [place("w_hi0", [P, GB, T], F32R, m), w_hi1]
        w_lo = [place("w_lo0", [P, GB, T], F32R, m), w_lo1]
        act_w = [place(f"act_w{i}", [P, T], F32, m) for i in range(2)]
        g_sb = [place(f"g_sb{i}", [P, T // TG, 4, TG], F32, m) for i in range(2)]
        ring_at = m[0]
        h_ring = place("h_ring", [P, GB, T], F32, m)
        m = [arena]
        hb = place("hb", [P, GB, T], F32, m)
        selt = place("selt", [P, 4, T], F32, m)
        sel_end = m[0]
        qt = place("qt", [P, 4, T], F32, m)
        subk = place("subk", [P, 2 * PH, NKEYS], F32, m)
        rest = place("rest", [P, 2 * NT, NKEYS], F32, m)
        topv = place("topv", [P, NT, 2, TOPK], F32, m)
        topi = place("topi", [P, NT, 2, TOPK], U32, m)
        topf = place("topf", [P, NT, 2, TOPK], F32, m)
        cand = place("cand", [P, NT, NC], F32, m)
        cidx = place("cidx", [P, NT, NC], F32, m)
        crest = place("crest", [P, NT, NC], F32, m)
        winp = place("winp", [P, NT, TOPK], U32, m)
        winf = place("winf", [P, NT, TOPK], F32, m)
        onehot = place("onehot", [P, NT * TOPK, NC], F32, m)
        winv = place("winv", [P, NT, PH, TOPK], F32, m)
        expert = place("expert", [P, NT, PH, TOPK], F32, m)
        exp_i = place("exp_i", [P, T], I32, m)
        exp_j = place("exp_j", [P, T], I32, m)
        sel = place("sel", [P, 2, NT, P], F32, m)
        gsum = place("gsum", [P, NT * PH], F32, m)
        assert m[0] <= ring_at
        m = [sel_end]
        stage = [place(f"stage{i}", [P, NKEYS, TG], F32, m) for i in range(2)]
        hot1 = [place(f"hot1_{i}", [P, 8, NKEYS], F32, m) for i in range(2)]
        hot2 = [place(f"hot2_{i}", [P, 8, NKEYS], F32, m) for i in range(2)]
        n1_cols = [place(f"n1_cols{i}", [P, 8], F32, m) for i in range(2)]
        gaps = [place(f"gaps{i}", [P, ACT_HOT2, NKEYS], F32, m) for i in range(2)]
        assert m[0] <= ring_at
        m = [ring_at]
        e_t = place("e_t", [P, KD, T], F32, m)
        m = [arena + 2 * 4 * KD * T]
        e_sq = place("e_sq", [P, KD, T], F32, m)
        m = [ring_at - 4 * 4 * T * 2]
        p_sb = place("p_sb", [P, 2, T], F32, m)
        p_hi = place("p_hi", [P, 2, T], F32R, m)
        p_lo = place("p_lo", [P, 2, T], F32R, m)

        bank = [ctx.enter_context(nc.psum_tensor(f"bank{i}", [P, T], F32)) for i in range(8)]

        ident = consts[:, C_ID:C_ID + P]
        tri = consts[:, C_TRI:C_TRI + P]
        same_chunk = consts[:, C_CHUNK:C_CHUNK + P]
        eps_col = consts[:, C_EPS:C_EPS + 1]
        one_col = consts[:, C_ONE:C_ONE + 1]
        iota = consts[:, C_IOTA:C_IOTA + P]

        def over_heads(c):
            return consts[:, c:c + P].unsqueeze(1).to_broadcast([P, H, P])

        def heads(b):
            return bank[b][:].rearrange("p (h c) -> p h c", h=H)

        consts_loaded = sem("consts_loaded")
        x_loaded = sem("x_loaded")
        layer_end = sem("layer_end")
        layer_go = sem("layer_go")
        layer_seen = sem("layer_seen")
        out_ready = sem("out_ready")
        out_stored = sem("out_stored")
        names = """at_oc2 at_rec low_dve inv_cp tk_chain places_ready picks_ready par_loaded small_loaded p_loaded slab_hi slab_lo slab_used
            sq_ready ss_ready std_ready rs_ready rstd_bc norm_used act_hi_ready act_lo_ready normed
            win_evac conv_acc conv_done conv_chain ba_ready wba_hi_ready wba_lo_ready
            gate_act gate_dve gcol_ready lam_dve lam_act
            nat_ready nat_copied
            sc_ready at_dve at_max at_exp at_wgt at_tr at_trc at_out at_oc
            gcb_ready arg_ready dec_ready gram_ready low_ready lowt_ready pow_ready inv_pe inv_dve
            rhs_ready uw_ready uw_copied step_v step_vn step_so step_state og_copied state_zero
            mix_ready wout_added wq_evac subk_ready
            score_ready score_read tk_dve tk_act selt_ready selt_copied
            n1_ready hot1_ready hot2_ready hot2_gap hot2_act_ready gm_ready gm_copied stored_a stored_b
            u_gelu w_ready w_hi_ready w_lo_ready v_added
            wg_evac wp_evac p_hi_ready p_lo_ready ple_dve layer_res""".split()
        S = {n: sem(n) for n in names}
        slab_loaded = [sem(f"slab_loaded{i}") for i in range(RING)]
        g_loaded = [sem(f"g_loaded{i}") for i in range(2)]
        per_layer = [S[n] for n in names] + slab_loaded + g_loaded
        s_par, s_slab_hi, s_slab_lo, s_used = S["par_loaded"], S["slab_hi"], S["slab_lo"], S["slab_used"]

        NORM = {"in": (8, 1), "qk": (8, 8), "mix": (8, 8), "ffn": (8, 1), "ple": (8, 1)}
        order = list(NORM)

        def before(use, what):
            return sum(NORM[k][what] for k in order[:order.index(use)])

        def sq_seen(use):
            return before(use, 0)

        def bc_seen(use):
            return before(use, 1)

        def used_seen(use):
            return 2 * H if use == "mix" else 0

        def nth(use):
            return order.index(use)

        def split_hi(act, n, slot=None):
            k = n % RING if slot is None else slot
            act.wait_ge(slab_loaded[k], (n // RING + 1) * 16 if slot is None else (n - slot + RING) * 4)
            if slot is not None or n >= RING:
                act.wait_ge(s_used, n - RING + 1)
            nc.scalar.activation(whi[k][:], raw[k][:], ACT.Copy).then_inc(s_slab_hi, 1)

        def split_lo(dve, n, slot=None):
            k = n % RING if slot is None else slot
            dve.wait_ge(s_slab_hi, n + 1)
            if slot is not None or n >= RING:
                dve.wait_ge(s_used, n - RING + 1)
            nc.vector.tensor_tensor(wlo[k][:], raw[k][:], whi[k][:].bitcast(F32), ALU.subtract).then_inc(s_slab_lo, 1)

        def three_pass(out, a_hi, a_lo, b_hi, b_lo, first, last):
            nc.tensor.matmul(out, a_hi, b_hi, start=first, stop=False)
            nc.tensor.matmul(out, a_hi, b_lo, start=False, stop=False)
            return nc.tensor.matmul(out, a_lo, b_hi, start=False, stop=last)

        def slab_product(pe, n, slot, out, hi, lo, fresh=None):
            pe.wait_ge(s_slab_lo, n + 1)
            for k in range(KD):
                if fresh is not None:
                    pe.wait_ge(S["act_lo_ready"], fresh + k + 1)
                last = three_pass(out, whi[slot][:, k, :], wlo[slot][:, k, :], hi[:, k, :], lo[:, k, :],
                                  k == 0, k == KD - 1)
            last.then_inc(s_used, 1)

        def norm_sums(pe, use, groups, chunks, sq):
            base = sq_seen(use)
            for g in range(groups):
                pe.wait_ge(S["sq_ready"], base + (g + 1) * chunks)
                for t in range(NT):
                    for c in range(chunks):
                        last = nc.tensor.matmul(bank[4][:, t * groups + g:t * groups + g + 1],
                                                sq[:, g * chunks + c, t * P:(t + 1) * P], one_col,
                                                start=c == 0, stop=c == chunks - 1)
            last.then_inc(S["ss_ready"], 1)

        def norm_spread(pe, use, groups, some=None):
            pe.wait_ge(S["rs_ready"], nth(use) + 1)
            for g in some or range(groups):
                if g >= 2:
                    pe.wait_ge(S["norm_used"], used_seen(use) + g - 1)
                for t in range(NT):
                    last = nc.tensor.matmul(bank[5 + g % 2][:, t * P:(t + 1) * P],
                                            rs[:, t * groups + g:t * groups + g + 1].to_broadcast([P, P]), ident,
                                            start=True, stop=True)
                last.then_inc(S["rstd_bc"], 1)

        def norm_std(act, use, groups, scale):
            act.wait_ge(S["ss_ready"], nth(use) + 1)
            nc.scalar.activation(cols[:, 0:NT * groups], bank[4][:, 0:NT * groups], ACT.Sqrt,
                                 bias=eps_col, scale=scale).then_inc(S["std_ready"], 1)

        def norm_rs(dve, use, groups):
            dve.wait_ge(S["std_ready"], nth(use) + 1)
            nc.vector.reciprocal(rs[:, 0:NT * groups], cols[:, 0:NT * groups]).then_inc(S["rs_ready"], 1)

        def act_squares(act, src, n, dst):
            for k in range(n):
                nc.scalar.activation(dst[:, k, :], src[:, k, :], ACT.Square).then_inc(S["sq_ready"], 1)

        def act_low_chunk(dve, src, base, k):
            dve.wait_ge(S["act_hi_ready"], base + k + 1)
            nc.vector.tensor_tensor(act_lo[:, k, :], src[:, k, :], act_hi[:, k, :].bitcast(F32),
                                    ALU.subtract).then_inc(S["act_lo_ready"], 1)

        def scale_to_wide(dve, use, gains, low_base):
            dve.wait_ge(S["rstd_bc"], bc_seen(use) + 1)
            for k in range(KD):
                last = nc.vector.scalar_tensor_tensor(wide[:, k, :], res[:, k, :], par[:, gains + k:gains + k + 1],
                                                      bank[5][:], ALU.mult, ALU.mult)
                last.then_inc(S["normed"], 1)
                if k > 0:
                    act_low_chunk(dve, wide, low_base, k - 1)
            act_low_chunk(dve, wide, low_base, KD - 1)

        def act_high(act, src, seen, base):
            for k in range(KD):
                act.wait_ge(seen, base + k + 1)
                nc.scalar.activation(act_hi[:, k, :], src[:, k, :], ACT.Copy).then_inc(S["act_hi_ready"], 1)

        def act_low(dve, src, base):
            for k in range(KD):
                act_low_chunk(dve, src, base, k)

        def mixer(delta, attend):
            for t in range(NT):
                for s in range(16):
                    delta(t, s)
                    if s % 2 == 1:
                        a = 8 * t + s // 2
                        attend(a // 2, a % 2)
            attend(H * NT, 0)

        block = ctx.enter_context(nc.Block())

        @block.sync
        def _(sp):
            sp.dma_start(consts[:], consts_d).then_inc(consts_loaded, 16)
            sp.dma_start(res[:], x_t).then_inc(x_loaded, 16)
            with sp.Fori(0, DEPTH) as layer:
                sp.dma_start(par[:], params[layer]).then_inc(s_par, 16)
                for n in range(RING):
                    sp.dma_start(raw[n][:], slabs[layer, n]).then_inc(slab_loaded[n], 16)
                sp.dma_start(wba[:], w_ba[layer]).then_inc(S["small_loaded"], 16)
                with sp.Fori(0, N_SLABS // RING - 1) as q:
                    for k in range(RING):
                        sp.wait_ge(s_slab_lo, q * RING + k + 1)
                        sp.dma_start(raw[k][:], slabs[layer, (q + 1) * RING + k]).then_inc(slab_loaded[k], 16)
                for n in range(N_SLABS // RING * RING, N_SLABS):
                    sp.wait_ge(s_slab_lo, n - RING + 1)
                    sp.dma_start(raw[n % RING][:], slabs[layer, n]).then_inc(slab_loaded[n % RING], 16)
                sp.wait_ge(S["layer_res"], KD)
                sp.sem_inc(layer_end, 1)
                sp.wait_ge(layer_go, 1)
                sp.sem_inc(layer_seen, 1)
            sp.wait_ge(out_ready, KD)
            sp.dma_start(out_t, wide[:]).then_inc(out_stored, 16)
            sp.wait_ge(out_stored, 16)

        @block.gpsimd
        def _(pool):
            pool.wait_ge(consts_loaded, 16)
            with pool.Fori(0, DEPTH) as layer:
                for hd in range(PH - 1):
                    pool.wait_ge(S["places_ready"], hd + 1)
                    for t in range(NT):
                        rows = onehot[:, t * TOPK:(t + 1) * TOPK, :]
                        nc.gpsimd.tensor_tensor(rows, rows, cidx[:, t, :].unsqueeze(1).to_broadcast([P, TOPK, NC]),
                                                ALU.mult).then_inc(S["picks_ready"], 1)
                pool.wait_ge(S["selt_copied"], NT)
                with pool.Fori(0, T // TG // 2) as q:
                    for b in range(2 * TG // 8):
                        pool.wait_ge(S["gm_ready"], q * (TG // 2) + 2 * b + 2)
                        nc.gpsimd.tensor_copy(n1_cols[b % 2][:], selt[:, 0, bass.ds(q * 2 * TG + 8 * b, 8)]
                                              ).then_inc(S["n1_ready"], 1)
                        pool.wait_ge(S["n1_ready"], q * (TG // 4) + b + 1)
                        nc.gpsimd.tensor_tensor(at_c2[:, 6:7], one_col, one_col, ALU.add)
                        for tok in range(DVE_HOT1, 8):
                            last = nc.gpsimd.tensor_scalar(hot1[b % 2][:, tok, :], iota,
                                                           n1_cols[b % 2][:, tok:tok + 1], None, ALU.is_equal)
                        last.then_inc(S["hot1_ready"], 1)
                pool.wait_ge(layer_end, 4)
                pool.nop()
                first = per_layer[0].num
                pool.sem_clear(range(first, first + len(per_layer)))
                pool.sem_clear(layer_end)
                pool.sem_inc(layer_go, 1)
                pool.wait_ge(layer_seen, 4)
                pool.nop()
                pool.sem_clear(layer_go)
                pool.sem_clear(layer_seen)

        @block.scalar
        def _(act):
            act.wait_ge(consts_loaded, 16)
            act.wait_ge(x_loaded, 16)
            with act.Fori(0, DEPTH) as layer:
                for n in range(AHEAD):
                    split_hi(act, n)
                act_squares(act, res, KD, squares)
                norm_std(act, "in", 1, 1.0 / D)
                act_high(act, wide, S["normed"], 0)
                act.wait_ge(S["small_loaded"], 16)
                nc.scalar.activation(wba_hi[:], wba[:], ACT.Copy).then_inc(S["wba_hi_ready"], 1)
                def small(i):
                    return gsm[:, i, :].rearrange("p (t c) -> p t c", t=NT)

                def decay_step(i):
                    ga = S["gate_act"]
                    if i == 0:
                        act.wait_ge(S["gate_dve"], 1)
                        ba = gsm[:, 12:14, :].rearrange("p r (t c) -> p (r t) c", c=2 * H)
                        nc.scalar.activation(small(0), ba[:, :, 0:H], ACT.Sigmoid).then_inc(ga, 1)
                        nc.scalar.activation(gsm[:, 1, 0:H], par[:, Q_ALOG:Q_ALOG + H], ACT.Exp).then_inc(ga, 1)
                        act.wait_ge(S["lam_dve"], 2)
                        nc.scalar.activation(lam[:, 66:68], lam[:, 64:66], ACT.Exp).then_inc(S["lam_act"], 1)
                        act.wait_ge(S["gate_dve"], 4)
                        nc.scalar.activation(gsm[:, 4, :], gsm[:, 4, :], ACT.Exp).then_inc(ga, 1)
                        act.wait_ge(ga, 3)
                        nc.scalar.activation(gsm[:, 4, :], gsm[:, 4, :], ACT.Ln, bias=one_col).then_inc(ga, 1)
                    else:
                        act.wait_ge(S["gate_dve"], 7)
                        nc.scalar.activation(gsm[:, 7, :], gsm[:, 14, :], ACT.Exp).then_inc(ga, 1)
                        act.wait_ge(S["gate_dve"], 8)
                        nc.scalar.activation(gsm[:, 9, :], gsm[:, 8, :], ACT.Exp).then_inc(ga, 1)

                for n in range(28):
                    split_hi(act, n + AHEAD)
                    act.wait_ge(s_used, n + 1)
                    b = bank[n % RING]
                    if n < 12:
                        if n >= 2:
                            act.wait_ge(S["conv_acc"], n - 1)
                        i = nc.scalar.activation(craw[n % 2][:], b[:], ACT.Copy)
                    elif n < 16:
                        i = nc.scalar.activation(gzt[:, n - 12, :], b[:], ACT.Silu)
                    else:
                        i = nc.scalar.activation((daq, dak, davt)[(n - 16) // H][:, n % H, :], b[:], ACT.Copy)
                    i.then_inc(S["win_evac"], 1)
                    if 0 < n <= 12:
                        c = n - 1
                        dst = (gqt, gkt, gvt)[c // H]
                        act.wait_ge(S["conv_acc"], c + 1)
                        nc.scalar.activation(dst[:, c % H, :], dst[:, c % H, :], ACT.Silu).then_inc(S["conv_done"], 1)
                    if n == 13:
                        decay_step(0)
                    if n in (14, 15):
                        act.wait_ge(S["conv_done"], 2 * H)
                        src = (gqt, gkt)[n - 14]
                        for j in range(H):
                            nc.scalar.activation(mixt[:, (n - 14) * H + j, :], src[:, j, :],
                                                 ACT.Square).then_inc(S["sq_ready"], 1)
                    if n == 16:
                        decay_step(1)
                    if n == 18:
                        norm_std(act, "qk", 2 * H, 1.0)
                for i in range(12):
                    act.wait_ge(S["nat_ready"], i + 1)
                    dst = (v_nat, gv_nat, kn_nat)[i // NT]
                    nc.scalar.activation(dst[:, i % NT].rearrange("p h c -> p (h c)"), bank[(4, 7)[i % 2]][:],
                                         ACT.Copy).then_inc(S["nat_copied"], 1)

                def attend(u, half):
                    t = u % NT
                    kl = (t + 1) * P
                    if half == 0:
                        if u > 0 and t == 0:
                            act.wait_ge(S["at_out"], u)
                            nc.scalar.activation(mixt[:, u // NT - 1, :], bank[4][:], ACT.Copy).then_inc(S["at_oc"], 1)
                        for c in range(2):
                            if u == H * NT:
                                break
                            act.wait_ge(S["at_max"], 2 * u + c + 1)
                            nc.scalar.activation(at_s[:, c, 0:kl], at_s[:, c, 0:kl], ACT.Exp, bias=at_c[:, c:c + 1],
                                                 scale=DQK ** -0.5, accum_out=at_c[:, 2 + c:3 + c]
                                                 ).then_inc(S["at_exp"], 1)
                    else:
                        act.wait_ge(S["at_tr"], u + 1)
                        if u > 0:
                            act.wait_ge(S["at_out"], u)
                        nc.scalar.activation(at_wt[:, 0:t + 1, :], heads(5)[:, 0:t + 1, :],
                                             ACT.Copy).then_inc(S["at_trc"], 1)

                def delta(t, s):
                    if s == 0:
                        act.wait_ge(S["arg_ready"], 8 * t + 8)
                        nc.scalar.activation(egc_b[:], heads(6), ACT.Exp).then_inc(S["dec_ready"], 1)
                        nc.scalar.activation(dec_t[:], dec_t[:], ACT.Exp).then_inc(S["dec_ready"], 1)
                        nc.scalar.activation(dec[:], dec[:], ACT.Exp, scale=-1.0).then_inc(S["dec_ready"], 1)
                    elif s == 11:
                        act.wait_ge(S["uw_ready"], t + 1)
                        nc.scalar.activation(w_tr[:], heads(7), ACT.Copy).then_inc(S["uw_copied"], 1)
                    elif s in (13, 15):
                        j = (s - 13) // 2
                        act.wait_ge(S["step_so"], 2 * t + j + 1)
                        src = bank[3][:, 0:H * CHUNK].rearrange("p (h c) -> p h c", h=H)
                        dst = mixt[:, H:2 * H, t * P + j * CHUNK:t * P + (j + 1) * CHUNK]
                        nc.scalar.activation(dst, src, ACT.Copy).then_inc(S["og_copied"], 1)

                mixer(delta, attend)
                act.wait_ge(S["at_oc"], H)
                act.wait_ge(S["og_copied"], 2 * NT)
                act.wait_ge(S["step_state"], 2 * NT)
                act_squares(act, mixt, 2 * H, sq_mix)
                norm_std(act, "mix", 2 * H, 1.0 / P)
                for k in range(KD):
                    if k < H:
                        act.wait_ge(S["norm_used"], used_seen("mix") + k + 1)
                    else:
                        act.wait_ge(S["mix_ready"], k - H + 1)
                    nc.scalar.activation(act_hi[:, k, :], mixt[:, k, :], ACT.Copy).then_inc(S["act_hi_ready"], 1)
                for n in range(S_OUT, S_WQ):
                    split_hi(act, n + AHEAD)
                for k in range(KD):
                    act.wait_ge(S["wout_added"], k + 1)
                    nc.scalar.activation(squares[:, k, :], res[:, k, :], ACT.Square).then_inc(S["sq_ready"], 1)
                norm_std(act, "ffn", 1, 1.0 / D)
                act.wait_ge(s_used, S_WQ)
                act_high(act, wide, S["normed"], KD)
                act.dma_start(subk[:], subkeys[layer]).then_inc(S["subk_ready"], 16)
                for p, (kind, i) in enumerate(SEL_SEQ):
                    n = S_WQ + p
                    split_hi(act, n + AHEAD)
                    act.wait_ge(s_used, n + 1)
                    if p == 0:
                        act.wait_ge(S["act_lo_ready"], 3 * KD)
                    if kind == "q":
                        if i >= 4:
                            act.wait_ge(S["score_ready"], i // 2 - 1)
                        nc.scalar.activation(qt[:, i % 4, :], bank[i % 2][:], ACT.Copy).then_inc(S["wq_evac"], 1)
                    else:
                        dst = hb if i < GB else h_ring
                        nc.scalar.activation(dst[:, i % GB, :], bank[2 + i % 2][:], ACT.Gelu).then_inc(S["u_gelu"], 1)
                act.wait_ge(S["tk_dve"], 1)
                nc.scalar.activation(winv[:], winv[:], ACT.Exp).then_inc(S["tk_act"], 1)
                def gap_rows(batch, first_token, slot):
                    act.wait_ge(S["gm_ready"], batch * 2 + 2)
                    for tok in range(8 - ACT_HOT2, 8):
                        last = nc.scalar.activation(gaps[slot][:, tok - 8 + ACT_HOT2, :], iota, ACT.Abs,
                                                    bias=selt[:, 1, bass.ds(first_token + tok, 1)], scale=-1.0)
                    last.then_inc(S["hot2_gap"], 1)

                def gate_rows(batch, first_token, slot):
                    act.wait_ge(S["hot2_gap"], batch + 1)
                    for tok in range(8 - ACT_HOT2, 8):
                        last = nc.scalar.activation(hot2[slot][:, tok, :], gaps[slot][:, tok - 8 + ACT_HOT2, :], ACT.Relu,
                                                    bias=selt[:, 2, bass.ds(first_token + tok, 1)],
                                                    scale=selt[:, 3, bass.ds(first_token + tok, 1)])
                    last.then_inc(S["hot2_act_ready"], 1)

                def two_stages(q, final):
                    for i in range(2 * TG // 4):
                        half, at4 = divmod(i, TG // 4)
                        rows = not (final and i >= 2 * TG // 4 - 2)
                        ahead = q * (TG // 4) + (i // 2 + 1)
                        token = q * (2 * TG) + 8 * (i // 2 + 1)
                        if rows and i % 2 == 0:
                            gap_rows(ahead, token, (i // 2 + 1) % 2)
                        act.wait_ge(S["gm_ready"], q * (TG // 2) + i + 5)
                        if at4 == 0:
                            act.wait_ge((S["stored_a"], S["stored_b"])[half], q * 16 + 1)
                        dst = stage[half][:, :, 4 * at4:4 * at4 + 4].rearrange("p n t -> p t n")
                        nc.scalar.activation(dst, heads(4 + i % 4), ACT.Copy).then_inc(S["gm_copied"], 1)
                        if rows and i % 2 == 0:
                            gate_rows(ahead, token, (i // 2 + 1) % 2)
                        if at4 == TG // 4 - 1:
                            act.wait_ge(S["gm_copied"], q * (TG // 2) + i + 5)
                            act.dma_start(g_dram[q * 2 + half], stage[half][:]).then_inc(
                                (S["stored_a"], S["stored_b"])[half], 16)
                act.wait_ge(S["selt_copied"], NT)
                gap_rows(0, 0, 0)
                gate_rows(0, 0, 0)
                with act.Fori(0, T // TG // 2 - 1) as q:
                    two_stages(q, False)
                two_stages(T // TG // 2 - 1, True)
                act.wait_ge(S["stored_a"], T // TG // 2 * 16 + 1)
                act.wait_ge(S["stored_b"], T // TG // 2 * 16 + 1)

                def load_gates(g, s):
                    act.dma_start(g_sb[s][:].rearrange("p s b t -> p s (b t)"),
                                  g_dram[:, :, bass.ds(g * GB + 4 * s, 4), :].rearrange("s p n t -> p s (n t)")
                                  ).then_inc(g_loaded[s], 16)

                def w_high(g, j, pg):
                    act.wait_ge(S["w_ready"], g * GB + j + 1)
                    nc.scalar.activation(w_hi[pg][:, j, :], act_w[j % 2][:], ACT.Copy).then_inc(S["w_hi_ready"], 1)
                    if j % 4 == 3 and not (isinstance(g, int) and g == GROUPS - 1):
                        load_gates(g + 1, j // 4)

                load_gates(0, 0)
                load_gates(0, 1)
                for j in range(GB):
                    w_high(0, j, 0)

                def group(g, pg):
                    for j in range(GB):
                        n = g * 16 + (S_UV + 2 * j)
                        split_hi(act, n + AHEAD, (2 * j + AHEAD) % RING)
                        w_high(g + 1, j, 1 - pg)
                        act.wait_ge(s_used, n + 1)
                        nc.scalar.activation(h_ring[:, j, :], bank[2 * (j % 2)][:], ACT.Gelu).then_inc(S["u_gelu"], 1)
                        split_hi(act, n + 1 + AHEAD, (2 * j + 1 + AHEAD) % RING)
                with act.Fori(0, 7) as it:
                    group(it * 2, 0)
                    group(it * 2 + 1, 1)
                def res_high(k):
                    act.wait_ge(S["v_added"], (GROUPS - 1) * KD + k + 2)
                    nc.scalar.activation(act_hi[:, k, :], res[:, k, :], ACT.Copy).then_inc(S["act_hi_ready"], 1)

                for p, (kind, j) in enumerate(TAIL):
                    n = S_V_LAST + p
                    split_hi(act, n + AHEAD)
                    if j < GB and kind == "v":
                        w_high(GROUPS - 1, j, 1)
                    if j == GB - 1:
                        act.dma_start(p_sb[:], p_t[layer]).then_inc(S["p_loaded"], 16)
                    if j == GB + 1:
                        act.wait_ge(S["p_loaded"], 16)
                        nc.scalar.activation(p_hi[:], p_sb[:], ACT.Copy).then_inc(S["p_hi_ready"], 1)
                    if kind == "v" and GB < j != 12:
                        res_high(j - GB - 1)
                    if kind == "p":
                        act.wait_ge(s_used, n + 1)
                        for i in range(4):
                            nc.scalar.activation(e_t[:, 4 * j + i, :], bank[4 + i][:], ACT.Copy).then_inc(S["wp_evac"], 1)
                        if j == 0:
                            res_high(3)
                    if j in (12, 13) and kind == "v":
                        for k in range(4 * (j - 12), 4 * (j - 12) + 4):
                            act.wait_ge(S["wp_evac"], k + 1)
                            nc.scalar.activation(e_sq[:, k, :], e_t[:, k, :], ACT.Square).then_inc(S["sq_ready"], 1)
                    if j == 15:
                        norm_std(act, "ple", 1, 1.0 / D)
                res_high(KD - 1)
                for i in range(KD):
                    if S_WG + i + AHEAD < N_SLABS:
                        split_hi(act, S_WG + i + AHEAD)
                    act.wait_ge(s_used, S_WG + i + 1)
                    if i >= 2:
                        act.wait_ge(S["layer_res"], i - 1)
                    nc.scalar.activation(act_w[i % 2][:], bank[i % RING][:], ACT.Sigmoid).then_inc(S["wg_evac"], 1)
                act.wait_ge(S["layer_res"], KD)
                act.sem_inc(layer_end, 1)
                act.wait_ge(layer_go, 1)
                act.sem_inc(layer_seen, 1)
            act_squares(act, res, KD, squares)
            norm_std(act, "in", 1, 1.0 / D)

        @block.tensor
        def _(pe):
            pe.wait_ge(consts_loaded, 16)
            with pe.Fori(0, DEPTH) as layer:
                norm_sums(pe, "in", 1, KD, squares)
                norm_spread(pe, "in", 1)
                for n in range(RING):
                    slab_product(pe, n, n, bank[n][:], act_hi, act_lo, 0 if n == 0 else None)
                def four_slabs(q):
                    for k in range(RING):
                        pe.wait_ge(S["win_evac"], q * RING + k + 1)
                        slab_product(pe, q * RING + k + RING, k, bank[k][:], act_hi, act_lo)
                with pe.Fori(0, 2) as q:
                    four_slabs(q)
                pe.wait_ge(S["wba_lo_ready"], 1)
                for t in range(NT):
                    for k in range(KD):
                        ts = slice(t * P, (t + 1) * P)
                        last = three_pass(bank[7][:, 8 * t:8 * t + 8], act_hi[:, k, ts], act_lo[:, k, ts],
                                          wba_hi[:, k, :], wba_lo[:, k, :], k == 0, k == KD - 1)
                last.then_inc(S["ba_ready"], 1)
                four_slabs(2)
                pe.wait_ge(S["gate_dve"], 6)
                nc.tensor.matmul(bank[7][:, 64:80], tri, gsm[:, 6, :], start=True, stop=True)
                nc.tensor.matmul(bank[7][:, 80:96], same_chunk, gsm[:, 6, :], start=True,
                                 stop=True).then_inc(S["gcol_ready"], 1)
                four_slabs(3)
                norm_sums(pe, "qk", 2 * H, 1, mixt)
                four_slabs(4)
                for k in range(RING):
                    norm_spread(pe, "qk", 2 * H, range(2 * k, 2 * k + 2))
                    pe.wait_ge(S["win_evac"], 5 * RING + k + 1)
                    slab_product(pe, 6 * RING + k, k, bank[k][:], act_hi, act_lo)
                pe.wait_ge(S["gate_dve"], 7)
                pe.wait_ge(S["conv_done"], 12)
                pe.wait_ge(S["win_evac"], S_OUT)
                pe.wait_ge(S["norm_used"], used_seen("qk") + 2 * H)
                for i in range(12):
                    if i >= 2:
                        pe.wait_ge(S["nat_copied"], i - 1)
                    src = (davt, gvt, gkt)[i // NT]
                    t = i % NT
                    for hd in range(H):
                        last = nc.tensor.transpose(heads((4, 7)[i % 2])[:, hd, :], src[:, hd, t * P:(t + 1) * P], ident)
                    last.then_inc(S["nat_ready"], 1)

                def attend(u, half):
                    if half == 0 and u > 0:
                        hd, t = divmod(u - 1, NT)
                        pe.wait_ge(S["at_trc"], u)
                        if t == 0 and hd > 0:
                            pe.wait_ge(S["at_oc"], hd)
                        for k in range(t + 1):
                            last = nc.tensor.matmul(bank[4][:, t * P:(t + 1) * P], v_nat[:, k, hd, :], at_wt[:, k, :],
                                                    start=k == 0, stop=k == t)
                        last.then_inc(S["at_out"], 1)
                    if u == H * NT:
                        return
                    hd, t = divmod(u, NT)
                    kl = (t + 1) * P
                    if half == 0:
                        if u > 0:
                            pe.wait_ge(S["at_dve"], 1 + 2 * u)
                        for c in range(2):
                            cs = slice(c * DQK, (c + 1) * DQK)
                            nc.tensor.matmul(bank[c][:, 0:kl], daq[cs, hd, t * P:(t + 1) * P], dak[cs, hd, 0:kl],
                                             start=True, stop=True).then_inc(S["sc_ready"], 1)
                    else:
                        pe.wait_ge(S["at_wgt"], u + 1)
                        if u > 0:
                            pe.wait_ge(S["at_trc"], u)
                        for k in range(t + 1):
                            last = nc.tensor.transpose(heads(5)[:, k, :], at_w[:, k * P:(k + 1) * P], ident)
                        last.then_inc(S["at_tr"], 1)

                def four(out, lhs, rhs):
                    for hd in range(H):
                        last = nc.tensor.matmul(out[:, hd, :], lhs[:, hd, :], rhs[:, hd, :], start=True, stop=True)
                    return last

                def delta(t, s):
                    ts = slice(t * P, (t + 1) * P)
                    b = 5 * t
                    if s == 0:
                        if t > 0:
                            pe.wait_ge(S["step_state"], 2 * t)
                            pe.wait_ge(S["og_copied"], 2 * t)
                        for hd in range(H):
                            col = gsm[:, 6, t * H + hd:t * H + hd + 1]
                            last = nc.tensor.matmul(heads(6)[:, hd, :], col.to_broadcast([P, P]), tri,
                                                    start=True, stop=True)
                        last.then_inc(S["gcb_ready"], 1)
                        for hd in range(H):
                            nc.tensor.matmul(heads(2)[:, hd, :], gkt[:, hd, ts], gkt[:, hd, ts], start=True, stop=True)
                        for hd in range(H):
                            last = nc.tensor.matmul(heads(3)[:, hd, :], gkt[:, hd, ts], gqt[:, hd, ts],
                                                    start=True, stop=True)
                        last.then_inc(S["gram_ready"], 1)
                    elif s == 2:
                        pe.wait_ge(S["low_ready"], t + 1)
                        for hd in range(H):
                            last = nc.tensor.transpose(heads(7)[:, hd, :], low64[:, hd, :], ident)
                        last.then_inc(S["lowt_ready"], 1)
                    elif s == 3:
                        pe.wait_ge(S["pow_ready"], b + 1)
                        four(heads(2), pow_n, pow_m)
                        four(heads(7), pow_m, pow_n).then_inc(S["inv_pe"], 1)
                    elif s == 4:
                        pe.wait_ge(S["pow_ready"], b + 2)
                        four(heads(6), pow_m2, inv_a)
                        four(heads(2), pow_n2, pow_m2)
                        four(heads(7), pow_m2, pow_n2).then_inc(S["inv_pe"], 1)
                    elif s == 5:
                        pe.wait_ge(S["pow_ready"], b + 3)
                        four(heads(6), pow_m, inv_b)
                        four(heads(2), pow_n, pow_m).then_inc(S["inv_pe"], 1)
                    elif s == 6:
                        pe.wait_ge(S["pow_ready"], b + 4)
                        four(heads(6), pow_m2, inv_a).then_inc(S["inv_pe"], 1)
                    elif s in (7, 9):
                        i = (s - 7) // 2
                        low, cur = ((low32, inv_b), (low64, inv_a))[i]
                        pe.wait_ge(S["inv_dve"], 6 * t + 1 + 3 * i)
                        four(heads(2), low, cur)
                        for hd in range(H):
                            last = nc.tensor.transpose(heads(7)[:, hd, :], cur[:, hd, :], ident)
                        last.then_inc(S["inv_pe"], 1)
                    elif s in (8, 10):
                        pe.wait_ge(S["inv_dve"], 6 * t + 3 + 3 * ((s - 8) // 2))
                        four(heads(6), inv_t, zmat).then_inc(S["inv_pe"], 1)
                    elif s == 11:
                        pe.wait_ge(S["pow_ready"], b + 5)
                        pe.wait_ge(S["rhs_ready"], 16 * (t + 1))
                        four(heads(2), inv_b, vbeta)
                        four(heads(7), kbg, inv_b).then_inc(S["uw_ready"], 1)
                    elif s >= 12:
                        j = (s - 12) // 2
                        c = 2 * t + j
                        rows = slice(j * CHUNK, (j + 1) * CHUNK)
                        s_in = state[c % 2]
                        if s % 2 == 0:
                            pe.wait_ge(S["uw_copied"], 2 * t + 2)
                            if c == 0:
                                pe.wait_ge(S["state_zero"], 1)
                            else:
                                pe.wait_ge(S["step_state"], c)
                            for hd in range(H):
                                last = nc.tensor.matmul(heads(6)[rows, hd, :], w_tr[:, hd, rows], s_in[:, hd, :],
                                                        start=True, stop=True)
                            last.then_inc(S["step_v"], 1)
                        else:
                            pe.wait_ge(S["step_vn"], c + 1)
                            if c > 0:
                                pe.wait_ge(S["og_copied"], c)
                            for hd in range(H):
                                out = bank[3][:, hd * CHUNK:(hd + 1) * CHUNK]
                                nc.tensor.matmul(out, s_in[:, hd, :], qdec[:, hd, rows], start=True, stop=False)
                                last = nc.tensor.matmul(out, vnew[rows, hd, :], intra[rows, hd, rows],
                                                        start=False, stop=True)
                            for hd in range(H):
                                last = nc.tensor.matmul(heads(2)[:, hd, :], kdec[rows, hd, :], vnew[rows, hd, :],
                                                        start=True, stop=True)
                            last.then_inc(S["step_so"], 1)

                pe.wait_ge(S["nat_copied"], 12)
                mixer(delta, attend)
                pe.wait_ge(S["at_oc"], H)
                norm_sums(pe, "mix", 2 * H, 1, sq_mix)
                norm_spread(pe, "mix", 2 * H)
                for i in range(KD):
                    if i >= RING:
                        pe.wait_ge(S["wout_added"], i - RING + 1)
                    slab_product(pe, S_OUT + i, i % RING, bank[i % RING][:], act_hi, act_lo, KD if i == 0 else None)
                norm_sums(pe, "ffn", 1, KD, squares)
                norm_spread(pe, "ffn", 1)
                pe.wait_ge(S["subk_ready"], 16)
                for p, (kind, i) in enumerate(SEL_SEQ):
                    if i >= 2:
                        pe.wait_ge(S["wq_evac" if kind == "q" else "u_gelu"], i - 1)
                    b = bank[i % 2 if kind == "q" else 2 + i % 2]
                    slab_product(pe, S_WQ + p, p % RING, b[:], act_hi, act_lo, 2 * KD if p == 0 else None)
                    if (kind == "u" and i % 2 == 0 and i < 14) or p == 1:
                        for hd in ([0] if p == 1 else [i // 2 + 1]):
                            pe.wait_ge(S["wq_evac"], 2 * hd + 2)
                            if hd >= 2:
                                pe.wait_ge(S["score_read"], hd - 1)
                            for t in range(NT):
                                for c in range(2):
                                    last = nc.tensor.matmul(heads(4 + 2 * (hd % 2) + t // 2)[:, t % 2 * 2 + c, :],
                                                            qt[:, 2 * (hd % 2) + c, t * P:(t + 1) * P],
                                                            subk[:, 2 * hd + c, :], start=True, stop=True)
                            last.then_inc(S["score_ready"], 1)
                pe.wait_ge(S["tk_dve"], 2)
                pe.wait_ge(S["u_gelu"], 2 * GB)
                for t in range(NT):
                    for i in range(3):
                        src = sel[:, i, t, :] if i < 2 else winv[:, t].rearrange("p h k -> p (h k)")
                        last = nc.tensor.transpose(heads(t)[:, i, :], src, ident)
                    last.then_inc(S["selt_ready"], 1)
                pe.sem_inc(S["gm_ready"], 4)
                pe.sem_inc(S["gm_copied"], 4)
                with pe.Fori(0, T // TG // 2) as q:
                    for b in range(2 * TG // 8):
                        pe.wait_ge(S["hot1_ready"], q * (TG // 4) + b + 1)
                        pe.wait_ge(S["hot2_ready"], q * (TG // 4) + b + 1)
                        pe.wait_ge(S["hot2_act_ready"], q * (TG // 4) + b + 1)
                        for half in range(2):
                            i = 2 * b + half
                            pe.wait_ge(S["gm_copied"], q * (TG // 2) + i + 1)
                            for s in range(4):
                                tok = 4 * half + s
                                last = nc.tensor.matmul(heads(4 + i % 4)[:, s, :], hot1[b % 2][:, tok, :],
                                                        hot2[b % 2][:, tok, :], start=True, stop=True)
                            last.then_inc(S["gm_ready"], 1)

                def v_slab(g, pg, j, n, slot):
                    pe.wait_ge(S["w_lo_ready"], g * GB + GB)
                    if j > 0:
                        pe.wait_ge(S["v_added"], g * GB + j)
                    slab_product(pe, n, slot, bank[1 + 2 * (j % 2)][:], w_hi[pg], w_lo[pg])

                def group(g, pg):
                    for j in range(GB):
                        n = g * 16 + (S_UV + 2 * j)
                        pe.wait_ge(S["u_gelu"], g * GB + (2 * GB + j - 1))
                        slab_product(pe, n, 2 * j % RING, bank[2 * (j % 2)][:], act_hi, act_lo)
                        v_slab(g, pg, j, n + 1, (2 * j + 1) % RING)
                with pe.Fori(0, 7) as it:
                    group(it * 2, 0)
                    group(it * 2 + 1, 1)
                for p, (kind, j) in enumerate(TAIL):
                    n = S_V_LAST + p
                    if kind == "v":
                        v_slab(GROUPS - 2 + j // GB, j // GB, j % GB, n, n % RING)
                    else:
                        pe.wait_ge(S["p_lo_ready"], 1)
                        pe.wait_ge(s_slab_lo, n + 1)
                        for i in range(4):
                            if j == 1:
                                pe.wait_ge(S["wp_evac"], i + 1)
                            for k in range(2):
                                last = three_pass(bank[4 + i][:], whi[n % RING][:, 2 * i + k, :],
                                                  wlo[n % RING][:, 2 * i + k, :], p_hi[:, k, :], p_lo[:, k, :],
                                                  k == 0, k == 1)
                        last.then_inc(s_used, 1)
                    if j == 14:
                        norm_sums(pe, "ple", 1, KD, e_sq)
                norm_spread(pe, "ple", 1)
                for i in range(KD):
                    if i >= RING:
                        pe.wait_ge(S["wg_evac"], i - RING + 1)
                    n = S_WG + i
                    slab_product(pe, n, n % RING, bank[i % RING][:], act_hi, act_lo, 3 * KD if i == 0 else None)
                pe.wait_ge(S["layer_res"], KD)
                pe.sem_inc(layer_end, 1)
                pe.wait_ge(layer_go, 1)
                pe.sem_inc(layer_seen, 1)
            norm_sums(pe, "in", 1, KD, squares)
            norm_spread(pe, "in", 1)

        @block.vector
        def _(dve):
            V = nc.vector
            dve.wait_ge(consts_loaded, 16)
            dve.wait_ge(x_loaded, 16)
            with dve.Fori(0, DEPTH) as layer:
                for n in range(AHEAD):
                    split_lo(dve, n)
                dve.wait_ge(s_par, 16)
                lamv = par[:, Q_LAM:Q_LAM + 4 * DQK].rearrange("p (i c) -> p i c", i=4)
                V.tensor_tensor_reduce(lam[:, 0:DQK], lamv[:, 0, :], lamv[:, 1, :], 1.0, 0.0, ALU.mult, ALU.add,
                                       lam[:, 64:65]).then_inc(S["lam_dve"], 1)
                dve.wait_ge(S["lam_dve"], 1)
                V.tensor_tensor_reduce(lam[:, 0:DQK], lamv[:, 2, :], lamv[:, 3, :], 1.0, 0.0, ALU.mult, ALU.add,
                                       lam[:, 65:66]).then_inc(S["lam_dve"], 1)
                norm_rs(dve, "in", 1)
                scale_to_wide(dve, "in", Q_MIX, 0)
                dve.wait_ge(S["wba_hi_ready"], 1)
                V.tensor_tensor(wba_lo[:], wba[:], wba_hi[:].bitcast(F32), ALU.subtract).then_inc(S["wba_lo_ready"], 1)
                def small(i):
                    return gsm[:, i, :].rearrange("p (t c) -> p t c", t=NT)
                gd = S["gate_dve"]

                def decay_step(i):
                    if i == 0:
                        dve.wait_ge(S["ba_ready"], 1)
                        V.tensor_copy(gsm[:, 12:14, :], bank[7][:, 0:32].rearrange("p (r c) -> p r c", r=2)).then_inc(gd, 1)
                        dve.wait_ge(gd, 1)
                        ba = gsm[:, 12:14, :].rearrange("p r (t c) -> p (r t) c", c=2 * H)
                        V.tensor_tensor(small(2), ba[:, :, H:2 * H],
                                        par[:, Q_DT:Q_DT + H].unsqueeze(1).to_broadcast([P, NT, H]),
                                        ALU.add).then_inc(gd, 1)
                        dve.wait_ge(gd, 2)
                        V.tensor_scalar(gsm[:, 3, :], gsm[:, 2, :], 0.0, None, ALU.max).then_inc(gd, 1)
                        V.scalar_tensor_tensor(gsm[:, 4, :], gsm[:, 2, :], -1.0, gsm[:, 2, :],
                                               ALU.mult, ALU.min).then_inc(gd, 1)
                    elif i == 1:
                        dve.wait_ge(S["gate_act"], 4)
                        V.tensor_tensor(gsm[:, 5, :], gsm[:, 3, :], gsm[:, 4, :], ALU.add).then_inc(gd, 1)
                        dve.wait_ge(gd, 5)
                        V.scalar_tensor_tensor(small(6), small(5), -1.0,
                                               gsm[:, 1, 0:H].unsqueeze(1).to_broadcast([P, NT, H]),
                                               ALU.mult, ALU.mult).then_inc(gd, 1)
                        dve.wait_ge(S["lam_act"], 1)
                        V.tensor_tensor(lam[:, 68:69], lam[:, 66:67], lam[:, 67:68], ALU.subtract).then_inc(S["lam_dve"], 1)
                        dve.wait_ge(S["lam_dve"], 3)
                        V.tensor_tensor(lam[:, 69:70], lam[:, 68:69], par[:, Q_LINIT:Q_LINIT + 1],
                                        ALU.add).then_inc(S["lam_dve"], 1)
                        V.tensor_tensor(lam[:, 70:71], par[:, Q_SUB:Q_SUB + 1], par[:, Q_LINIT + 1:Q_LINIT + 2],
                                        ALU.mult).then_inc(S["lam_dve"], 1)
                    else:
                        dve.wait_ge(S["gcol_ready"], 1)
                        V.tensor_copy(gsm[:, 14:16, :], bank[7][:, 64:96].rearrange("p (r c) -> p r c", r=2)).then_inc(gd, 1)
                        dve.wait_ge(gd, 7)
                        V.tensor_tensor(gsm[:, 8, :], gsm[:, 15, :], gsm[:, 14, :], ALU.subtract).then_inc(gd, 1)
                        dve.wait_ge(S["gate_act"], 5)
                        V.tensor_tensor(gsm[:, 11, :], gsm[:, 0, :], gsm[:, 7, :], ALU.mult).then_inc(gd, 1)

                for n in range(28):
                    split_lo(dve, n + AHEAD)
                    if n < 12:
                        c = n
                        dst = (gqt, gkt, gvt)[c // H][:, c % H, :]
                        dve.wait_ge(S["win_evac"], n + 1)
                        taps = [par[:, Q_CONV + tap * 12 + c:Q_CONV + tap * 12 + c + 1] for tap in range(CONV_K)]
                        V.tensor_scalar(dst, craw[c % 2][:], taps[3], None, ALU.mult).then_inc(S["conv_chain"], 1)
                        for lag in range(1, CONV_K):
                            dve.wait_ge(S["conv_chain"], 3 * c + lag)
                            i = V.scalar_tensor_tensor(dst[:, lag:T], craw[c % 2][:, 0:T - lag], taps[3 - lag],
                                                       dst[:, lag:T], ALU.mult, ALU.add)
                            i.then_inc(S["conv_chain"] if lag < 3 else S["conv_acc"], 1)
                    if n in (12, 14, 16):
                        decay_step((n - 12) // 2)
                    if n == 19:
                        norm_rs(dve, "qk", 2 * H)
                    if n >= 24:
                        for j in (2 * (n - 24), 2 * (n - 24) + 1):
                            dve.wait_ge(S["rstd_bc"], bc_seen("qk") + j + 1)
                            x = (gqt if j < H else gkt)[:, j % H, :]
                            V.scalar_tensor_tensor(x, x, P ** -0.5 if j < H else 1.0, bank[5 + j % 2][:], ALU.mult,
                                                   ALU.mult).then_inc(S["norm_used"], 1)
                dve.wait_ge(S["conv_acc"], 12)
                dve.sem_inc(S["at_dve"], 1)

                ad = S["at_dve"]
                SLOPE = [2.0 ** (-8.0 * (i + 1) / H) for i in range(H)]

                def attend(u, half):
                    if u == H * NT:
                        return
                    hd, t = divmod(u, NT)
                    kl = (t + 1) * P
                    if half == 1:
                        weights(u, kl)
                        return
                    if u > 0:
                        dve.wait_ge(S["at_wgt"], u)
                        dve.wait_ge(S["at_exp"], 2 * u)
                    bias = consts[:, C_DIST + T - kl:C_DIST + T]
                    for c in range(2):
                        dve.wait_ge(S["sc_ready"], 2 * u + c + 1)
                        V.scalar_tensor_tensor(at_s[:, c, 0:kl], bias, SLOPE[hd] * DQK ** 0.5, bank[c][:, 0:kl],
                                               ALU.mult, ALU.add).then_inc(ad, 1)
                    for c in range(2):
                        dve.wait_ge(ad, 1 + 2 * u + c + 1)
                        V.tensor_reduce(at_c[:, 4 + c:5 + c], at_s[:, c, 0:kl], AX_X, ALU.max).then_inc(S["at_oc2"], 1)
                    for c in range(2):
                        dve.wait_ge(S["at_oc2"], 2 * u + c + 1)
                        V.tensor_scalar(at_c[:, c:c + 1], at_c[:, 4 + c:5 + c], -DQK ** -0.5, None,
                                        ALU.mult).then_inc(S["at_max"], 1)

                def weights(u, kl):
                    dve.wait_ge(S["at_exp"], 2 * u + 2)
                    V.reciprocal(at_c[:, 4:6], at_c[:, 2:4]).then_inc(S["at_rec"], 1)
                    dve.wait_ge(S["at_rec"], 3 * u + 1)
                    V.tensor_tensor(at_c[:, 6:7], at_c[:, 5:6], lam[:, 69:70], ALU.mult).then_inc(S["at_rec"], 1)
                    dve.wait_ge(S["at_rec"], 3 * u + 2)
                    V.tensor_scalar(at_s[:, 1, 0:kl], at_s[:, 1, 0:kl], at_c[:, 6:7], None,
                                    ALU.mult).then_inc(S["at_rec"], 1)
                    dve.wait_ge(S["at_rec"], 3 * u + 3)
                    if u > 0:
                        dve.wait_ge(S["at_tr"], u)
                    V.scalar_tensor_tensor(at_w[:, 0:kl], at_s[:, 0, 0:kl], at_c[:, 4:5], at_s[:, 1, 0:kl],
                                           ALU.mult, ALU.subtract).then_inc(S["at_wgt"], 1)

                def delta(t, s):
                    if s == 0:
                        if t == 0:
                            V.memset(state[0][:], 0.0).then_inc(S["state_zero"], 1)
                        dve.wait_ge(S["gcb_ready"], t + 1)
                        for hd in range(H):
                            col = gsm[:, 14, t * H + hd:t * H + hd + 1]
                            V.scalar_tensor_tensor(dec_t[:, hd, :], heads(6)[:, hd, :], col,
                                                   consts[:, C_NEGT:C_NEGT + P],
                                                   ALU.subtract, ALU.add).then_inc(S["arg_ready"], 1)
                            V.scalar_tensor_tensor(dec[:, hd, :], heads(6)[:, hd, :], col,
                                                   consts[:, C_POSD:C_POSD + P],
                                                   ALU.subtract, ALU.add).then_inc(S["arg_ready"], 1)
                        for hd in range(H):
                            i = t * H + hd
                            V.tensor_scalar(vbeta[:, hd, :], gv_nat[:, t, hd, :], gsm[:, 0, i:i + 1], None,
                                            ALU.mult).then_inc(S["rhs_ready"], 1)
                            V.tensor_scalar(kbg[:, hd, :], kn_nat[:, t, hd, :], gsm[:, 11, i:i + 1], None,
                                            ALU.mult).then_inc(S["rhs_ready"], 1)
                            V.tensor_scalar(kdec[:, hd, :], kn_nat[:, t, hd, :], gsm[:, 9, i:i + 1], None,
                                            ALU.mult).then_inc(S["rhs_ready"], 1)
                    elif s == 1:
                        dve.wait_ge(S["dec_ready"], 3 * t + 3)
                        dve.wait_ge(S["gram_ready"], t + 1)
                        for hd in range(H):
                            V.scalar_tensor_tensor(low64[:, hd, :], heads(2)[:, hd, :],
                                                   gsm[:, 0, t * H + hd:t * H + hd + 1],
                                                   dec[:, hd, :], ALU.mult, ALU.mult).then_inc(S["low_dve"], 1)
                        V.tensor_tensor(intra[:], heads(3), dec_t[:], ALU.mult).then_inc(S["low_dve"], 1)
                        dve.wait_ge(S["low_dve"], 8 * t + 5)
                        V.tensor_tensor(pow_m[:], low64[:], over_heads(C_M16), ALU.mult).then_inc(S["low_ready"], 1)
                        V.tensor_tensor(low32[:], low64[:], over_heads(C_M32), ALU.mult).then_inc(S["low_dve"], 1)
                        for hd in range(H):
                            V.tensor_tensor(qdec[:, hd, :], gqt[:, hd, t * P:(t + 1) * P], egc_b[:, hd, :],
                                            ALU.mult).then_inc(S["rhs_ready"], 1)
                    elif s == 2:
                        dve.wait_ge(S["lowt_ready"], t + 1)
                        V.tensor_tensor(pow_n[:], heads(7), over_heads(C_M16), ALU.mult).then_inc(S["low_dve"], 1)
                        V.tensor_tensor(low64[:], low64[:], over_heads(C_M64), ALU.mult).then_inc(S["low_dve"], 1)
                        dve.wait_ge(S["low_dve"], 8 * t + 8)
                        V.tensor_tensor(inv_a[:], over_heads(C_ID), pow_n[:], ALU.subtract).then_inc(S["pow_ready"], 1)
                    elif s == 3:
                        dve.wait_ge(S["inv_pe"], 8 * t + 1)
                        V.tensor_copy(pow_m2[:], heads(2)).then_inc(S["inv_cp"], 1)
                        V.tensor_copy(pow_n2[:], heads(7)).then_inc(S["pow_ready"], 1)
                    elif s == 4:
                        dve.wait_ge(S["inv_pe"], 8 * t + 2)
                        V.tensor_copy(pow_m[:], heads(2)).then_inc(S["inv_cp"], 1)
                        V.tensor_copy(pow_n[:], heads(7)).then_inc(S["inv_cp"], 1)
                        V.tensor_tensor(inv_b[:], inv_a[:], heads(6), ALU.add).then_inc(S["pow_ready"], 1)
                    elif s == 5:
                        dve.wait_ge(S["inv_pe"], 8 * t + 3)
                        V.tensor_copy(pow_m2[:], heads(2)).then_inc(S["inv_cp"], 1)
                        dve.wait_ge(S["pow_ready"], 5 * t + 3)
                        V.tensor_tensor(inv_a[:], inv_b[:], heads(6), ALU.add).then_inc(S["pow_ready"], 1)
                    elif s == 6:
                        dve.wait_ge(S["inv_pe"], 8 * t + 4)
                        dve.wait_ge(S["pow_ready"], 5 * t + 4)
                        V.tensor_tensor(inv_b[:], inv_a[:], heads(6), ALU.add).then_inc(S["inv_dve"], 1)
                    elif s in (7, 9):
                        dve.wait_ge(S["inv_pe"], 8 * t + s - 2)
                        V.tensor_copy(zmat[:], heads(2)).then_inc(S["inv_dve"], 1)
                        V.tensor_copy(inv_t[:], heads(7)).then_inc(S["inv_dve"], 1)
                    elif s in (8, 10):
                        i = (s - 8) // 2
                        cur, new = ((inv_b, inv_a), (inv_a, inv_b))[i]
                        dve.wait_ge(S["inv_pe"], 8 * t + s - 2)
                        dve.wait_ge(S["inv_dve"], 6 * t + 1 + 3 * i)
                        V.tensor_tensor(new[:], cur[:], heads(6), ALU.subtract).then_inc(
                            S["inv_dve"] if i == 0 else S["pow_ready"], 1)
                    elif s == 11:
                        dve.wait_ge(S["uw_ready"], t + 1)
                        V.tensor_copy(u_sb[:], heads(2)).then_inc(S["uw_copied"], 1)
                    else:
                        j = (s - 12) // 2
                        c = 2 * t + j
                        rows = slice(j * CHUNK, (j + 1) * CHUNK)
                        if s % 2 == 0:
                            dve.wait_ge(S["step_v"], c + 1)
                            dve.wait_ge(S["uw_copied"], 2 * t + 2)
                            V.tensor_tensor(vnew[rows], u_sb[rows], heads(6)[rows], ALU.subtract).then_inc(S["step_vn"], 1)
                        else:
                            dve.wait_ge(S["step_so"], c + 1)
                            end = j * CHUNK + CHUNK - 1
                            for hd in range(H):
                                i = V.scalar_tensor_tensor(state[(c + 1) % 2][:, hd, :], state[c % 2][:, hd, :],
                                                           egc_b[:, hd, end:end + 1], heads(2)[:, hd, :],
                                                           ALU.mult, ALU.add)
                            i.then_inc(S["step_state"], 1)

                dve.wait_ge(S["nat_copied"], 12)
                dve.wait_ge(S["lam_dve"], 5)
                mixer(delta, attend)
                norm_rs(dve, "mix", 2 * H)
                for j in range(2 * H):
                    dve.wait_ge(S["rstd_bc"], bc_seen("mix") + j + 1)
                    gain = lam[:, 70:71] if j < H else par[:, Q_GDN:Q_GDN + 1]
                    i = V.scalar_tensor_tensor(mixt[:, j, :], mixt[:, j, :], gain, bank[5 + j % 2][:], ALU.mult, ALU.mult)
                    i.then_inc(S["norm_used"], 1)
                for j in range(2 * H):
                    dve.wait_ge(S["norm_used"], used_seen("mix") + j + 1)
                    if j >= H:
                        V.tensor_tensor(mixt[:, j, :], mixt[:, j, :], gzt[:, j - H, :], ALU.mult).then_inc(S["mix_ready"], 1)
                act_low(dve, mixt, KD)
                for i in range(KD):
                    split_lo(dve, S_OUT + i + AHEAD)
                    dve.wait_ge(s_used, S_OUT + i + 1)
                    V.tensor_tensor(res[:, i, :], res[:, i, :], bank[i % RING][:], ALU.add).then_inc(S["wout_added"], 1)
                norm_rs(dve, "ffn", 1)
                dve.wait_ge(S["wout_added"], KD)
                scale_to_wide(dve, "ffn", Q_FFN, 2 * KD)
                tks = S["tk_chain"]
                tk = {"n": 0}

                def step(ins):
                    tk["n"] += 1
                    ins.then_inc(tks, 1)

                def settle():
                    dve.wait_ge(tks, tk["n"])

                picks = onehot[:].rearrange("p (t k) c -> p t k c", t=NT)

                def select(hd, part):
                    def score(i):
                        return heads(4 + 2 * (hd % 2) + i // 4)[:, i % 4, :]
                    units = range(2 * NT)
                    tv = topv[:].rearrange("p t c k -> p (t c) k")
                    ti = topi[:].rearrange("p t c k -> p (t c) k")
                    wv = winv[:, :, hd, :]
                    if part == 0:
                        dve.wait_ge(S["score_ready"], hd + 1)
                        settle()
                        for i in units:
                            step(V.max(tv[:, i, 0:8], score(i)))
                        settle()
                        for i in units:
                            step(V.match_replace(rest[:, i, :], tv[:, i, 0:8], score(i), NEG))
                            step(V.max_index(ti[:, i, 0:8], tv[:, i, 0:8], score(i)))
                        settle()
                        dve.sem_inc(S["score_read"], 1)
                    elif part == 1:
                        for i in units:
                            step(V.max(tv[:, i, 8:16], rest[:, i, :]))
                        settle()
                        for i in units:
                            step(V.max_index(ti[:, i, 8:16], tv[:, i, 8:16], rest[:, i, :]))
                        settle()
                        if hd > 0:
                            dve.wait_ge(S["picks_ready"], hd * NT)
                            sum_experts(hd - 1)
                        step(V.tensor_copy(topf[:], topi[:]))
                        settle()
                        step(V.tensor_scalar(topf[:, :, 0, :], topf[:, :, 0, :], float(NKEYS), None, ALU.mult))
                        settle()
                        for dst, src in ((cand, topv), (cidx, topf)):
                            for a in range(8):
                                o, n = CAND_AT[a], CAND_ROWS[a]
                                step(V.tensor_tensor(dst[:, :, o:o + n], src[:, :, 1, 0:n],
                                                     src[:, :, 0, a:a + 1].to_broadcast([P, NT, n]), ALU.add))
                            o, n = CAND_AT[8], TOPK - 8
                            step(V.tensor_tensor(dst[:, :, o:o + n], src[:, :, 0, 8:TOPK],
                                                 src[:, :, 1, 0:1].to_broadcast([P, NT, n]), ALU.add))
                    elif part == 2:
                        settle()
                        for t in range(NT):
                            step(V.max(wv[:, t, 0:8], cand[:, t, :]))
                        settle()
                        for t in range(NT):
                            step(V.match_replace(crest[:, t, :], wv[:, t, 0:8], cand[:, t, :], NEG))
                            step(V.max_index(winp[:, t, 0:8], wv[:, t, 0:8], cand[:, t, :]))
                        settle()
                        for t in range(NT):
                            step(V.max(wv[:, t, 8:16], crest[:, t, :]))
                        settle()
                        for t in range(NT):
                            step(V.max_index(winp[:, t, 8:16], wv[:, t, 8:16], crest[:, t, :]))
                        settle()
                        step(V.tensor_copy(winf[:], winp[:]))
                        settle()
                        mark_places()
                        if hd < PH - 1:
                            dve.sem_inc(S["places_ready"], 1)


                def mark_places():
                    for t in range(NT):
                        step(V.tensor_tensor(picks[:, t], winf[:, t, :].unsqueeze(2).to_broadcast([P, TOPK, NC]),
                                             consts[:, C_POS:C_POS + NC].unsqueeze(1).to_broadcast([P, TOPK, NC]),
                                             ALU.is_equal))
                    settle()

                def sum_experts(hd):
                    step(V.tensor_reduce(expert[:, :, hd, :], picks, AX_X, ALU.add))
                    settle()

                for p in range(2):
                    split_lo(dve, S_WQ + p + AHEAD)
                for hd in range(PH):
                    for part in range(4):
                        p = 2 + 4 * hd + part
                        if p < len(SEL_SEQ):
                            split_lo(dve, S_WQ + p + AHEAD)
                        if part < 3:
                            select(hd, part)
                for t in range(NT):
                    step(V.tensor_tensor(picks[:, t], picks[:, t], cidx[:, t, :].unsqueeze(1).to_broadcast([P, TOPK, NC]),
                                         ALU.mult))
                settle()
                sum_experts(PH - 1)
                wv = winv[:].rearrange("p t h k -> p (t h) k")
                step(V.tensor_copy(gsum[:], wv[:, :, 0]))
                step(V.tensor_copy(exp_i[:], expert[:].rearrange("p t h k -> p (t h k)")))
                settle()
                step(V.tensor_tensor(wv, wv, gsum[:].unsqueeze(2).to_broadcast([P, NT * PH, TOPK]), ALU.subtract))
                step(V.tensor_scalar(exp_j[:], exp_i[:], 7, None, ALU.logical_shift_right))
                settle()
                dve.sem_inc(S["tk_dve"], 1)
                step(V.tensor_scalar(exp_i[:], exp_i[:], NKEYS - 1, None, ALU.bitwise_and))
                step(V.tensor_copy(sel[:, 0].rearrange("p t c -> p (t c)"), exp_j[:]))
                settle()
                step(V.tensor_copy(sel[:, 1].rearrange("p t c -> p (t c)"), exp_i[:]))
                dve.wait_ge(S["tk_act"], 1)
                step(V.tensor_reduce(gsum[:], wv, AX_X, ALU.add))
                settle()
                step(V.reciprocal(gsum[:], gsum[:]))
                settle()
                step(V.tensor_tensor(wv, wv, gsum[:].unsqueeze(2).to_broadcast([P, NT * PH, TOPK]), ALU.mult))
                settle()
                dve.sem_inc(S["tk_dve"], 1)
                for t in range(NT):
                    dve.wait_ge(S["selt_ready"], t + 1)
                    V.tensor_scalar(selt[:, 3, t * P:(t + 1) * P], heads(t)[:, 2, :], -1.0, None, ALU.mult)
                    V.tensor_copy(selt[:, 0:3, t * P:(t + 1) * P], heads(t)[:, 0:3, :]).then_inc(S["selt_copied"], 1)
                dve.wait_ge(S["selt_copied"], NT)
                dve.sem_inc(S["stored_a"], 1)
                dve.sem_inc(S["stored_b"], 1)
                with dve.Fori(0, T // TG // 2) as q:
                    for b in range(2 * TG // 8):
                        dve.wait_ge(S["gm_ready"], q * (TG // 2) + 2 * b + 2)
                        V.tensor_tensor(hot1[b % 2][:, 0:DVE_HOT1, :], iota.unsqueeze(1).to_broadcast([P, DVE_HOT1, NKEYS]),
                                        selt[:, 0, bass.ds(q * 2 * TG + 8 * b, DVE_HOT1)].unsqueeze(2).to_broadcast(
                                            [P, DVE_HOT1, NKEYS]), ALU.is_equal)
                        for tok in range(8 - ACT_HOT2):
                            at_tok = q * 2 * TG + (8 * b + tok)
                            last = V.tensor_scalar(hot2[b % 2][:, tok, :], iota, selt[:, 1, bass.ds(at_tok, 1)],
                                                   selt[:, 2, bass.ds(at_tok, 1)], ALU.is_equal, ALU.mult)
                        last.then_inc(S["hot2_ready"], 1)

                dve.sem_inc(S["v_added"], 1)

                def weigh(g, j, h):
                    if j >= 4:
                        dve.wait_ge(g_loaded[1], g * 16 + 16)
                    else:
                        dve.wait_ge(g_loaded[0], g * 16 + 16)
                    if not (isinstance(g, int) and g * GB + j < 2):
                        dve.wait_ge(S["w_lo_ready"], g * GB + j - 1)

                    def tokens(x):
                        return x.rearrange("p (s t) -> p s t", t=TG)
                    V.tensor_tensor(tokens(act_w[j % 2][:]), tokens(h[:, j, :]), g_sb[j // 4][:, :, j % 4, :],
                                    ALU.mult).then_inc(S["w_ready"], 1)

                def w_low(g, j, pg):
                    dve.wait_ge(S["w_hi_ready"], g * GB + j + 1)
                    V.tensor_tensor(w_lo[pg][:, j, :], act_w[j % 2][:], w_hi[pg][:, j, :].bitcast(F32),
                                    ALU.subtract).then_inc(S["w_lo_ready"], 1)

                def add_block(j, used):
                    dve.wait_ge(s_used, used)
                    V.tensor_tensor(res[:, j, :], res[:, j, :], bank[1 + 2 * (j % 2)][:], ALU.add).then_inc(S["v_added"], 1)

                dve.wait_ge(S["u_gelu"], 2 * GB)
                for j in range(GB):
                    weigh(0, j, hb)
                    if j > 0:
                        w_low(0, j - 1, 0)
                w_low(0, GB - 1, 0)

                def group(g, pg):
                    for j in range(GB):
                        n = g * 16 + (S_UV + 2 * j)
                        split_lo(dve, n + AHEAD, (2 * j + AHEAD) % RING)
                        dve.wait_ge(S["u_gelu"], g * GB + (GB + j + 1))
                        weigh(g + 1, j, h_ring)
                        split_lo(dve, n + 1 + AHEAD, (2 * j + 1 + AHEAD) % RING)
                        w_low(g + 1, j, 1 - pg)
                        add_block(j, n + 2)
                with dve.Fori(0, 7) as it:
                    group(it * 2, 0)
                    group(it * 2 + 1, 1)
                for p, (kind, j) in enumerate(TAIL):
                    n = S_V_LAST + p
                    split_lo(dve, n + AHEAD)
                    if kind == "p":
                        if j == 0:
                            act_low_chunk(dve, res, 3 * KD, 3)
                        continue
                    if j < GB:
                        dve.wait_ge(S["u_gelu"], (GROUPS - 1) * GB + j + 1)
                        weigh(GROUPS - 1, j, h_ring)
                        w_low(GROUPS - 1, j, 1)
                    if GB < j != 12:
                        act_low_chunk(dve, res, 3 * KD, j - GB - 1)
                    if j == GB + 1:
                        dve.wait_ge(S["p_hi_ready"], 1)
                        V.tensor_tensor(p_lo[:], p_sb[:], p_hi[:].bitcast(F32), ALU.subtract).then_inc(S["p_lo_ready"], 1)
                    add_block(j % GB, n + 1)
                act_low_chunk(dve, res, 3 * KD, KD - 1)
                norm_rs(dve, "ple", 1)
                dve.wait_ge(S["rstd_bc"], bc_seen("ple") + 1)
                pd = S["ple_dve"]
                for k in range(KD):
                    if S_WG + k + AHEAD < N_SLABS:
                        split_lo(dve, S_WG + k + AHEAD)
                    V.scalar_tensor_tensor(e_t[:, k, :], e_t[:, k, :], par[:, Q_PLE + k:Q_PLE + k + 1], bank[5][:],
                                           ALU.mult, ALU.mult).then_inc(pd, 1)
                    dve.wait_ge(S["wg_evac"], k + 1)
                    dve.wait_ge(pd, 2 * k + 1)
                    V.tensor_tensor(act_w[k % 2][:], act_w[k % 2][:], e_t[:, k, :], ALU.mult).then_inc(pd, 1)
                    dve.wait_ge(pd, 2 * k + 2)
                    V.tensor_tensor(res[:, k, :], res[:, k, :], act_w[k % 2][:], ALU.add).then_inc(S["layer_res"], 1)
                dve.wait_ge(S["layer_res"], KD)
                dve.sem_inc(layer_end, 1)
                dve.wait_ge(layer_go, 1)
                dve.sem_inc(layer_seen, 1)
            norm_rs(dve, "in", 1)
            dve.wait_ge(S["rstd_bc"], 1)
            for k in range(KD):
                nc.vector.scalar_tensor_tensor(wide[:, k, :], res[:, k, :], par[:, Q_FIN + k:Q_FIN + k + 1], bank[5][:],
                                               ALU.mult, ALU.mult).then_inc(out_ready, 1)


def constants():
    import numpy as np
    c = np.zeros((P, NCONST), np.float32)
    i = np.arange(P)
    row, col = i[:, None], i[None, :]
    same = row // CHUNK == col // CHUNK
    c[:, C_ID:C_ID + P] = row == col
    c[:, C_ONE:C_ONE + P] = 1
    c[:, C_TRI:C_TRI + P] = (row <= col) & same
    c[:, C_CHUNK:C_CHUNK + P] = same
    c[:, C_NEGT:C_NEGT + P] = np.where((row <= col) & same, 0, NEG)
    c[:, C_POSD:C_POSD + P] = np.where((col < row) & same, 0, -NEG)
    c[:, C_M16:C_M16 + P] = row // 16 == col // 16
    c[:, C_M32:C_M32 + P] = (row // 32 == col // 32) & (row // 16 != col // 16)
    c[:, C_M64:C_M64 + P] = same & (row // 32 != col // 32)
    j = np.arange(T)[None, :] - (T - P)
    c[:, C_DIST:C_DIST + T] = np.where(j <= row, j - row, NEG)
    c[:, C_IOTA:C_IOTA + P] = col
    c[:, C_POS:C_POS + NC] = np.arange(NC)
    c[:, C_EPS] = EPS
    return c


def kernel(**inputs):
    import math
    import numpy as np
    import concourse.bacc as bacc
    from concourse.bass_utils import run_bass_kernel_spmd

    a = {k: np.asarray(v) for k, v in inputs.items()}

    def by_columns(w):
        n = w.shape[1] // P
        return w.reshape(-1, P, n, P).transpose(2, 1, 0, 3)

    def chunked(v):
        return v.reshape(-1, P).T

    slabs = np.empty((DEPTH, N_SLABS, P, KD, P), np.float32)
    w_ba = np.empty((DEPTH, P, KD, 8), np.float32)
    subkeys = np.empty((DEPTH, P, 2 * PH, NKEYS), np.float32)
    params = np.zeros((DEPTH, P, NPAR), np.float32)
    for i in range(DEPTH):
        w_in = a["w_in"][i]
        slabs[i, S_IN:S_OUT] = by_columns(w_in[:, :28 * P])[IN_ORDER]
        w_ba[i] = w_in[:, 28 * P:].reshape(KD, P, 8).transpose(1, 0, 2)
        slabs[i, S_OUT:S_WQ] = by_columns(a["w_out"][i])
        wq = by_columns(a["peer_wq"][i])
        u = a["peer_u"][i].reshape(NKEYS, NKEYS, KD, P).transpose(1, 3, 2, 0)
        v = a["peer_v"][i].reshape(NKEYS, GROUPS, GB, KD, P).transpose(1, 3, 0, 2, 4).reshape(-1, P, GB, P)
        for n, (kind, j) in enumerate(SEL_SEQ):
            slabs[i, S_WQ + n] = wq[j] if kind == "q" else u[j]
        slabs[i, S_UV:S_V_LAST:2] = u[2 * GB:]
        slabs[i, S_UV + 1:S_V_LAST:2] = v[:(GROUPS - 2) * KD]
        wp = by_columns(a["ple_wp"][i]).reshape(2, 4, P, 2, P).transpose(0, 2, 1, 3, 4).reshape(2, P, KD, P)
        for n, (kind, j) in enumerate(TAIL):
            slabs[i, S_V_LAST + n] = v[(GROUPS - 2) * KD + j] if kind == "v" else wp[j]
        slabs[i, S_WG:] = by_columns(a["ple_wg"][i])
        subkeys[i] = a["peer_subkeys"][i].reshape(2 * PH, NKEYS, P).transpose(2, 0, 1)
        q = params[i]
        q[:, Q_MIX:Q_MIX + 8] = chunked(a["ln_mix_g"][i])
        q[:, Q_FFN:Q_FFN + 8] = chunked(a["ln_ffn_g"][i])
        q[:, Q_PLE:Q_PLE + 8] = chunked(a["ple_norm_g"][i])
        q[:, Q_FIN:Q_FIN + 8] = chunked(a["final_norm_g"])
        for tap in range(CONV_K):
            q[:, Q_CONV + 12 * tap:Q_CONV + 12 * tap + 12] = chunked(a["conv_w"][i, tap])
        q[:, Q_GDN] = a["gdn_norm_g"][i]
        q[:, Q_SUB] = a["diff_subln_g"][i]
        q[:, Q_ALOG:Q_ALOG + H] = a["gdn_a_log"][i][None]
        q[:, Q_DT:Q_DT + H] = a["gdn_dt_bias"][i][None]
        q[:, Q_LAM:Q_LAM + 4 * DQK] = a["diff_lambda"][i].reshape(1, -1)
        lam_init = 0.8 - 0.6 * math.exp(-0.3 * i)
        q[:, Q_LINIT] = lam_init
        q[:, Q_LINIT + 1] = 1.0 - lam_init
    x_t = a["x"][0].T.reshape(KD, P, T).transpose(1, 0, 2)
    p_t = a["p"][:DEPTH, 0].transpose(0, 2, 1).reshape(DEPTH, 2, P, T).transpose(0, 2, 1, 3)
    arrays = {"x_t": x_t, "p_t": p_t, "slabs": slabs, "w_ba": w_ba, "subkeys": subkeys,
              "params": params, "constants": constants()}
    arrays = {k: np.ascontiguousarray(v) for k, v in arrays.items()}

    nc = bacc.Bacc("TRN2", target_bir_lowering=False, num_devices=1)
    args = [nc.dram_tensor(k, v.shape, F32, kind="ExternalInput").ap() for k, v in arrays.items()]
    out = nc.dram_tensor("out_t", (P, KD, T), F32, kind="ExternalOutput").ap()
    trunk(nc, *args, out)
    r = run_bass_kernel_spmd(nc, [arrays], core_ids=[0])
    y = r.results[0]["out_t"]
    return np.ascontiguousarray(y.transpose(1, 0, 2).reshape(D, T).T)[None]
```
